# Optimizing a Trainium2 kernel written in Bass

```python
import math
import jax
import jax.numpy as jnp
from jax import lax
import numpy as np

D_MODEL = 1024
BATCH = 1
SEQ = 512
DEPTH = 1

N_BRANCH = 4
BRANCH_W = 512

SSD_D_INNER = 512
SSD_HEAD_DIM = 64
SSD_HEADS = SSD_D_INNER // SSD_HEAD_DIM
SSD_GROUPS = 2
SSD_HPG = SSD_HEADS // SSD_GROUPS
SSD_STATE = 64
SSD_CONV = 4
SSD_CHUNK = 128
SSD_CONV_CH = SSD_D_INNER + 2 * SSD_GROUPS * SSD_STATE

DIL_PAIRS = ((128, 1), (512, 4), (2048, 16))
DIL_HPG = 4
DIL_HEAD_DIM = 128
DIL_HEADS = DIL_HPG * len(DIL_PAIRS)
DIL_BLOCK = 128

DIFF_HEADS = 4
DIFF_HEAD_DIM = 64
DIFF_QBLOCK = 128

HG_HEADS = 8
HG_KEY_DIM = 64
HG_VAL_DIM = BRANCH_W // HG_HEADS
HG_CHUNK = 64

N_EXPERTS = 64
N_EXPERT_GROUPS = 8
EXPERTS_PER_GROUP = N_EXPERTS // N_EXPERT_GROUPS
TOP_K = 2
D_EXPERT = 256
MOE_BLOCK = 128

NORM_EPS = 1e-6
MASK_VALUE = -1e30

IN_WIDTHS = (
    SSD_D_INNER,
    SSD_CONV_CH,
    SSD_HEADS,
    DIL_HEADS * DIL_HEAD_DIM,
    DIL_HEADS * DIL_HEAD_DIM,
    DIL_HEADS * DIL_HEAD_DIM,
    2 * DIFF_HEADS * DIFF_HEAD_DIM,
    2 * DIFF_HEADS * DIFF_HEAD_DIM,
    DIFF_HEADS * 2 * DIFF_HEAD_DIM,
    HG_HEADS * HG_KEY_DIM,
    HG_HEADS * HG_KEY_DIM,
    HG_HEADS * HG_VAL_DIM,
    HG_HEADS * HG_VAL_DIM,
    N_BRANCH * D_MODEL,
)
IN_OFFSETS = tuple(sum(IN_WIDTHS[:i + 1]) for i in range(len(IN_WIDTHS) - 1))
D_IN = sum(IN_WIDTHS)

kernel_name = "hybrid_gated_ssd_dilated_diff_hgrn2_moe"

def rms_norm(x, w):
    xf = x.astype(jnp.float32)
    y = xf * lax.rsqrt(jnp.mean(xf * xf, axis=-1, keepdims=True) + NORM_EPS)
    return (y * w.astype(jnp.float32)).astype(x.dtype)

def modulate(h, shift, scale):
    return h * (1.0 + scale[:, None, :]) + shift[:, None, :]

def causal_depthwise_conv(x, w, b):
    k = w.shape[0]
    y = lax.conv_general_dilated(x, w[:, None, :], window_strides=(1,), padding=[(k - 1, 0)],
                                 dimension_numbers=("NWC", "WIO", "NWC"),
                                 feature_group_count=x.shape[-1])
    return y + b

def segsum(x):
    t = x.shape[-1]
    cs = jnp.cumsum(x, axis=-1)
    diff = cs[..., :, None] - cs[..., None, :]
    mask = jnp.tril(jnp.ones((t, t), dtype=bool))
    return jnp.where(mask, diff, MASK_VALUE)

def ssd_chunked(xh, dt, a, bm, cm):
    b, s, g, e, p = xh.shape
    n = bm.shape[-1]
    nc = s // SSD_CHUNK
    x = (xh * dt[..., None]).reshape(b, nc, SSD_CHUNK, g, e, p)
    adt = (dt * a).reshape(b, nc, SSD_CHUNK, g, e).transpose(0, 3, 4, 1, 2)
    bm = bm.reshape(b, nc, SSD_CHUNK, g, n)
    cm = cm.reshape(b, nc, SSD_CHUNK, g, n)
    a_cs = jnp.cumsum(adt, axis=-1)
    lmat = jnp.exp(segsum(adt))
    cb = jnp.einsum("bclgn,bcsgn->bgcls", cm, bm)
    y_diag = jnp.einsum("bgecls,bcsgep->bclgep", cb[:, :, None] * lmat, x)
    decay_states = jnp.exp(a_cs[..., -1:] - a_cs)
    states = jnp.einsum("bclgn,bgecl,bclgep->bcgepn", bm, decay_states, x)
    states = jnp.concatenate([jnp.zeros_like(states[:, :1]), states], axis=1)
    chunk_tot = jnp.pad(a_cs[..., -1], ((0, 0), (0, 0), (0, 0), (1, 0)))
    decay_chunk = jnp.exp(segsum(chunk_tot))
    states = jnp.einsum("bgezc,bcgepn->bzgepn", decay_chunk, states)[:, :-1]
    y_off = jnp.einsum("bclgn,bcgepn,bgecl->bclgep", cm, states, jnp.exp(a_cs))
    return (y_diag + y_off).reshape(b, s, g, e, p)

def banded_causal_attention(q, k, v, max_dist):
    n, l, h, dh = q.shape
    blk = DIL_BLOCK
    nb = -(-l // blk)
    lp = nb * blk
    pad_end = lp - l
    qb = jnp.pad(q, ((0, 0), (0, pad_end), (0, 0), (0, 0))).reshape(n, nb, blk, h, dh)

    def key_blocks(t):
        tp = jnp.pad(t, ((0, 0), (blk, pad_end), (0, 0), (0, 0))).reshape(n, nb + 1, blk, h, dh)
        return jnp.concatenate([tp[:, :-1], tp[:, 1:]], axis=2)

    kb = key_blocks(k)
    vb = key_blocks(v)
    q_idx = jnp.arange(nb)[:, None] * blk + jnp.arange(blk)[None, :]
    k_idx = jnp.arange(nb)[:, None] * blk - blk + jnp.arange(2 * blk)[None, :]
    dist = q_idx[:, :, None] - k_idx[:, None, :]
    valid = (dist >= 0) & (dist <= max_dist) & (k_idx[:, None, :] >= 0)
    sc = jnp.einsum("nbqhd,nbkhd->nbhqk", qb, kb).astype(jnp.float32) * (dh ** -0.5)
    sc = jnp.where(valid[None, :, None], sc, MASK_VALUE)
    m = jnp.max(sc, axis=-1, keepdims=True)
    pr = jnp.exp(sc - m)
    denom = jnp.sum(pr, axis=-1, keepdims=True)
    o = jnp.einsum("nbhqk,nbkhd->nbqhd", pr / denom, vb.astype(jnp.float32))
    lse = (m + jnp.log(denom))[..., 0]
    o = o.reshape(n, lp, h, dh)[:, :l]
    lse = lse.transpose(0, 1, 3, 2).reshape(n, lp, h)[:, :l]
    return o, lse

def dilated_attention(q, k, v):
    b, s, _, dh = q.shape
    outs, lses = [], []
    for g, (window, dil) in enumerate(DIL_PAIRS):
        hs = slice(g * DIL_HPG, (g + 1) * DIL_HPG)
        sub_len = s // dil

        def to_sub(t):
            return t.reshape(b, sub_len, dil, DIL_HPG, dh).transpose(0, 2, 1, 3, 4).reshape(b * dil, sub_len, DIL_HPG, dh)

        o, lse = banded_causal_attention(to_sub(q[:, :, hs]), to_sub(k[:, :, hs]), to_sub(v[:, :, hs]), window // dil)
        outs.append(o.reshape(b, dil, sub_len, DIL_HPG, dh).transpose(0, 2, 1, 3, 4).reshape(b, s, DIL_HPG, dh))
        lses.append(lse.reshape(b, dil, sub_len, DIL_HPG).transpose(0, 2, 1, 3).reshape(b, s, DIL_HPG))
    wts = jax.nn.softmax(jnp.stack(lses, axis=0), axis=0)
    return jnp.sum(wts[..., None] * jnp.stack(outs, axis=0), axis=0)

def differential_attention(q, k, v, lam, lam_init, subln_w):
    b, s, h2, dh = q.shape
    h = h2 // 2
    nblk = s // DIFF_QBLOCK
    qb = q.reshape(b, nblk, DIFF_QBLOCK, h2, dh).transpose(1, 0, 2, 3, 4)
    k_pos = jnp.arange(s)
    vf = v.astype(jnp.float32)
    scale = dh ** -0.5

    def one_block(args):
        q_blk, blk = args
        sc = jnp.einsum("bqhd,bkhd->bhqk", q_blk, k).astype(jnp.float32) * scale
        q_pos = blk * DIFF_QBLOCK + jnp.arange(DIFF_QBLOCK)
        causal = k_pos[None, :] <= q_pos[:, None]
        pr = jax.nn.softmax(jnp.where(causal, sc, MASK_VALUE), axis=-1).reshape(b, h, 2, DIFF_QBLOCK, s)
        attn = pr[:, :, 0] - lam * pr[:, :, 1]
        return jnp.einsum("bhqk,bkhe->bqhe", attn, vf)

    o = lax.map(one_block, (qb, jnp.arange(nblk)))
    o = o.transpose(1, 0, 2, 3, 4).reshape(b, s, h, 2 * dh)
    return rms_norm(o, subln_w) * (1.0 - lam_init)

def hgrn2_chunked(q, k, v, log_f):
    b, s, h, dk = q.shape
    dv = v.shape[-1]
    nc = s // HG_CHUNK

    def chunks(t):
        return t.reshape(b, nc, HG_CHUNK, h, t.shape[-1]).transpose(1, 0, 3, 2, 4)

    causal = jnp.tril(jnp.ones((HG_CHUNK, HG_CHUNK), dtype=bool))

    def step(state, inp):
        qi, ki, vi, gi = inp
        gcum = jnp.cumsum(gi, axis=2)
        o_inter = jnp.einsum("bhik,bhkv->bhiv", qi * jnp.exp(gcum), state)
        rel = gcum[:, :, :, None, :] - gcum[:, :, None, :, :]
        decay = jnp.exp(jnp.where(causal[:, :, None], rel, MASK_VALUE))
        attn = jnp.einsum("bhik,bhjk,bhijk->bhij", qi, ki, decay)
        o_intra = jnp.einsum("bhij,bhjv->bhiv", attn, vi)
        g_last = gcum[:, :, -1:]
        new_state = jnp.exp(g_last[:, :, 0])[..., None] * state + jnp.einsum("bhjk,bhjv->bhkv", ki * jnp.exp(g_last - gcum), vi)
        return new_state, o_inter + o_intra

    state0 = jnp.zeros((b, h, dk, dv), jnp.float32)
    _, o = lax.scan(step, state0, (chunks(q), chunks(k), chunks(v), chunks(log_f)))
    return o.transpose(1, 0, 3, 2, 4).reshape(b, s, h, dv)

def token_mixer(h, layer, w_in, conv_w, conv_b, dt_bias, a_log, d_skip, ssd_norm_w, diff_lambda,
                diff_subln_w, lower_bound, hgrn_norm_w, w_merge, w_out):
    b, s, d = h.shape
    f32 = jnp.float32
    (z, xbc, dt_raw, q_b, k_b, v_b, q_c, k_c, v_c, q_d, f_d, i_d, g_d, gate_logits) = jnp.split(h @ w_in, IN_OFFSETS, axis=-1)

    xbc = jax.nn.silu(causal_depthwise_conv(xbc, conv_w, conv_b))
    xs, bm, cm = jnp.split(xbc, (SSD_D_INNER, SSD_D_INNER + SSD_GROUPS * SSD_STATE), axis=-1)
    dt = jax.nn.softplus(dt_raw.astype(f32) + dt_bias.astype(f32))
    a = -jnp.exp(a_log.astype(f32))
    xh = xs.astype(f32).reshape(b, s, SSD_GROUPS, SSD_HPG, SSD_HEAD_DIM)
    y = ssd_chunked(xh, dt.reshape(b, s, SSD_GROUPS, SSD_HPG), a.reshape(SSD_GROUPS, SSD_HPG),
                    bm.astype(f32).reshape(b, s, SSD_GROUPS, SSD_STATE), cm.astype(f32).reshape(b, s, SSD_GROUPS, SSD_STATE))
    y = y + d_skip.astype(f32).reshape(SSD_GROUPS, SSD_HPG)[..., None] * xh
    y = y.reshape(b, s, SSD_D_INNER).astype(h.dtype)
    o_a = rms_norm(y * jax.nn.silu(z), ssd_norm_w)

    dil_shape = (b, s, DIL_HEADS, DIL_HEAD_DIM)
    o_b = dilated_attention(q_b.reshape(dil_shape), k_b.reshape(dil_shape), v_b.reshape(dil_shape))
    o_b = o_b.reshape(b, s, BRANCH_W).astype(h.dtype)

    lam_q1, lam_k1, lam_q2, lam_k2 = diff_lambda.astype(f32)
    lam_init = 0.8 - 0.6 * math.exp(-0.3 * layer)
    lam = jnp.exp(jnp.sum(lam_q1 * lam_k1)) - jnp.exp(jnp.sum(lam_q2 * lam_k2)) + lam_init
    qk_shape = (b, s, 2 * DIFF_HEADS, DIFF_HEAD_DIM)
    o_c = differential_attention(q_c.reshape(qk_shape), k_c.reshape(qk_shape),
                                 v_c.reshape(b, s, DIFF_HEADS, 2 * DIFF_HEAD_DIM), lam, lam_init, diff_subln_w)
    o_c = o_c.reshape(b, s, BRANCH_W).astype(h.dtype)

    lb = lower_bound.reshape(HG_HEADS, HG_KEY_DIM)
    f_logit = f_d.astype(f32).reshape(b, s, HG_HEADS, HG_KEY_DIM)
    f_gate = lb + (1.0 - lb) * jax.nn.sigmoid(f_logit)
    log_f = jnp.log(f_gate)
    k_in = 1.0 - f_gate
    q_hg = jax.nn.silu(q_d.astype(f32).reshape(b, s, HG_HEADS, HG_KEY_DIM))
    v_hg = i_d.astype(f32).reshape(b, s, HG_HEADS, HG_VAL_DIM)
    o = hgrn2_chunked(q_hg, k_in, v_hg, log_f)
    o_d = rms_norm(o, hgrn_norm_w) * jax.nn.silu(g_d.astype(f32).reshape(b, s, HG_HEADS, HG_VAL_DIM))
    o_d = o_d.reshape(b, s, BRANCH_W).astype(h.dtype)

    branches = jnp.stack([o_a, o_b, o_c, o_d], axis=2)
    proj = jnp.einsum("bsnw,nwd->bsnd", branches, w_merge)
    gates = jax.nn.sigmoid(gate_logits.reshape(b, s, N_BRANCH, d))
    return jnp.sum(gates * proj, axis=2) @ w_out

def moe_ffn(h, w_router, router_bias, w_gate, w_up, w_down):
    b, s, d = h.shape
    n_tok = b * s
    t = h.reshape(n_tok, d)
    scores = jax.nn.sigmoid((t @ w_router).astype(jnp.float32))
    sel = scores + router_bias.astype(jnp.float32)
    group_score = jnp.sum(lax.top_k(sel.reshape(n_tok, N_EXPERT_GROUPS, EXPERTS_PER_GROUP), 2)[0], axis=-1)
    best_group = jnp.argmax(group_score, axis=-1)
    in_group = (jnp.arange(N_EXPERTS) // EXPERTS_PER_GROUP)[None, :] == best_group[:, None]
    _, idx = lax.top_k(jnp.where(in_group, sel, MASK_VALUE), TOP_K)
    wts = jnp.take_along_axis(scores, idx, axis=-1)
    wts = wts / jnp.sum(wts, axis=-1, keepdims=True)

    flat_e = idx.reshape(-1).astype(jnp.int32)
    flat_tok = jnp.repeat(jnp.arange(n_tok, dtype=jnp.int32), TOP_K)
    flat_w = wts.reshape(-1)
    order = jnp.argsort(flat_e)
    e_s, tok_s, w_s = flat_e[order], flat_tok[order], flat_w[order]
    counts = jnp.bincount(flat_e, length=N_EXPERTS)
    padded = ((counts + MOE_BLOCK - 1) // MOE_BLOCK) * MOE_BLOCK
    start = jnp.cumsum(counts) - counts
    pend = jnp.cumsum(padded)
    pstart = pend - padded
    dest = pstart[e_s] + (jnp.arange(n_tok * TOP_K) - start[e_s])
    n_rows = n_tok * TOP_K + N_EXPERTS * MOE_BLOCK
    n_blocks = n_rows // MOE_BLOCK
    row_tok = jnp.zeros((n_rows,), jnp.int32).at[dest].set(tok_s)
    row_w = jnp.zeros((n_rows,), jnp.float32).at[dest].set(w_s)
    blk_start = jnp.arange(n_blocks) * MOE_BLOCK
    blk_e = jnp.minimum(jnp.sum(pend[None, :] <= blk_start[:, None], axis=1), N_EXPERTS - 1)
    xs = t[row_tok].reshape(n_blocks, MOE_BLOCK, d)

    def expert_block(args):
        xb, e = args
        hid = jax.nn.silu(xb @ w_gate[e]) * (xb @ w_up[e])
        return hid @ w_down[e]

    ys = lax.map(expert_block, (xs, blk_e)).reshape(n_rows, d)
    out = jnp.zeros((n_tok, d), h.dtype).at[row_tok].add(ys * row_w[:, None].astype(h.dtype))
    return out.reshape(b, s, d)

def setup_inputs(seed: int = 0) -> dict:
    key = jax.random.key(seed)
    ks = jax.random.split(key, 26)
    f32 = jnp.float32

    def nrm(k, shape, scale):
        return jax.random.normal(k, shape, f32) * scale

    dt0 = jnp.exp(jax.random.uniform(ks[9], (DEPTH, SSD_HEADS), f32) * (math.log(0.1) - math.log(1e-3)) + math.log(1e-3))
    return {
        "x": nrm(ks[0], (BATCH, SEQ, D_MODEL), 1.0),
        "c": nrm(ks[1], (BATCH, D_MODEL), 1.0),
        "w_ada": nrm(ks[2], (DEPTH, D_MODEL, 6 * D_MODEL), 0.5 * D_MODEL ** -0.5),
        "b_ada": nrm(ks[3], (DEPTH, 6 * D_MODEL), 0.01),
        "norm_mix_w": 1.0 + nrm(ks[4], (DEPTH, D_MODEL), 0.02),
        "norm_ffn_w": 1.0 + nrm(ks[5], (DEPTH, D_MODEL), 0.02),
        "w_in": nrm(ks[6], (DEPTH, D_MODEL, D_IN), D_MODEL ** -0.5),
        "conv_w": nrm(ks[7], (DEPTH, SSD_CONV, SSD_CONV_CH), SSD_CONV ** -0.5),
        "conv_b": nrm(ks[8], (DEPTH, SSD_CONV_CH), 0.01),
        "ssd_dt_bias": dt0 + jnp.log(-jnp.expm1(-dt0)),
        "ssd_a_log": jnp.log(jax.random.uniform(ks[10], (DEPTH, SSD_HEADS), f32, 1.0, 16.0)),
        "ssd_d": 1.0 + nrm(ks[11], (DEPTH, SSD_HEADS), 0.1),
        "ssd_norm_w": 1.0 + nrm(ks[12], (DEPTH, SSD_D_INNER), 0.02),
        "diff_lambda": nrm(ks[13], (DEPTH, 4, DIFF_HEAD_DIM), 0.1),
        "diff_subln_w": 1.0 + nrm(ks[14], (DEPTH, 2 * DIFF_HEAD_DIM), 0.02),
        "hgrn_lb_logits": nrm(ks[15], (DEPTH, HG_HEADS * HG_KEY_DIM), 1.0),
        "hgrn_norm_w": 1.0 + nrm(ks[16], (DEPTH, HG_VAL_DIM), 0.02),
        "w_merge": nrm(ks[17], (DEPTH, N_BRANCH, BRANCH_W, D_MODEL), BRANCH_W ** -0.5),
        "w_out": nrm(ks[18], (DEPTH, D_MODEL, D_MODEL), D_MODEL ** -0.5),
        "w_router": nrm(ks[19], (D_MODEL, N_EXPERTS), D_MODEL ** -0.5),
        "router_bias": nrm(ks[20], (N_EXPERTS,), 0.01),
        "w_expert_gate": nrm(ks[21], (DEPTH, N_EXPERTS, D_MODEL, D_EXPERT), D_MODEL ** -0.5),
        "w_expert_up": nrm(ks[22], (DEPTH, N_EXPERTS, D_MODEL, D_EXPERT), D_MODEL ** -0.5),
        "w_expert_down": nrm(ks[23], (DEPTH, N_EXPERTS, D_EXPERT, D_MODEL), D_EXPERT ** -0.5),
        "final_norm_w": 1.0 + nrm(ks[24], (D_MODEL,), 0.02),
    }

def reference(x, c, w_ada, b_ada, norm_mix_w, norm_ffn_w, w_in, conv_w, conv_b, ssd_dt_bias, ssd_a_log,
              ssd_d, ssd_norm_w, diff_lambda, diff_subln_w, hgrn_lb_logits, hgrn_norm_w, w_merge, w_out,
              w_router, router_bias, w_expert_gate, w_expert_up, w_expert_down, final_norm_w):
    lb_p = jax.nn.softmax(hgrn_lb_logits.astype(jnp.float32), axis=0)
    lower_bounds = jnp.cumsum(lb_p, axis=0) - lb_p[0]
    c_act = jax.nn.silu(c)
    for l in range(DEPTH):
        mod = c_act @ w_ada[l] + b_ada[l]
        sh1, sc1, g1, sh2, sc2, g2 = jnp.split(mod, 6, axis=-1)
        h = modulate(rms_norm(x, norm_mix_w[l]), sh1, sc1)
        mix = token_mixer(h, l, w_in[l], conv_w[l], conv_b[l], ssd_dt_bias[l], ssd_a_log[l], ssd_d[l],
                          ssd_norm_w[l], diff_lambda[l], diff_subln_w[l], lower_bounds[l], hgrn_norm_w[l],
                          w_merge[l], w_out[l])
        x = x + g1[:, None, :] * mix
        h = modulate(rms_norm(x, norm_ffn_w[l]), sh2, sc2)
        x = x + g2[:, None, :] * moe_ffn(h, w_router, router_bias, w_expert_gate[l], w_expert_up[l], w_expert_down[l])
    return rms_norm(x, final_norm_w)


_drawn_inputs = setup_inputs


def setup_inputs(seed=0):
    import zlib

    import numpy as np

    out = dict(_drawn_inputs(seed))
    spreads = {}
    factors = {'norm_mix_w': 3.385,
     'conv_b': 42.27,
     'ssd_norm_w': 54.431,
     'diff_lambda': 8.0,
     'diff_subln_w': 64.0,
     'hgrn_norm_w': 7.859,
     'final_norm_w': 8.349,
     'norm_ffn_w': 8.0,
     'ssd_d': 8.0,
     'router_bias': 4.178}
    for name, (base, spread) in spreads.items():
        noise = np.random.default_rng([zlib.crc32(name.encode()), seed]).standard_normal(out[name].shape)
        drawn = base * np.exp(spread * noise) if base else spread * noise
        out[name] = jnp.asarray(drawn.astype(out[name].dtype))
    for name, factor in factors.items():
        out[name] = (out[name] * factor).astype(out[name].dtype)
    return out
```

```python
from contextlib import ExitStack

import concourse.bass as bass
from concourse import mybir

F32 = mybir.dt.float32
U32 = mybir.dt.uint32
ALU = mybir.AluOpType
ACT = mybir.ActivationFunctionType
AX_X = mybir.AxisListType.X

P = 128
T = 512
NT = T // P
D = 1024
KD = D // P
BW = 512
KB = BW // P
EPS = 1e-6
NEG = -1e30
SSD_H, SSD_P = 8, 64
CONV_CH, CONV_K = 768, 4
DIL_H, DIL_D = 4, 128
DIL_BLOCKS = 15
DIFF_H = 4
HG_H = 8
LEVELS = [1, 2, 4, 8, 16, 32, 64]
LAM_INIT = 0.8 - 0.6
N_EXP, GROUPS, F_EXP = 64, 8, 256
BLK = 64
MAX_BLOCKS = N_EXP + (2 * T - N_EXP) // BLK
E_SLOTS = 4
N_BLK = -(-MAX_BLOCKS // E_SLOTS) * E_SLOTS
MIN_BLOCKS = 2 * T // BLK
LIST = (N_BLK + 2) * BLK

C_Z, C_XBC, C_DT = 0, 512, 1280
C_QB, C_KB, C_VB = 1288, 2824, 4360
C_QC, C_KC, C_VC = 5896, 6408, 6920
C_QD, C_FD, C_ID, C_GD = 7432, 7944, 8456, 8968
C_GATE = 9480

R_BADA, R_NMIX, R_NFFN, R_FIN, R_CONVB, R_CONVW, R_SSDN, R_SUBLN, R_HGN, R_LB = 0, 48, 56, 64, 72, 78, 102, 106, 107, 108
N_ROWS = 112
B_DTB, B_ALOG, B_DSK, B_LAM, B_RB = 0, 8, 16, 24, 280
N_BC = 344

STAGE = 99


class Order:

    def __init__(self, eng, own):
        self.eng, self.own, self.count = eng, own, {}

    def __call__(self, ins, sem=None):
        sem = self.own if sem is None else sem
        ins.then_inc(sem, 1)
        self.count[sem.name] = self.count.get(sem.name, 0) + 1
        self.eng.wait_ge(sem, self.count[sem.name])


def tokens_of(view, g, a):
    return view[:, P * a:P * a + P] if g == 0 else view.rearrange("p (i r) -> p r i", r=4)[:, a, :]


def build(nc, x, c, w_ada, b_ada, norm_mix_w, norm_ffn_w, w_in, conv_w, conv_b, ssd_dt_bias, ssd_a_log,
          ssd_d, ssd_norm_w, diff_lambda, diff_subln_w, hgrn_lb_logits, hgrn_norm_w, w_merge, w_out,
          w_router, router_bias, w_expert_gate, w_expert_up, w_expert_down, final_norm_w,
          list_dram, h2_dram, y_dram, stat_dram, weight_dram, out):
    x_dram = x.rearrange("a (i p) d -> p (a i) d", p=P)
    out_dram = out.rearrange("a (i p) d -> p (a i) d", p=P)
    ada_dram = w_ada[0].rearrange("(p k) n -> p k n", p=P)
    in_dram = w_in[0].rearrange("(k p) n -> p k n", p=P)

    with ExitStack() as ctx:
        def sb(name, shape, dt=F32):
            return ctx.enter_context(nc.sbuf_tensor(name, shape, dt))

        def sem(name):
            return ctx.enter_context(nc.semaphore(name))

        proj_ps = [ctx.enter_context(nc.psum_tensor(f"proj_ps{i}", [P, 512], F32)) for i in range(2)]
        bank = [ctx.enter_context(nc.psum_tensor(f"bank{i}", [P, 512], F32)) for i in range(6)]

        ident = sb("ident", [P, P])
        ones = sb("ones", [P, P])
        upper = sb("upper", [P, P])
        upper_strict = sb("upper_strict", [P, P])
        causal = sb("causal", [P, P])
        band_prev = sb("band_prev", [P, P])
        apart = sb("apart", [P, P], U32)
        causal_4th = sb("causal_4th", [P, P])
        level_mask = sb("level_mask", [P, len(LEVELS), P])
        two_heads = sb("two_heads", [P, P])
        iota_exp = sb("iota_exp", [P, N_EXP])
        iota_grp = sb("iota_grp", [P, GROUPS])
        iota_blk = sb("iota_blk", [N_EXP, N_BLK])
        entry = sb("entry", [P, NT, 2, 2], U32)
        rows = sb("rows", [N_ROWS, P])
        cols = sb("cols", [P, N_ROWS])
        bc_row = sb("bc_row", [1, N_BC])
        bc = sb("bc", [P, N_BC])
        mod = sb("mod", [P, 48])
        c_raw = sb("c_raw", [P, KD])
        c_act = sb("c_act", [P, KD])
        scale_mix = sb("scale_mix", [P, KD])
        scale_ffn = sb("scale_ffn", [P, KD])
        hT = sb("hT", [P, KD, T])
        branchT = sb("branchT", [P, 4 * KB, T])
        w_ring = [sb(f"w_ring{i}", [P, KD * 512]) for i in range(2)]
        small = sb("small", [P, 1024])
        arena = sb("arena", [P, 25600])
        taken = {}

        def place(who, n):
            at = taken.get(who, 0)
            taken[who] = at + n
            assert taken[who] <= 25600, (who, taken[who])
            return arena[:, at:at + n]

        w_slot = [w[:].rearrange("p (k n) -> p k n", k=KD) for w in w_ring]

        dve_order, act_order, pool_order = sem("dve_order"), sem("act_order"), sem("pool_order")
        consts_ready, apart_ready = sem("consts_ready"), sem("apart_ready")
        x_loaded, vec_loaded = sem("x_loaded"), sem("vec_loaded")
        w_loaded = [sem(f"w_loaded{i}") for i in range(2)]
        w_used = sem("w_used")
        cols_turned, bc_spread = sem("cols_turned"), sem("bc_spread")
        c_ready = sem("c_ready")
        mod_copied = sem("mod_copied")
        xn_ready = sem("xn_ready")
        x_turned, h_ready = sem("x_turned"), sem("h_ready")
        proj_done, proj_out = sem("proj_done"), sem("proj_out")
        ssd_conv, ssd_act = sem("ssd_conv"), sem("ssd_act")
        ssd_turned, ssd_tok = sem("ssd_turned"), sem("ssd_tok")
        dt_abs, dt_exp, dt_arg, dt_ln = sem("dt_abs"), sem("dt_exp"), sem("dt_arg"), sem("dt_ln")
        adt_ready, acs_done, acs_ready = sem("adt_ready"), sem("acs_done"), sem("acs_ready")
        acs_exp = sem("acs_exp")
        ssd_score, ssd_diff, ssd_decay, ssd_m = sem("ssd_score"), sem("ssd_diff"), sem("ssd_decay"), sem("ssd_m")
        ssd_y, ssd_state, ssd_gated, squared = sem("ssd_y"), sem("ssd_state"), sem("ssd_gated"), sem("squared")
        z_act, var_ready, std_ready = sem("z_act"), sem("var_ready"), sem("std_ready")
        ssd_o, ssd_oT, ssd_out = sem("ssd_o"), sem("ssd_oT"), sem("ssd_out")

        x_tok = place("open", NT * D).rearrange("p (i d) -> p i d", i=NT)
        x_nrm = place("open", NT * D).rearrange("p (i d) -> p i d", i=NT)
        junk = place("open", D)
        at = [0]

        def sm(n):
            at[0] += n
            assert at[0] <= 1024
            return small[:, at[0] - n:at[0]]

        x_sq, x_var, x_std, x_rstd = sm(NT), sm(NT), sm(NT), sm(NT)

        def over(ap, n):
            return ap.unsqueeze(1).to_broadcast([ap.shape[0], n, ap.shape[1]])

        def along(ap, n):
            return ap.unsqueeze(2).to_broadcast([ap.shape[0], ap.shape[1], n])

        PROJ = [("z", C_Z, 512, 4), ("xbc_a", C_XBC, 512, 4), ("xbc_b", C_XBC + 512, 264, 3),
                ("q_d", C_QD, 512, 4), ("f_d", C_FD, 512, 4), ("i_d", C_ID, 512, 4), ("g_d", C_GD, 512, 4),
                ("q_c", C_QC, 512, 4), ("k_c", C_KC, 512, 4), ("v_c", C_VC, 512, 4)]
        for g in range(3):
            PROJ += [(f"q_b{g}", C_QB + 512 * g, 512, 4), (f"k_b{g}", C_KB + 512 * g, 512, 4),
                     (f"v_b{g}", C_VB + 512 * g, 512, 4)]
        ADA_FIRST, ADA = 4, 12
        unit_of = {name: ADA_FIRST + i for i, (name, _, _, _) in enumerate(PROJ)}
        first_out = {name: sum(o for _, _, _, o in PROJ[:i]) for i, (name, _, _, _) in enumerate(PROJ)}
        outs_of = {name: o for name, _, _, o in PROJ}
        N_PROJ_UNITS = ADA_FIRST + len(PROJ)

        def out_ready(name):
            return first_out[name] + outs_of[name]

        xbc_raw = place("ssd", 6 * (T + 3)).rearrange("p (c t) -> p c t", c=6)
        xbcT = place("ssd", 6 * T).rearrange("p (c t) -> p c t", c=6)
        z_tok = place("ssd", NT * BW).rearrange("p (i n) -> p i n", i=NT)
        xs_tok = place("ssd", NT * BW).rearrange("p (i n) -> p i n", i=NT)
        xs_dt = place("ssd", 2 * BW).rearrange("p (i n) -> p i n", i=2)
        xs_dec = place("ssd", 2 * BW).rearrange("p (i n) -> p i n", i=2)
        b_tok = place("ssd", NT * P).rearrange("p (i n) -> p i n", i=NT)
        ssd_l = place("ssd", SSD_H * P).rearrange("p (h l) -> p h l", h=SSD_H)
        ssd_cb = place("ssd", 2 * P).rearrange("p (g l) -> p g l", g=2)
        ssd_r = place("ssd", BW)
        ssd_tmp = place("ssd", BW)
        ssd_yt = place("ssd", BW)
        dt_raw, dt_a, dt_e, dt, adt = sm(32), sm(32), sm(32), sm(32), sm(32)
        a_neg = sm(8)
        acs, eacs, dec = sm(64), sm(64), sm(32)
        y_sq, y_var, y_std, y_rstd = sm(NT), sm(NT), sm(NT), sm(NT)

        def hg_tiles():
            return place("hg", NT * T).rearrange("p (n t) -> p n t", n=NT)

        hg_q, hg_k, hg_v, hg_g, hg_log, hg_cum = (hg_tiles() for _ in range(6))
        hg_qk = [hg_tiles() for _ in range(2)]
        hg_ktok = hg_tiles()
        hg_qg = hg_log
        hg_attn = place("hg", NT * 2 * NT * P).rearrange("p (i s n q) -> p i s n q", i=NT, s=2, n=NT)
        hg_r = place("hg", BW).rearrange("p (n v) -> p n v", n=NT)
        hg_tmp, hg_o = place("hg", BW), place("hg", BW)
        lb_e, lb_r, lb, lb_rest = sm(4), sm(4), sm(4), sm(4)
        hg_last = sm(16)
        hg_sq, hg_var, hg_std, hg_rstd = sm(8), sm(8), sm(8), sm(8)
        lb_arg, lb_exp = sem("lb_arg"), sem("lb_exp")
        hg_sig, hg_f, hg_ln, hg_scan = sem("hg_sig"), sem("hg_f"), sem("hg_ln"), sem("hg_scan")
        hg_silu, hg_expq, hg_expk, hg_expl = sem("hg_silu"), sem("hg_expq"), sem("hg_expk"), sem("hg_expl")
        hg_kgarg, hg_kg, hg_qgr = sem("hg_kgarg"), sem("hg_kg"), sem("hg_qgr")
        hg_kturned, hg_kcopied, hg_zeroed = sem("hg_kturned"), sem("hg_kcopied"), sem("hg_zeroed")
        hg_dist, hg_decay, hg_scaled = sem("hg_dist"), sem("hg_decay"), sem("hg_scaled")
        hg_score, hg_pick, hg_y, hg_state = sem("hg_score"), sem("hg_pick"), sem("hg_y"), sem("hg_state")
        hg_ready, hg_oT, hg_out = sem("hg_ready"), sem("hg_oT"), sem("hg_out")

        df_q, df_k, df_v = (place("diff", NT * T).rearrange("p (n t) -> p n t", n=NT) for _ in range(3))
        df_s = place("diff", 4 * T).rearrange("p (b m t) -> p b m t", b=2, m=2)
        df_attn = place("diff", 2 * T).rearrange("p (b t) -> p b t", b=2)
        df_attnT = place("diff", 2 * T).rearrange("p (b t) -> p b t", b=2)
        df_tmp, df_o = place("diff", BW), place("diff", BW)
        lam_p, lam_s, lam_e, lam_neg, sub_w = sm(128), sm(2), sm(2), sm(1), sm(1)
        df_nmax, df_den, df_r = sm(4), sm(4), sm(4)
        df_sq, df_var, df_std, df_rstd = sm(4), sm(4), sm(4), sm(4)
        lam_arg, lam_exp = sem("lam_arg"), sem("lam_exp")
        df_score, df_masked, df_prob, df_mixed = sem("df_score"), sem("df_masked"), sem("df_prob"), sem("df_mixed")
        df_turned, df_copied, df_y = sem("df_turned"), sem("df_copied"), sem("df_y")
        df_ready, df_oT, df_out = sem("df_ready"), sem("df_oT"), sem("df_out")

        dl_q, dl_k = ([place("dil", NT * T).rearrange("p (n t) -> p n t", n=NT) for _ in range(2)] for _ in range(2))
        dl_v = [place("dil", NT * BW).rearrange("p (i n) -> p i n", i=NT) for _ in range(3)]
        dl_p = place("dil", DIL_H * DIL_BLOCKS * P).rearrange("p (j b k) -> p j b k", j=DIL_H, b=DIL_BLOCKS)
        dl_pT = place("dil", DIL_BLOCKS * P).rearrange("p (b k) -> p b k", b=DIL_BLOCKS)
        dl_stat = [sm(32).rearrange("p (a v) -> p a v", v=8) for _ in range(3)]
        dl_prev = sm(32).rearrange("p (a v) -> p a v", v=8)
        dl_nat = [sm(32).rearrange("p (a v) -> p a v", v=8) for _ in range(2)]
        dl_w = [sm(16).rearrange("p (a j) -> p a j", j=4) for _ in range(3)]
        dl_wg = [sm(16).rearrange("p (a j) -> p a j", j=4) for _ in range(2)]
        dl_low, dl_z, dl_t = (sm(16).rearrange("p (a j) -> p a j", j=4) for _ in range(3))
        dl_score, dl_masked, dl_prob = sem("dl_score"), sem("dl_masked"), sem("dl_prob")
        dl_stored, dl_back, dl_wstored, dl_wback = sem("dl_stored"), sem("dl_back"), sem("dl_wstored"), sem("dl_wback")
        dl_warg, dl_wexp, dl_weighed, dl_scaled = sem("dl_warg"), sem("dl_wexp"), sem("dl_weighed"), sem("dl_scaled")
        dl_turned, dl_copied, dl_y, dl_out = sem("dl_turned"), sem("dl_copied"), sem("dl_y"), sem("dl_out")
        DIL_SCORES = []
        for g in range(3):
            for j in range(DIL_H):
                DIL_SCORES.append((g, j, (0, 7, 11)[g], range(NT), False))
                if g == 0:
                    DIL_SCORES.append((g, j, 4, range(1, NT), True))

        gate_sb = place("late", 2 * T).rearrange("p (b t) -> p b t", b=2)
        merged = place("late", KD * T).rearrange("p (k t) -> p k t", k=KD)
        m_ring = [place("late", KB * 512).rearrange("p (k n) -> p k n", k=KB) for _ in range(2)]
        x2 = place("late", NT * D).rearrange("p (i d) -> p i d", i=NT)
        bc_gate1, bc_scale2, bc_shift2, bc_gate2, bc_final = (place("late", D) for _ in range(5))
        xg = [place("late", D) for _ in range(2)]
        xgT = [place("late", KD * BLK).rearrange("p (k t) -> p k t", k=KD) for _ in range(2)]
        e_act, e_hid = (place("late", 2 * BLK).rearrange("p (j t) -> p j t", j=2) for _ in range(2))
        yb = [place("late", D) for _ in range(2)]
        h2 = merged.rearrange("p k t -> p (k t)").rearrange("p (i d) -> p i d", i=NT)
        h2T = hT
        old_branches = branchT[:].rearrange("p c t -> p (c t)")
        w_wide = [w_slot[0], w_slot[1], hT[:], old_branches[:, 0:KD * 512].rearrange("p (k n) -> p k n", k=KD)]
        w_down = [m.rearrange("p k n -> p (k n)") for m in m_ring] + [old_branches[:, KD * 512 + 2 * D * i:KD * 512 + 2 * D * i + 2 * D] for i in range(2)]
        w_down = [w.rearrange("p (j d) -> p j d", j=2) for w in w_down]
        scores = gate_sb[:, 0, 0:256].rearrange("p (i e) -> p i e", i=NT)
        sel = gate_sb[:, 0, 256:512].rearrange("p (i e) -> p i e", i=NT)
        hot = [gate_sb[:, 1, 256 * s:256 * s + 256].rearrange("p (i e) -> p i e", i=NT) for s in range(2)]
        both_hot = sb("both_hot", [P, NT, N_EXP])
        rank = sb("rank", [P, NT, N_EXP])
        picked = sb("picked", [P, NT, N_EXP])
        best8 = sb("best8", [P, NT * GROUPS, 8])
        grp_score = sm(32).rearrange("p (i g) -> p i g", i=NT)
        grp_pen = sm(32).rearrange("p (i g) -> p i g", i=NT)
        top8 = sb("top8", [P, NT, 8])
        top_i = sb("top_i", [P, NT, 8], U32)
        top_f = sb("top_f", [P, NT, 8])
        n_blk_e, blk_end = sb("n_blk_e", [P, N_EXP]), sb("blk_end", [P, N_EXP])
        pair_s = sm(8).rearrange("p (i s) -> p i s", i=NT)
        pair_z = sm(4)
        pair_row = sm(8).rearrange("p (i s) -> p i s", i=NT)
        row_id = sb("row_id", [P, NT, 2], U32)
        nbc, endc = sb("nbc", [N_EXP, 2]), sb("endc", [N_EXP, 1])
        ended = sb("ended", [N_EXP, N_BLK])
        blk_exp = sb("blk_exp", [1, N_BLK], U32)
        n_blocks = sb("n_blocks", [1, 1], U32)
        no_entry = sb("no_entry", [P, LIST // P, 2], U32)
        blk_tok = [sb(f"blk_tok{i}", [BLK, 2], U32) for i in range(2)]
        blk_dst = [sb(f"blk_dst{i}", [BLK, 2], U32) for i in range(2)]
        f_sq, f_var, f_std, f_rstd = sm(8), sm(8), sm(8), sm(8)
        out_ring = [w_ring[1][:, D * i:D * i + D] for i in range(NT)]
        yg = [w_ring[0][:, D * i:D * i + D] for i in range(4)]

        m_loaded = [sem(f"m_loaded{i}") for i in range(2)]
        gate_done, gate_out, merge_done, merge_out = sem("gate_done"), sem("gate_out"), sem("merge_done"), sem("merge_out")
        merge_mul = sem("merge_mul")
        x2_loaded, scale2_ready = sem("x2_loaded"), sem("scale2_ready")
        row_spread, row_ready = sem("row_spread"), sem("row_ready")
        o_done, o_out = sem("o_done"), sem("o_out")
        h2_ready, h2_stored, h2_turned, h2T_ready = sem("h2_ready"), sem("h2_stored"), sem("h2_turned"), sem("h2T_ready")
        router_loaded, routed, scored = sem("router_loaded"), sem("routed"), sem("scored")
        hot_ready, ranked, nbc_ready, ends_done, ended_ready, owners_done = (
            sem("hot_ready"), sem("ranked"), sem("nbc_ready"), sem("ends_done"), sem("ended_ready"), sem("owners_done"))
        plan_ready, rows_ready, list_zeroed, list_filled = sem("plan_ready"), sem("rows_ready"), sem("list_zeroed"), sem("list_filled")
        passed = sem("passed")

        e_loaded = [sem(f"e_loaded{i}") for i in range(E_SLOTS)]
        down_loaded = [sem(f"down_loaded{i}") for i in range(E_SLOTS)]
        ids_loaded, dst_loaded, xg_loaded = sem("ids_loaded"), sem("dst_loaded"), sem("xg_loaded")
        xg_turned, xgT_ready = sem("xg_turned"), sem("xgT_ready")
        gu_done, gu_act, hid_ready = sem("gu_done"), sem("gu_act"), sem("hid_ready")
        down_done, y_act, y_dve = sem("down_done"), sem("y_act"), sem("y_dve")
        y_stored = [sem(f"y_stored{i}") for i in range(2)]
        yg_loaded, x3_ready = [sem(f"yg_loaded{i}") for i in range(2)], sem("x3_ready")
        out_ready_, out_stored = sem("out_ready"), sem("out_stored")

        GATE0 = N_PROJ_UNITS + ADA - ADA_FIRST
        OUT0 = GATE0 + 8

        def in_slot(n):
            return 16 * (n // 2 + 1)

        block = ctx.enter_context(nc.Block())

        @block.sync
        def _(sp):
            def load_vec(row, src, n):
                sp.dma_start(rows[row:row + n, :], src).then_inc(vec_loaded, 16)

            for i in range(NT):
                sp.dma_start(x_tok[:, i, :], x_dram[:, i, :]).then_inc(x_loaded, 16)
            sp.dma_start(c_raw[:], c.rearrange("a (p k) -> (a p) k", k=KD)).then_inc(vec_loaded, 16)
            load_vec(R_BADA, b_ada.rearrange("a (j q) -> (a j) q", q=P), 48)
            load_vec(R_NMIX, norm_mix_w.rearrange("a (j q) -> (a j) q", q=P), KD)
            load_vec(R_NFFN, norm_ffn_w.rearrange("a (j q) -> (a j) q", q=P), KD)
            load_vec(R_FIN, final_norm_w.rearrange("(j q) -> j q", q=P), KD)
            load_vec(R_CONVB, conv_b.rearrange("a (j q) -> (a j) q", q=P), 6)
            load_vec(R_CONVW, conv_w.rearrange("a k (j q) -> (a k j) q", q=P), 24)
            load_vec(R_SSDN, ssd_norm_w.rearrange("a (j q) -> (a j) q", q=P), KB)
            load_vec(R_SUBLN, diff_subln_w, 1)
            for half in range(2):
                sp.dma_start(rows[R_HGN:R_HGN + 1, 64 * half:64 * half + 64], hgrn_norm_w).then_inc(vec_loaded, 16)
            load_vec(R_LB, hgrn_lb_logits.rearrange("a (j q) -> (a j) q", q=P), KB)
            for at_, src in ((B_DTB, ssd_dt_bias), (B_ALOG, ssd_a_log), (B_DSK, ssd_d),
                             (B_LAM, diff_lambda.rearrange("a i n -> a (i n)")),
                             (B_RB, router_bias.rearrange("(a n) -> a n", a=1))):
                n = src.shape[1]
                sp.dma_start(bc_row[:, at_:at_ + n], src).then_inc(vec_loaded, 16)

            def load_unit(n, src, width):
                if 2 <= n < ADA_FIRST + 2:
                    sp.wait_ge(w_used, n - 1)
                elif n >= 2:
                    sp.wait_ge(proj_done, out_ready(PROJ[n - 2 - ADA_FIRST][0]))
                sp.dma_start(w_slot[n % 2][:, :, 0:width], src).then_inc(w_loaded[n % 2], 16)

            for u in range(ADA_FIRST):
                load_unit(u, ada_dram[:, :, 512 * u:512 * u + 512], 512)
            for name, c0, width, _ in PROJ:
                load_unit(unit_of[name], in_dram[:, :, c0:c0 + width], width)
            def gate_unit(b, half):
                sp.dma_start(w_slot[(GATE0 + half) % 2], in_dram[:, :, bass.ds(C_GATE + b * D + 512 * half, 512)])\
                  .then_inc(w_loaded[(GATE0 + half) % 2], 16)
                sp.dma_start(m_ring[half], w_merge[0][bass.ds(b, 1)].rearrange("a (k p) n -> p (a k) n", p=P)[:, :, 512 * half:512 * half + 512])\
                  .then_inc(m_loaded[half], 16)

            for u in range(2):
                n = N_PROJ_UNITS + u
                load_unit(n, ada_dram[:, :, 512 * (ADA_FIRST + u):512 * (ADA_FIRST + u) + 512], 512)
            with sp.Fori(1, (ADA - ADA_FIRST) // 2) as i:
                for s in range(2):
                    sp.wait_ge(w_used, ADA_FIRST + 2 * i + s - 1)
                    sp.dma_start(w_slot[(N_PROJ_UNITS + s) % 2], ada_dram[:, :, bass.ds(512 * ADA_FIRST + 1024 * i + 512 * s, 512)])\
                      .then_inc(w_loaded[(N_PROJ_UNITS + s) % 2], 16)
            sp.wait_ge(dl_out, NT)
            sp.dma_start(x2, x_dram).then_inc(x2_loaded, 16)
            for half in range(2):
                sp.wait_ge(w_used, ADA - 1 + half)
                gate_unit(0, half)
            with sp.Fori(1, 4) as b:
                for half in range(2):
                    sp.wait_ge(merge_done, 8 * b + 4 * half - 4)
                    gate_unit(b, half)
            for half in range(2):
                sp.wait_ge(merge_done, 28 + 4 * half)
                sp.dma_start(w_slot[(OUT0 + half) % 2], w_out[0].rearrange("(k p) n -> p k n", p=P)[:, :, 512 * half:512 * half + 512])\
                  .then_inc(w_loaded[(OUT0 + half) % 2], 16)
            sp.dma_start(m_ring[0].rearrange("p k n -> p (k n)")[:, 0:KD * N_EXP].rearrange("p (k e) -> p k e", k=KD),
                         w_router.rearrange("(k p) e -> p k e", p=P)).then_inc(router_loaded, 16)
            for i in range(NT):
                sp.wait_ge(h2_ready, i + 1)
                sp.dma_start(h2_dram.rearrange("(i p) d -> p i d", p=P)[:, i, :], h2[:, i, :]).then_inc(h2_stored, 16)

            sp.wait_ge(o_done, 8)
            sp.wait_ge(routed, 1)
            sp.wait_ge(plan_ready, 2)
            n_valid = sp.value_load(n_blocks[0:1, 0:1], min_val=MIN_BLOCKS, max_val=MAX_BLOCKS)

            def expert_weights(b, s, first):
                e = sp.value_load(blk_exp[0:1, bass.ds(b, 1)], min_val=0, max_val=N_EXP - 1)
                if not first:
                    sp.wait_ge(gu_done, b - (E_SLOTS - 1))
                for half, w in enumerate((w_expert_gate, w_expert_up)):
                    sp.dma_start(w_wide[s][:, :, F_EXP * half:F_EXP * half + F_EXP],
                                 w[0][bass.ds(e, 1)].rearrange("a (p k) f -> (a p) k f", k=KD)).then_inc(e_loaded[s], 16)
                if not first:
                    sp.wait_ge(down_done, b - (E_SLOTS - 1))
                sp.dma_start(w_down[s], w_expert_down[0][bass.ds(e, 1)].rearrange("a (j p) d -> p (a j) d", j=2))\
                  .then_inc(down_loaded[s], 16)

            for s in range(E_SLOTS):
                expert_weights(s, s, True)
            with sp.Fori(1, N_BLK // E_SLOTS) as it:
                for s in range(E_SLOTS):
                    b = E_SLOTS * it + s
                    with sp.If(b < n_valid):
                        expert_weights(b, s, False)
            for s in range(2):
                sp.wait_ge(y_stored[s], 16 * ((n_valid + 1 - s) // 2))
            for i in range(NT):
                for s in range(2):
                    if i >= 2:
                        sp.wait_ge(x3_ready, i - 1)
                    sp.dma_start(yg[2 * (i % 2) + s], y_dram[T * s + P * i:T * s + P * i + P, :]).then_inc(yg_loaded[i % 2], 16)

        @block.gpsimd
        def _(pool):
            p = Order(pool, pool_order)
            p(pool.memset(ones[:], 1.0))
            for m in (ident, causal, band_prev, level_mask):
                p(pool.memset(m[:], 0.0))
            p(pool.affine_select(out=ident[:], in_=ident[:], compare_op=ALU.not_equal, fill=1.0, base=0,
                                 pattern=[[-1, P]], channel_multiplier=1))
            p(pool.affine_select(out=upper[:], in_=ones[:], compare_op=ALU.is_ge, fill=0.0, base=0,
                                 pattern=[[1, P]], channel_multiplier=-1))
            p(pool.affine_select(out=upper_strict[:], in_=ones[:], compare_op=ALU.is_gt, fill=0.0, base=0,
                                 pattern=[[1, P]], channel_multiplier=-1))
            p(pool.affine_select(out=causal[:], in_=causal[:], compare_op=ALU.is_ge, fill=NEG, base=0,
                                 pattern=[[-1, P]], channel_multiplier=1))
            p(pool.affine_select(out=band_prev[:], in_=band_prev[:], compare_op=ALU.is_ge, fill=NEG, base=0,
                                 pattern=[[1, P]], channel_multiplier=-1))
            p(pool.iota(apart[:], pattern=[[-1, P]], base=P, channel_multiplier=1), apart_ready)
            for n, b in enumerate(LEVELS):
                m = level_mask[:, n, :].rearrange("p (k s i) -> p k s i", s=2, i=b)[:, :, 1, :]
                one = ones[:].rearrange("p (k s i) -> p k s i", s=2, i=b)[:, :, 1, :]
                p(pool.affine_select(out=m, in_=one, compare_op=ALU.is_ge, fill=0.0, base=0,
                                     pattern=[[-2 * b, P // (2 * b)], [0, b]], channel_multiplier=1))
                p(pool.affine_select(out=m, in_=m, compare_op=ALU.is_ge, fill=0.0, base=b - 1,
                                     pattern=[[2 * b, P // (2 * b)], [0, b]], channel_multiplier=-1))
            h2 = two_heads[:].rearrange("p (h n) -> p h n", h=2)
            p(pool.affine_select(out=h2, in_=ones[:].rearrange("p (h n) -> p h n", h=2), compare_op=ALU.is_ge,
                                 fill=0.0, base=0, pattern=[[-64, 2], [0, 64]], channel_multiplier=1))
            p(pool.affine_select(out=h2, in_=h2, compare_op=ALU.is_ge, fill=0.0, base=63,
                                 pattern=[[64, 2], [0, 64]], channel_multiplier=-1))
            pool.iota(iota_exp[:], pattern=[[1, N_EXP]], base=0, channel_multiplier=0,
                      allow_small_or_imprecise_dtypes=True).then_inc(consts_ready, 1)
            pool.iota(iota_grp[:], pattern=[[1, GROUPS]], base=0, channel_multiplier=0,
                      allow_small_or_imprecise_dtypes=True).then_inc(consts_ready, 1)
            pool.iota(iota_blk[:], pattern=[[1, N_BLK]], base=0, channel_multiplier=0,
                      allow_small_or_imprecise_dtypes=True).then_inc(consts_ready, 1)
            pool.iota(entry[:, :, :, 0], pattern=[[P, NT], [0, 2]], base=0, channel_multiplier=1).then_inc(consts_ready, 1)
            pool.iota(entry[:, :, :, 1], pattern=[[P, NT], [T, 2]], base=0, channel_multiplier=1).then_inc(consts_ready, 1)
            pool.wait_ge(ssd_out, NT)
            pool.memset(hg_attn, 0.0).then_inc(hg_zeroed, 1)
            pool.wait_ge(dl_prob, len(DIL_SCORES))
            for g in range(2):
                pool.dma_start(stat_dram[g].rearrange("(p a) v -> p a v", a=4), dl_stat[g + 1]).then_inc(dl_stored, 16)
            pool.wait_ge(dl_stored, 32)
            for g in range(2):
                pool.dma_start(dl_nat[g], stat_dram[g].rearrange("(a p) v -> p a v", p=P)).then_inc(dl_back, 16)
            pool.wait_ge(dl_weighed, 3)
            for g in range(2):
                pool.dma_start(weight_dram[g].rearrange("(a p) v -> p a v", p=P), dl_w[g + 1]).then_inc(dl_wstored, 16)
            pool.wait_ge(dl_wstored, 32)
            for g in range(2):
                pool.dma_start(dl_wg[g], weight_dram[g].rearrange("(p a) v -> p a v", a=4)).then_inc(dl_wback, 16)
            p(pool.memset(no_entry[:, :, 0], 0))
            p(pool.memset(no_entry[:, :, 1], 2 * T))
            pool.dma_start(list_dram.rearrange("(p n) a -> p n a", p=P), no_entry[:]).then_inc(list_zeroed, 16)
            pool.wait_ge(list_zeroed, 16)
            pool.wait_ge(rows_ready, 1)
            for i in range(NT):
                for s in range(2):
                    pool.indirect_dma_start(out=list_dram, out_offset=bass.IndirectOffsetOnAxis(ap=row_id[:, i, s:s + 1], axis=0),
                                            in_=entry[:, i, s, :], in_offset=None).then_inc(list_filled, 16)
            pool.wait_ge(list_filled, 16 * 2 * NT)
            pool.wait_ge(h2_stored, 16 * NT)
            pool.wait_ge(plan_ready, 2)
            n_valid = pool.value_load(n_blocks[0:1, 0:1], min_val=MIN_BLOCKS, max_val=MAX_BLOCKS)

            def gather(b, s):
                pool.dma_start(blk_tok[s][:], list_dram[bass.ds(b * BLK, BLK), :]).then_inc(ids_loaded, 16)
                pool.wait_ge(ids_loaded, 16 * b + 16)
                pool.sem_inc(passed)
                pool.indirect_dma_start(out=xg[s][0:BLK, :], out_offset=None, in_=h2_dram,
                                        in_offset=bass.IndirectOffsetOnAxis(ap=blk_tok[s][:, 0:1], axis=0)).then_inc(xg_loaded, 16)

            def scatter(b, s):
                pool.dma_start(blk_dst[s][:], list_dram[bass.ds(b * BLK, BLK), :]).then_inc(dst_loaded, 16)
                pool.wait_ge(dst_loaded, 16 * b + 16)
                pool.wait_ge(y_act, b + 1)
                pool.wait_ge(y_dve, b + 1)
                pool.sem_inc(passed)
                pool.indirect_dma_start(out=y_dram, out_offset=bass.IndirectOffsetOnAxis(ap=blk_dst[s][:, 1:2], axis=0),
                                        in_=yb[s][0:BLK, :], in_offset=None, bounds_check=2 * T - 1, oob_is_err=False).then_inc(y_stored[s], 16)

            gather(0, 0)
            gather(1, 1)
            pool.wait_ge(xg_turned, 1)
            gather(2, 0)
            scatter(0, 0)
            with pool.Fori(1, N_BLK // 2) as it:
                for s in range(2):
                    b = 2 * it + s
                    with pool.If(b < n_valid):
                        pool.wait_ge(xg_turned, b)
                        gather(b + 1, 1 - s)
                    with pool.If(b - 1 < n_valid):
                        scatter(b - 1, 1 - s)

        @block.tensor
        def _(pe):
            pe.wait_ge(consts_ready, 5)
            pe.wait_ge(vec_loaded, 16 * 17)
            pe.transpose(bank[2][:, 0:N_ROWS], rows[:], ident[0:N_ROWS, 0:N_ROWS]).then_inc(cols_turned, 1)
            pe.matmul(bank[3][:, 0:N_BC], ones[0:1, :], bc_row[:], start=True, stop=True).then_inc(bc_spread, 1)

            def ada(n, u, psum):
                for j in range(4):
                    for k in range(KD):
                        mm = pe.matmul(psum(j), w_slot[n % 2][:, k, P * j:P * j + P], c_act[:, k:k + 1],
                                       start=(k == 0), stop=(k == KD - 1))
                mm.then_inc(w_used, 1)

            pe.wait_ge(c_ready, 1)
            for u in range(ADA_FIRST):
                pe.wait_ge(w_loaded[u % 2], 16 * (u // 2 + 1))
                ada(u, u, lambda j: bank[4][:, 4 * u + j:4 * u + j + 1])

            pe.wait_ge(xn_ready, NT)
            for k in range(KD):
                if k >= 2:
                    pe.wait_ge(h_ready, k - 1)
                for i in range(NT):
                    mm = pe.transpose(bank[k % 2][:, P * i:P * i + P], x_nrm[:, i, P * k:P * k + P], ident[:])
                mm.then_inc(x_turned, 1)
            pe.wait_ge(h_ready, KD)

            def start_unit(name):
                n = unit_of[name]
                pe.wait_ge(w_loaded[n % 2], 16 * (n // 2 + 1))
                return w_slot[n % 2]

            def free_bank(o):
                if o >= 2:
                    pe.wait_ge(proj_out, o - 1)
                return proj_ps[o % 2]

            def project_ch(name, tiles):
                w, o = start_unit(name), first_out[name]
                for m in range(tiles):
                    ps = free_bank(o + m)
                    for k in range(KD):
                        mm = pe.matmul(ps[:], w[:, k, P * m:P * m + P], hT[:, k, :], start=(k == 0), stop=(k == KD - 1))
                    mm.then_inc(proj_done, 1)
                return mm

            def project_tok(name, g):
                w, o = start_unit(name), first_out[name]
                for a in range(NT):
                    ps = free_bank(o + a)
                    for k in range(KD):
                        mm = pe.matmul(ps[:], tokens_of(hT[:, k, :], g, a), w[:, k, :], start=(k == 0),
                                       stop=(k == KD - 1))
                    mm.then_inc(proj_done, 1)

            project_tok("z", 0)
            project_ch("xbc_a", 4)
            project_ch("xbc_b", 2)
            w, o = w_slot[unit_of["xbc_b"] % 2], first_out["xbc_b"] + 2
            ps = free_bank(o)
            for a in range(NT):
                for k in range(KD):
                    mm = pe.matmul(ps[:, 8 * a:8 * a + 8], hT[:, k, P * a:P * a + P], w[:, k, 256:264],
                                   start=(k == 0), stop=(k == KD - 1))
            mm.then_inc(proj_done, 1)
            pe.wait_ge(ssd_act, 6)
            for i in range(NT):
                if i >= 2:
                    pe.wait_ge(ssd_tok, i - 1)
                for t in range(4):
                    mm = pe.transpose(bank[i % 2][:, P * t:P * t + P], xbcT[:, t, P * i:P * i + P], ident[:])
                mm.then_inc(ssd_turned, 1)
            for i in range(NT):
                mm = pe.transpose(bank[2][:, P * i:P * i + P], xbcT[:, 4, P * i:P * i + P], ident[:])
            mm.then_inc(ssd_turned, 1)
            pe.wait_ge(adt_ready, 1)
            pe.matmul(bank[3][:, 0:32], upper[:], adt, start=True, stop=True)
            pe.matmul(bank[3][:, 32:64], ones[:], adt, start=True, stop=True).then_inc(acs_done, 1)
            pe.wait_ge(acs_ready, 1)
            pe.wait_ge(ssd_tok, NT + 1)
            for i in range(NT):
                s = slice(P * i, P * i + P)
                if i:
                    pe.wait_ge(ssd_m, i)
                    pe.wait_ge(ssd_state, i)
                for g in range(2):
                    pe.matmul(bank[5 * g][:, 0:P], xbcT[64 * g:64 * g + 64, 4, s], xbcT[64 * g:64 * g + 64, 5, s],
                              start=True, stop=True)
                for h in range(SSD_H):
                    mm = pe.matmul(bank[1 + h // 4][:, P * (h % 4):P * (h % 4) + P],
                                   adt[:, 8 * i + h:8 * i + h + 1].to_broadcast([P, P]), upper[:], start=True, stop=True)
                mm.then_inc(ssd_score, 1)
                pe.wait_ge(ssd_m, i + 1)
                if i:
                    pe.wait_ge(ssd_out, i)
                for h in range(SSD_H):
                    mm = pe.matmul(bank[3][:, 64 * h:64 * h + 64], ssd_l[:, h, :], xs_dt[:, i % 2, 64 * h:64 * h + 64],
                                   start=True, stop=True)
                if i:
                    pe.wait_ge(ssd_state, i)
                    mm = pe.matmul(bank[4][:], xbcT[:, 5, s], ssd_r, start=True, stop=True)
                if i < NT - 1:
                    mm = pe.matmul(bank[5][:], b_tok[:, i, :], xs_dec[:, i % 2, :], start=True, stop=True)
                mm.then_inc(ssd_y, 1)
                pe.wait_ge(ssd_o, i + 1)
                for j in range(KB):
                    mm = pe.transpose(bank[4][:, P * j:P * j + P], ssd_yt[:, P * j:P * j + P], ident[:])
                mm.then_inc(ssd_oT, 1)
            project_ch("q_d", 4)
            project_ch("f_d", 4)
            project_tok("i_d", 0)
            project_tok("g_d", 0)
            pe.wait_ge(hg_kg, 1)
            for i in range(NT):
                if i >= 2:
                    pe.wait_ge(hg_kcopied, i - 1)
                for n in range(NT):
                    mm = pe.transpose(bank[i % 2][:, P * n:P * n + P], hg_qk[0][:, n, P * i:P * i + P], ident[:])
                mm.then_inc(hg_kturned, 1)
            pe.wait_ge(hg_kcopied, NT)
            for lv in range(len(LEVELS) + 1):
                keys, queries = (hg_k, hg_q) if lv == 0 else (hg_qk[(lv - 1) % 2],) * 2
                if lv:
                    pe.wait_ge(hg_scaled, lv)
                for i in range(NT):
                    for s in range(2):
                        q = 8 * lv + 2 * i + s
                        if q >= 6:
                            pe.wait_ge(hg_pick, q - 5)
                        for n in range(NT):
                            mm = pe.matmul(bank[q % 6][:, P * n:P * n + P], keys[64 * s:64 * s + 64, n, P * i:P * i + P],
                                           queries[64 * s:64 * s + 64, n, P * i:P * i + P], start=True, stop=True)
                        mm.then_inc(hg_score, 1)
            pe.wait_ge(hg_pick, 8 * (len(LEVELS) + 1))
            pe.wait_ge(hg_qgr, 1)
            for i in range(NT):
                if i:
                    pe.wait_ge(hg_state, i)
                    pe.wait_ge(hg_ready, i)
                    for n in range(NT):
                        pe.matmul(bank[0][:, P * n:P * n + P], hg_qg[:, n, P * i:P * i + P], hg_r[:, n, :],
                                  start=(n == 0), stop=False, skip_group_check=True)
                for h in range(HG_H):
                    mm = pe.matmul(bank[0][:, 64 * h:64 * h + 64], hg_attn[:, i, h % 2, h // 2, :],
                                   hg_v[:, i, 64 * h:64 * h + 64], start=(i == 0 and h == 0), stop=(h == HG_H - 1),
                                   skip_group_check=True)
                if i < NT - 1:
                    for n in range(NT):
                        mm = pe.matmul(bank[1][:, P * n:P * n + P], hg_ktok[:, i, P * n:P * n + P],
                                       hg_v[:, i, P * n:P * n + P], start=True, stop=True)
                mm.then_inc(hg_y, 1)
                pe.wait_ge(hg_ready, i + 1)
                if i:
                    pe.wait_ge(hg_out, i)
                for j in range(KB):
                    mm = pe.transpose(bank[2][:, P * j:P * j + P], hg_o[:, P * j:P * j + P], ident[:])
                mm.then_inc(hg_oT, 1)
            project_ch("q_c", 4)
            project_ch("k_c", 4)
            project_tok("v_c", 0)
            DF_STEPS = [(i, h) for i in range(NT) for h in range(DIFF_H)]
            pe.wait_ge(proj_out, out_ready("v_c"))
            pe.wait_ge(hg_out, NT)

            def df_scores(n):
                i, h = DF_STEPS[n]
                if n >= 2:
                    pe.wait_ge(df_masked, 2 * n - 2)
                for m in range(2):
                    s = slice(64 * m, 64 * m + 64)
                    mm = pe.matmul(bank[2 * (n % 2) + m][:, 0:P * (i + 1)], df_q[s, h, P * i:P * i + P],
                                   df_k[s, h, 0:P * (i + 1)], start=True, stop=True)
                mm.then_inc(df_score, 1)

            df_scores(0)
            for n, (i, h) in enumerate(DF_STEPS):
                if n + 1 < len(DF_STEPS):
                    df_scores(n + 1)
                pe.wait_ge(df_mixed, n + 1)
                if n:
                    pe.wait_ge(df_copied, n)
                if h == 0 and i:
                    pe.wait_ge(df_out, i)
                for b in range(i + 1):
                    mm = pe.transpose(bank[4][:, P * b:P * b + P], df_attn[:, n % 2, P * b:P * b + P], ident[:])
                mm.then_inc(df_turned, 1)
                pe.wait_ge(df_copied, n + 1)
                for b in range(i + 1):
                    mm = pe.matmul(bank[5][:, P * h:P * h + P], df_attnT[:, n % 2, P * b:P * b + P],
                                   df_v[:, b, P * h:P * h + P], start=(b == 0), stop=(b == i))
                mm.then_inc(df_y, 1)
                if h == DIFF_H - 1:
                    pe.wait_ge(df_ready, i + 1)
                    for j in range(KB):
                        mm = pe.transpose(bank[4][:, P * j:P * j + P], df_o[:, P * j:P * j + P], ident[:])
                    mm.then_inc(df_oT, 1)

            for g in range(3):
                project_ch(f"q_b{g}", 4)
                project_ch(f"k_b{g}", 4)
                project_tok(f"v_b{g}", g)
                pe.wait_ge(proj_out, out_ready(f"v_b{g}"))
                if g == 0:
                    pe.wait_ge(df_out, NT)
                for n, (gg, j, _, tiles, prev) in enumerate(DIL_SCORES):
                    if gg != g:
                        continue
                    if n >= 4:
                        pe.wait_ge(dl_masked, n - 3)
                    for c_, a in enumerate(tiles):
                        mm = pe.matmul(bank[n % 4][:, P * c_:P * c_ + P], tokens_of(dl_q[g % 2][:, j, :], g, a),
                                       tokens_of(dl_k[g % 2][:, j, :], g, a - 1 if prev else a), start=True, stop=True)
                    mm.then_inc(dl_score, 1)
            for j in range(DIL_H):
                pe.wait_ge(dl_scaled, 4 * j + 4)
                if j:
                    pe.wait_ge(dl_copied, 4 * j)
                for b in range(DIL_BLOCKS):
                    mm = pe.transpose(bank[b // 4][:, P * (b % 4):P * (b % 4) + P], dl_p[:, j, b, :], ident[:])
                    if b % 4 == 3 or b == DIL_BLOCKS - 1:
                        mm.then_inc(dl_turned, 1)
                pe.wait_ge(dl_copied, 4 * j + 4)
                if j >= 2:
                    pe.wait_ge(dl_out, j - 1)
                y = bank[4 + j % 2][:]
                s = slice(P * j, P * j + P)
                for b in range(DIL_BLOCKS):
                    g, a, key = ((0, b, b) if b < 4 else (0, b - 3, b - 4) if b < 7 else
                                 (1, b - 7, b - 7) if b < 11 else (2, b - 11, b - 11))
                    mm = pe.matmul(tokens_of(y, g, a), dl_v[g][:, key, s], dl_pT[:, b, :],
                                   start=(b == 0), stop=(b == DIL_BLOCKS - 1), skip_group_check=True)
                mm.then_inc(dl_y, 1)
            with pe.Fori(0, (ADA - ADA_FIRST) // 2) as i:
                for s in range(2):
                    n = N_PROJ_UNITS + s
                    pe.wait_ge(w_loaded[n % 2], in_slot(n) + 16 * i)
                    ada(n, None, lambda j: proj_ps[0][:, bass.ds(4 * s + j + 8 * i, 1)])
            pe.wait_ge(mod_copied, 2)

            def merge_unit(b, half, first):
                pe.wait_ge(w_loaded[(GATE0 + half) % 2], in_slot(GATE0 + half) + 16 * b)
                pe.wait_ge(m_loaded[half], 16 * b + 16)
                w, wm = w_slot[(GATE0 + half) % 2], m_ring[half]
                for m in range(4):
                    t = 8 * b + 4 * half + m
                    late = not first or 4 * half + m >= 2
                    if late:
                        pe.wait_ge(gate_out, t - 1)
                    for k in range(KD):
                        mm = pe.matmul(proj_ps[m % 2][:], w[:, k, P * m:P * m + P], hT[:, k, :], start=(k == 0), stop=(k == KD - 1))
                    mm.then_inc(gate_done, 1)
                    if late:
                        pe.wait_ge(merge_out, t - 1)
                    for k in range(KB):
                        rhs = branchT[:, bass.ds(b * KB + k, 1), :].rearrange("p a t -> p (a t)")
                        mm = pe.matmul(bank[m % 2][:], wm[:, k, P * m:P * m + P], rhs, start=(k == 0), stop=(k == KB - 1))
                    mm.then_inc(merge_done, 1)

            for half in range(2):
                merge_unit(0, half, True)
            with pe.Fori(1, 4) as b:
                for half in range(2):
                    merge_unit(b, half, False)
            for v, (src, c0) in enumerate(((mod, 16), (scale_ffn, 0), (mod, 24), (mod, 40), (cols, R_FIN))):
                if v == 1:
                    pe.wait_ge(scale2_ready, 1)
                for half in range(2):
                    q = 2 * v + half
                    if q >= 2:
                        pe.wait_ge(row_ready, q - 1)
                    for j in range(4):
                        at_ = c0 + 4 * half + j
                        mm = pe.matmul(bank[2 + q % 2][:, P * j:P * j + P], src[:, at_:at_ + 1].to_broadcast([P, P]), ident[:],
                                       start=True, stop=True)
                    mm.then_inc(row_spread, 1)
            pe.wait_ge(merge_out, 32)
            for half in range(2):
                n = OUT0 + half
                pe.wait_ge(w_loaded[n % 2], in_slot(n))
                for i in range(NT):
                    o = NT * half + i
                    if o >= 2:
                        pe.wait_ge(o_out, o - 1)
                    for k in range(KD):
                        mm = pe.matmul(bank[4 + o % 2][:], merged[:, k, P * i:P * i + P], w_slot[n % 2][:, k, :],
                                       start=(k == 0), stop=(k == KD - 1))
                    mm.then_inc(o_done, 1)
            pe.wait_ge(h2_ready, NT)
            for k in range(KD):
                if k >= 2:
                    pe.wait_ge(h2T_ready, k - 1)
                for i in range(NT):
                    mm = pe.transpose(bank[k % 2][:, P * i:P * i + P], h2[:, i, P * k:P * k + P], ident[:])
                mm.then_inc(h2_turned, 1)
            pe.wait_ge(h2T_ready, KD)
            pe.wait_ge(router_loaded, 16)
            w_r = m_ring[0].rearrange("p k n -> p (k n)")[:, 0:KD * N_EXP].rearrange("p (k e) -> p k e", k=KD)
            for i in range(NT):
                for k in range(KD):
                    mm = pe.matmul(bank[2][:, N_EXP * i:N_EXP * i + N_EXP], h2T[:, k, P * i:P * i + P], w_r[:, k, :],
                                   start=(k == 0), stop=(k == KD - 1))
            mm.then_inc(routed, 1)
            pe.wait_ge(hot_ready, NT)
            for i in range(NT):
                r = bank[3][:, N_EXP * i:N_EXP * i + N_EXP]
                for j in range(i):
                    pe.matmul(r, ones[:], both_hot[:, j, :], start=(j == 0), stop=False)
                pe.matmul(r, upper_strict[:], both_hot[:, i, :], start=(i == 0), stop=True)
            for i in range(NT):
                pe.matmul(bank[4][:, 0:N_EXP], ones[:], both_hot[:, i, :], start=(i == 0), stop=(i == NT - 1))
            for i in range(NT):
                mm = pe.matmul(bank[5][0:N_EXP, 0:1], both_hot[:, i, :], ones[:, 0:1], start=(i == 0), stop=(i == NT - 1))
            mm.then_inc(ranked, 1)
            pe.wait_ge(nbc_ready, 1)
            pe.matmul(bank[5][0:N_EXP, 0:1], upper[0:N_EXP, 0:N_EXP], nbc[:, 0:1], start=True, stop=True).then_inc(ends_done, 1)
            pe.wait_ge(ended_ready, 1)
            pe.matmul(bank[4][0:1, 0:N_BLK], ones[0:N_EXP, 0:1], ended[:], start=True, stop=True).then_inc(owners_done, 1)

            pe.wait_ge(plan_ready, 2)
            n_valid = pe.value_load(n_blocks[0:1, 0:1], min_val=MIN_BLOCKS, max_val=MAX_BLOCKS)

            def turn_rows(b, s, first=False):
                pe.wait_ge(xg_loaded, 16 * b + 16)
                if not first:
                    pe.wait_ge(xgT_ready, b)
                pe.sem_inc(passed)
                for k in range(KD):
                    mm = pe.transpose(bank[0][:, BLK * k:BLK * k + BLK], xg[s][0:BLK, :].rearrange("p (q k) -> p k q", k=KD)[:, k, :],
                                      ident[0:BLK, 0:BLK])
                mm.then_inc(xg_turned, 1)

            def expert(b, s):
                pe.wait_ge(e_loaded[s], 8 * (b - s) + 32)
                pe.wait_ge(xgT_ready, b + 1)
                gu = bank[2 + s % 2]
                for m in range(4):
                    for k in range(KD):
                        mm = pe.matmul(gu[:, BLK * m:BLK * m + BLK], w_wide[s][:, k, P * m:P * m + P], xgT[s % 2][:, k, :],
                                       start=(k == 0), stop=(k == KD - 1))
                mm.then_inc(gu_done, 1)
                turn_rows(b + 1, 1 - s % 2)
                pe.wait_ge(down_loaded[s], 4 * (b - s) + 16)
                pe.wait_ge(hid_ready, b + 1)
                if not (isinstance(b, int) and b == 0):
                    pe.wait_ge(y_act, b)
                    pe.wait_ge(y_dve, b)
                for half in range(2):
                    for j in range(2):
                        mm = pe.matmul((bank[5], proj_ps[0])[half][0:BLK, :], e_hid[:, j, :],
                                       w_down[s][:, j, 512 * half:512 * half + 512], start=(j == 0), stop=(j == 1))
                mm.then_inc(down_done, 1)

            turn_rows(0, 0, True)
            for s in range(E_SLOTS):
                expert(s, s)
            with pe.Fori(1, N_BLK // E_SLOTS) as it:
                for s in range(E_SLOTS):
                    b = E_SLOTS * it + s
                    with pe.If(b < n_valid):
                        expert(b, s)

        @block.scalar
        def _(act):
            a_ = Order(act, act_order)
            act.wait_ge(vec_loaded, 16 * 17)
            act.activation(c_act[:], c_raw[:], ACT.Silu).then_inc(c_ready, 1)
            act.wait_ge(x_loaded, 16 * NT)
            for i in range(NT):
                a_(act.activation(junk, x_tok[:, i, :], ACT.Square, accum_out=x_sq[:, i:i + 1]))
            act.wait_ge(var_ready, 1)
            a_(act.activation(x_std, x_var, ACT.Sqrt), std_ready)

            def copy_out(name, dests):
                for i, dst in enumerate(dests):
                    act.wait_ge(proj_done, first_out[name] + i + 1)
                    src = proj_ps[(first_out[name] + i) % 2][:, 0:dst.shape[-1]]
                    act.activation(dst, src, ACT.Copy).then_inc(proj_out, 1)

            act.wait_ge(h_ready, KD)
            copy_out("z", [z_tok[:, i, :] for i in range(NT)])
            copy_out("xbc_a", [xbc_raw[:, i, 3:3 + T] for i in range(4)])
            copy_out("xbc_b", [xbc_raw[:, 4, 3:3 + T], xbc_raw[:, 5, 3:3 + T], dt_raw])
            for t in range(6):
                act.wait_ge(ssd_conv, t + 1)
                act.activation(xbcT[:, t, :], xbcT[:, t, :], ACT.Silu, bias=cols[:, R_CONVB + t:R_CONVB + t + 1])\
                   .then_inc(ssd_act, 1)
            act.activation(z_tok, z_tok, ACT.Silu).then_inc(z_act, 1)
            act.wait_ge(dt_abs, 1)
            act.activation(dt_e, dt_a, ACT.Exp).then_inc(dt_exp, 1)
            act.activation(a_neg, bc[:, B_ALOG:B_ALOG + 8], ACT.Exp).then_inc(dt_exp, 1)
            act.wait_ge(dt_arg, 1)
            act.activation(dt_e, dt_e, ACT.Ln).then_inc(dt_ln, 1)
            for i in range(NT + 1):
                act.wait_ge(ssd_turned, i + 1)
                dst = xs_tok[:, i, :] if i < NT else b_tok
                act.activation(dst, bank[i % 2 if i < NT else 2][:], ACT.Copy).then_inc(ssd_tok, 1)
            act.wait_ge(acs_ready, 1)
            act.activation(eacs, acs, ACT.Exp).then_inc(acs_exp, 1)
            act.wait_ge(acs_ready, 2)
            act.activation(dec, dec, ACT.Exp).then_inc(acs_exp, 1)
            for i in range(NT):
                act.wait_ge(ssd_diff, i + 1)
                act.activation(ssd_l, ssd_l, ACT.Exp).then_inc(ssd_decay, 1)
                act.wait_ge(ssd_gated, i + 1)
                act.activation(ssd_tmp, ssd_yt, ACT.Square, accum_out=y_sq[:, i:i + 1]).then_inc(squared, 1)
                act.wait_ge(var_ready, i + 2)
                act.activation(y_std[:, i:i + 1], y_var[:, i:i + 1], ACT.Sqrt).then_inc(std_ready, 1)
            act.wait_ge(lb_arg, 1)
            act.activation(lb_e, lb_e, ACT.Exp).then_inc(lb_exp, 1)
            act.wait_ge(ssd_out, NT)
            copy_out("q_d", [hg_q[:, n, :] for n in range(NT)])
            copy_out("f_d", [hg_k[:, n, :] for n in range(NT)])
            copy_out("i_d", [hg_v[:, n, :] for n in range(NT)])
            copy_out("g_d", [hg_g[:, n, :] for n in range(NT)])
            act.wait_ge(proj_out, out_ready("g_d"))
            act.activation(hg_k, hg_k, ACT.Sigmoid).then_inc(hg_sig, 1)
            act.activation(hg_q, hg_q, ACT.Silu).then_inc(hg_silu, 1)
            act.activation(hg_g, hg_g, ACT.Silu).then_inc(hg_silu, 1)
            act.wait_ge(hg_f, NT)
            act.activation(hg_log, hg_k, ACT.Ln).then_inc(hg_ln, 1)
            act.wait_ge(hg_scan, 16)
            act.activation(hg_last, hg_cum.rearrange("p n (i t) -> p (n i) t", t=P)[:, :, P - 1], ACT.Exp).then_inc(hg_expl, 1)
            act.wait_ge(hg_kgarg, 1)
            act.activation(hg_qk[0], hg_qk[0], ACT.Exp).then_inc(hg_expk, 1)
            act.activation(hg_qg, hg_cum, ACT.Exp).then_inc(hg_expq, 1)
            for i in range(NT):
                act.wait_ge(hg_kturned, i + 1)
                act.activation(hg_ktok[:, i, :], bank[i % 2][:], ACT.Copy).then_inc(hg_kcopied, 1)
            for lv in range(1, len(LEVELS) + 1):
                act.wait_ge(hg_dist, lv)
                act.activation(hg_qk[(lv - 1) % 2], hg_qk[(lv - 1) % 2], ACT.Exp).then_inc(hg_decay, 1)
            for i in range(NT):
                act.wait_ge(hg_y, i + 1)
                act.activation(hg_tmp, bank[0][:], ACT.Square).then_inc(squared, 1)
                act.wait_ge(var_ready, 1 + NT + i + 1)
                act.activation(hg_std, hg_var, ACT.Sqrt).then_inc(std_ready, 1)
            act.wait_ge(lam_arg, 1)
            act.activation(lam_e, lam_s, ACT.Exp).then_inc(lam_exp, 1)
            act.wait_ge(hg_out, NT)
            copy_out("q_c", [df_q[:, n, :] for n in range(NT)])
            copy_out("k_c", [df_k[:, n, :] for n in range(NT)])
            copy_out("v_c", [df_v[:, n, :] for n in range(NT)])

            def df_exp(n):
                i = n // DIFF_H
                act.wait_ge(df_masked, 2 * n + 2)
                if n >= 2:
                    act.wait_ge(df_mixed, n - 1)
                for m in range(2):
                    v = 2 * (n % 2) + m
                    act.activation(df_s[:, n % 2, m, 0:P * (i + 1)], df_s[:, n % 2, m, 0:P * (i + 1)], ACT.Exp,
                                   bias=df_nmax[:, v:v + 1], accum_out=df_den[:, v:v + 1]).then_inc(df_prob, 1)

            df_exp(0)
            for n in range(NT * DIFF_H):
                if n + 1 < NT * DIFF_H:
                    df_exp(n + 1)
                act.wait_ge(df_turned, n + 1)
                if n >= 2:
                    act.wait_ge(df_y, n - 1)
                w = P * (n // DIFF_H + 1)
                act.activation(df_attnT[:, n % 2, 0:w], bank[4][:, 0:w], ACT.Copy).then_inc(df_copied, 1)
                if n % DIFF_H == DIFF_H - 1:
                    act.wait_ge(df_y, n + 1)
                    act.activation(df_tmp, bank[5][:], ACT.Square).then_inc(squared, 1)
                    act.wait_ge(var_ready, 1 + 2 * NT + n // DIFF_H + 1)
                    act.activation(df_std, df_var, ACT.Sqrt).then_inc(std_ready, 1)

            act.wait_ge(df_out, NT)
            for g in range(3):
                if g == 2:
                    act.wait_ge(dl_score, 8)
                copy_out(f"q_b{g}", [dl_q[g % 2][:, n, :] for n in range(NT)])
                copy_out(f"k_b{g}", [dl_k[g % 2][:, n, :] for n in range(NT)])
                copy_out(f"v_b{g}", [dl_v[g][:, n, :] for n in range(NT)])
                for n, (gg, j, b0, tiles, prev) in enumerate(DIL_SCORES):
                    if gg == g and (g or prev):
                        act.wait_ge(dl_masked, n + 1)
                        for part, (first, who) in enumerate(((0, range(NT)), (4, range(1, NT))) if g == 0 else ((b0, tiles),)):
                            stat = dl_prev if part else dl_stat[g]
                            for c_, a in enumerate(who):
                                e = act.activation(dl_p[:, j, first + c_, :], dl_p[:, j, first + c_, :], ACT.Exp,
                                                   bias=dl_stat[g][:, a, j:j + 1], accum_out=stat[:, a, 4 + j:5 + j])
                            e.then_inc(dl_prob, 1)
            act.wait_ge(dl_warg, 3)
            for g in range(3):
                act.activation(dl_w[g], dl_w[g], ACT.Exp).then_inc(dl_wexp, 1)
            for j in range(DIL_H):
                if j:
                    act.wait_ge(dl_y, j)
                for q in range(4):
                    n = min(4, DIL_BLOCKS - 4 * q)
                    act.wait_ge(dl_turned, 4 * j + q + 1)
                    act.activation(dl_pT[:, 4 * q:4 * q + n, :], bank[q][:, 0:P * n].rearrange("p (b k) -> p b k", k=P), ACT.Copy)\
                       .then_inc(dl_copied, 1)
            def gate(b, half, first):
                for m in range(4):
                    t = 8 * b + 4 * half + m
                    act.wait_ge(gate_done, t + 1)
                    if not first or 4 * half + m >= 2:
                        act.wait_ge(merge_out, t - 1)
                    act.activation(gate_sb[:, m % 2, :], proj_ps[m % 2][:], ACT.Sigmoid).then_inc(gate_out, 1)

            act.wait_ge(dl_out, NT)
            for half in range(2):
                gate(0, half, True)
            with act.Fori(1, 4) as b:
                for half in range(2):
                    gate(b, half, False)
            for v, dst in enumerate((bc_gate1, bc_scale2, bc_shift2, bc_gate2, bc_final)):
                for half in range(2):
                    q = 2 * v + half
                    act.wait_ge(row_spread, q + 1)
                    act.activation(dst[:, 512 * half:512 * half + 512], bank[2 + q % 2][:], ACT.Copy).then_inc(row_ready, 1)
            for i in range(NT):
                act.wait_ge(o_out, NT + i + 1)
                act.wait_ge(squared, 3 * NT + i)
                act.activation(xg[0], x2[:, i, :], ACT.Square, accum_out=f_sq[:, i:i + 1]).then_inc(squared, 1)
            act.wait_ge(var_ready, 1 + 3 * NT + 1)
            act.activation(f_std[:, 0:NT], f_var[:, 0:NT], ACT.Sqrt).then_inc(std_ready, 1)
            act.wait_ge(routed, 1)
            act.activation(scores, bank[2][:, 0:NT * N_EXP].rearrange("p (i e) -> p i e", i=NT), ACT.Sigmoid).then_inc(scored, 1)

            act.wait_ge(plan_ready, 2)
            n_valid = act.value_load(n_blocks[0:1, 0:1], min_val=MIN_BLOCKS, max_val=MAX_BLOCKS)

            def rows_out(b, s):
                act.wait_ge(xg_turned, b + 1)
                act.activation(xgT[s], bank[0][:].rearrange("p (k t) -> p k t", k=KD), ACT.Copy).then_inc(xgT_ready, 1)

            def expert_act(b, s, first):
                act.wait_ge(gu_done, b + 1)
                act.activation(e_act, bank[2 + s % 2][:, 0:2 * BLK].rearrange("p (j t) -> p j t", j=2), ACT.Silu).then_inc(gu_act, 1)
                rows_out(b + 1, 1 - s)
                act.wait_ge(down_done, b + 1)
                if not first:
                    act.wait_ge(y_stored[s], 8 * (b - s))
                act.activation(yb[s][0:BLK, 0:512], bank[5][0:BLK, :], ACT.Copy).then_inc(y_act, 1)

            rows_out(0, 0)
            for s in range(2):
                expert_act(s, s, True)
            with act.Fori(1, N_BLK // 2) as it:
                for s in range(2):
                    b = 2 * it + s
                    with act.If(b < n_valid):
                        expert_act(b, s, False)
            for i in range(NT):
                act.wait_ge(x3_ready, i + 1)
                act.activation(out_ring[i], x2[:, i, :], ACT.Square, accum_out=f_sq[:, NT + i:NT + i + 1]).then_inc(squared, 1)
                act.wait_ge(var_ready, 1 + 3 * NT + i + 2)
                act.activation(f_std[:, NT + i:NT + i + 1], f_var[:, NT + i:NT + i + 1], ACT.Sqrt).then_inc(std_ready, 1)
                act.wait_ge(out_ready_, i + 1)
                act.dma_start(out_dram[:, i, :], out_ring[i]).then_inc(out_stored, 16)
            act.wait_ge(out_stored, 16 * NT)

        @block.vector
        def _(dve):
            d = Order(dve, dve_order)
            dve.wait_ge(apart_ready, 1)
            d(dve.tensor_scalar(apart[:], apart[:], 3, None, ALU.bitwise_and))
            d(dve.tensor_scalar(causal_4th[:], apart[:], 0.0, NEG, ALU.is_gt, ALU.mult))
            dve.wait_ge(cols_turned, 1)
            d(dve.tensor_copy(cols[:], bank[2][:, 0:N_ROWS]))
            dve.wait_ge(bc_spread, 1)
            d(dve.tensor_copy(bc[:], bank[3][:, 0:N_BC]))
            dve.wait_ge(act_order, NT)
            d(dve.tensor_scalar(x_var, x_sq, 1.0 / D, EPS, ALU.mult, ALU.add), var_ready)
            dve.wait_ge(std_ready, 1)
            d(dve.reciprocal(x_rstd, x_std))
            for i in range(NT):
                d(dve.tensor_scalar(x_nrm[:, i, :], x_tok[:, i, :], x_rstd[:, i:i + 1], None, ALU.mult), xn_ready)
            dve.wait_ge(w_used, ADA_FIRST)
            d(dve.tensor_tensor(mod[:, 0:16], bank[4][:, 0:16], cols[:, 0:16], ALU.add), mod_copied)
            d(dve.scalar_tensor_tensor(scale_mix[:], mod[:, 8:16], 1.0, cols[:, R_NMIX:R_NMIX + KD], ALU.add, ALU.mult))
            for k in range(KD):
                dve.wait_ge(x_turned, k + 1)
                d(dve.tensor_scalar(hT[:, k, :], bank[k % 2][:], scale_mix[:, k:k + 1], mod[:, k:k + 1],
                                    ALU.mult, ALU.add), h_ready)
            dve.wait_ge(proj_out, out_ready("xbc_b"))
            d(dve.memset(xbc_raw[:, :, 0:3], 0.0))
            for t in range(6):
                for k in range(CONV_K):
                    w = cols[:, R_CONVW + 6 * k + t:R_CONVW + 6 * k + t + 1]
                    if k == 0:
                        d(dve.tensor_scalar(xbcT[:, t, :], xbc_raw[:, t, 0:T], w, None, ALU.mult))
                    else:
                        d(dve.scalar_tensor_tensor(xbcT[:, t, :], xbc_raw[:, t, k:k + T], w, xbcT[:, t, :], ALU.mult, ALU.add),
                          ssd_conv if k == CONV_K - 1 else None)
            d(dve.tensor_tensor(dt_raw.rearrange("p (i h) -> p i h", h=8), dt_raw.rearrange("p (i h) -> p i h", h=8),
                                over(bc[:, B_DTB:B_DTB + 8], NT), ALU.add))
            d(dve.scalar_tensor_tensor(dt_a, dt_raw, -1.0, dt_raw, ALU.mult, ALU.min), dt_abs)
            dve.wait_ge(dt_exp, 2)
            d(dve.tensor_scalar(dt_e, dt_e, 1.0, None, ALU.add), dt_arg)
            dve.wait_ge(dt_ln, 1)
            d(dve.scalar_tensor_tensor(dt, dt_raw, 0.0, dt_e, ALU.max, ALU.add))
            d(dve.scalar_tensor_tensor(adt.rearrange("p (i h) -> p i h", h=8), dt.rearrange("p (i h) -> p i h", h=8), -1.0,
                                       over(a_neg, NT), ALU.mult, ALU.mult), adt_ready)
            dve.wait_ge(acs_done, 1)
            d(dve.tensor_copy(acs, bank[3][:, 0:64]), acs_ready)
            d(dve.tensor_tensor(dec, acs[:, 32:64], acs[:, 0:32], ALU.subtract), acs_ready)
            dve.wait_ge(acs_exp, 2)
            d(dve.tensor_tensor(dec, dec, dt, ALU.mult))
            heads = lambda ap: ap.rearrange("p (h n) -> p h n", n=64)
            for i in range(NT):
                e = slice(8 * i, 8 * i + 8)
                dve.wait_ge(ssd_score, i + 1)
                if i:
                    dve.wait_ge(ssd_y, i)
                for h in range(SSD_H):
                    d(dve.tensor_scalar(ssd_l[:, h, :], bank[1 + h // 4][:, P * (h % 4):P * (h % 4) + P],
                                        acs[:, 8 * i + h:8 * i + h + 1], 0.0, ALU.subtract, ALU.min),
                      ssd_diff if h == SSD_H - 1 else None)
                for g in range(2):
                    d(dve.tensor_tensor(ssd_cb[:, g, :], bank[5 * g][:, 0:P], upper[:], ALU.mult))
                dve.wait_ge(ssd_tok, i + 1)
                d(dve.tensor_tensor(heads(xs_dt[:, i % 2, :]), heads(xs_tok[:, i, :]), along(dt[:, e], 64), ALU.mult))
                d(dve.tensor_tensor(heads(xs_dec[:, i % 2, :]), heads(xs_tok[:, i, :]), along(dec[:, e], 64), ALU.mult))
                dve.wait_ge(ssd_decay, i + 1)
                for g in range(2):
                    d(dve.tensor_tensor(ssd_l[:, 4 * g:4 * g + 4, :], ssd_l[:, 4 * g:4 * g + 4, :], over(ssd_cb[:, g, :], 4), ALU.mult),
                      ssd_m if g else None)
                dve.wait_ge(ssd_y, i + 1)
                d(dve.tensor_tensor(heads(ssd_yt), heads(xs_tok[:, i, :]), along(bc[:, B_DSK:B_DSK + 8], 64), ALU.mult))
                d(dve.tensor_tensor(ssd_yt, ssd_yt, bank[3][:], ALU.add))
                if i:
                    d(dve.tensor_tensor(heads(ssd_tmp), heads(bank[4][:]), along(eacs[:, e], 64), ALU.mult))
                    d(dve.tensor_tensor(ssd_yt, ssd_yt, ssd_tmp, ALU.add))
                if i < NT - 1:
                    mask = along(two_heads[:, 0:P:64], 256)
                    grp = lambda ap: ap.rearrange("p (g n) -> p g n", g=2)
                    if i == 0:
                        d(dve.tensor_tensor(grp(ssd_r), grp(bank[5][:]), mask, ALU.mult), ssd_state)
                    else:
                        d(dve.tensor_tensor(heads(ssd_r), heads(ssd_r), along(eacs[:, 32 + 8 * i:40 + 8 * i], 64), ALU.mult))
                        d(dve.tensor_tensor(grp(ssd_tmp), grp(bank[5][:]), mask, ALU.mult))
                        d(dve.tensor_tensor(ssd_r, ssd_r, ssd_tmp, ALU.add), ssd_state)
                dve.wait_ge(z_act, 1)
                d(dve.tensor_tensor(ssd_yt, ssd_yt, z_tok[:, i, :], ALU.mult), ssd_gated)
                dve.wait_ge(squared, i + 1)
                d(dve.tensor_scalar(y_var[:, i:i + 1], y_sq[:, i:i + 1], 1.0 / BW, EPS, ALU.mult, ALU.add), var_ready)
                dve.wait_ge(std_ready, i + 2)
                d(dve.reciprocal(y_rstd[:, i:i + 1], y_std[:, i:i + 1]))
                d(dve.tensor_scalar(ssd_yt, ssd_yt, y_rstd[:, i:i + 1], None, ALU.mult), ssd_o)
                dve.wait_ge(ssd_oT, i + 1)
                d(dve.tensor_tensor(branchT[:, 0:KB, P * i:P * i + P], bank[4][:].rearrange("p (j t) -> p j t", j=KB),
                                    along(cols[:, R_SSDN:R_SSDN + KB], P), ALU.mult), ssd_out)
            lbl = cols[:, R_LB:R_LB + KB]
            d(dve.tensor_tensor(lb_e, lbl, lbl, ALU.subtract), lb_arg)
            dve.wait_ge(lb_exp, 1)
            d(dve.reciprocal(lb_r, lb_e))
            d(dve.tensor_tensor(lb_r, lb_r, lb_e, ALU.mult))
            d(dve.tensor_tensor(lb, lb_r, lb_r, ALU.subtract))
            d(dve.tensor_scalar(lb_rest, lb, -1.0, 1.0, ALU.mult, ALU.add))
            dve.wait_ge(hg_sig, 1)
            for n in range(NT):
                d(dve.tensor_scalar(hg_k[:, n, :], hg_k[:, n, :], lb_rest[:, n:n + 1], lb[:, n:n + 1], ALU.mult, ALU.add), hg_f)
            dve.wait_ge(hg_ln, 1)
            d(dve.tensor_scalar(hg_k, hg_k, -1.0, 1.0, ALU.mult, ALU.add))
            for n in range(NT):
                for i in range(NT):
                    s = slice(P * i, P * i + P)
                    d(dve.tensor_tensor_scan(hg_cum[:, n, s], ones[:], hg_log[:, n, s], 0.0, ALU.mult, ALU.add), hg_scan)
            cum16 = hg_cum.rearrange("p n (i t) -> p (n i) t", t=P)
            as16 = lambda ap: ap.rearrange("p n (i t) -> p (n i) t", t=P)
            d(dve.tensor_tensor(as16(hg_qk[0]), along(cum16[:, :, P - 1], P), cum16, ALU.subtract), hg_kgarg)
            dve.wait_ge(hg_expk, 1)
            d(dve.tensor_tensor(hg_qk[0], hg_qk[0], hg_k, ALU.mult), hg_kg)
            dve.wait_ge(hg_expq, 1)
            dve.wait_ge(hg_silu, 2)
            d(dve.tensor_tensor(hg_qg, hg_qg, hg_q, ALU.mult), hg_qgr)
            dve.wait_ge(hg_zeroed, 1)

            def pick(lv):
                mask = ident[:] if lv == 0 else level_mask[:, lv - 1, :]
                for i in range(NT):
                    for s in range(2):
                        q = 8 * lv + 2 * i + s
                        dve.wait_ge(hg_score, q + 1)
                        d(dve.copy_predicated(hg_attn[:, i, s], over(mask.bitcast(U32), NT),
                                              bank[q % 6][:].rearrange("p (n q) -> p n q", n=NT)), hg_pick)

            for lv in range(1, len(LEVELS) + 1):
                b, buf = LEVELS[lv - 1], hg_qk[(lv - 1) % 2]
                if lv == 1:
                    dve.wait_ge(hg_kturned, NT)
                if lv > 2:
                    dve.wait_ge(hg_score, 8 * (lv - 1))
                halves = lambda ap: ap.rearrange("p n (k s j) -> p (n k) s j", s=2, j=b)
                cum, dst = halves(hg_cum), halves(buf)
                edge = along(cum[:, :, 0, b - 1], b)
                d(dve.tensor_tensor(dst[:, :, 0, :], edge, cum[:, :, 0, :], ALU.subtract))
                d(dve.tensor_tensor(dst[:, :, 1, :], cum[:, :, 1, :], edge, ALU.subtract), hg_dist)
                pick(lv - 1)
                dve.wait_ge(hg_decay, lv)
                d(dve.tensor_tensor(dst[:, :, 0, :], dst[:, :, 0, :], halves(hg_k)[:, :, 0, :], ALU.mult))
                d(dve.tensor_tensor(dst[:, :, 1, :], dst[:, :, 1, :], halves(hg_q)[:, :, 1, :], ALU.mult), hg_scaled)
            pick(len(LEVELS))
            for i in range(NT):
                dve.wait_ge(hg_y, i + 1)
                if i < NT - 1:
                    grp = bank[1][:].rearrange("p (n v) -> p n v", n=NT)
                    if i == 0:
                        d(dve.tensor_tensor(hg_r, grp, over(two_heads[:], NT), ALU.mult), hg_state)
                    else:
                        dve.wait_ge(hg_expl, 1)
                        d(dve.tensor_tensor(hg_r, hg_r, along(hg_last[:, i:16:4], P), ALU.mult))
                        d(dve.tensor_tensor(hg_o.rearrange("p (n v) -> p n v", n=NT), grp, over(two_heads[:], NT), ALU.mult))
                        d(dve.tensor_tensor(hg_r, hg_r, hg_o.rearrange("p (n v) -> p n v", n=NT), ALU.add), hg_state)
                dve.wait_ge(squared, NT + i + 1)
                d(dve.tensor_reduce(hg_sq, hg_tmp.rearrange("p (h v) -> p h v", v=64), AX_X, ALU.add))
                d(dve.tensor_scalar(hg_var, hg_sq, 1.0 / 64, EPS, ALU.mult, ALU.add), var_ready)
                dve.wait_ge(std_ready, 1 + NT + i + 1)
                d(dve.reciprocal(hg_rstd, hg_std))
                d(dve.tensor_tensor(heads(hg_o), heads(bank[0][:]), along(hg_rstd, 64), ALU.mult))
                d(dve.tensor_tensor(hg_o, hg_o, hg_g[:, i, :], ALU.mult), hg_ready)
                dve.wait_ge(hg_oT, i + 1)
                d(dve.tensor_scalar(branchT[:, 3 * KB:4 * KB, P * i:P * i + P], bank[2][:].rearrange("p (j t) -> p j t", j=KB),
                                    cols[:, R_HGN:R_HGN + 1], None, ALU.mult), hg_out)
            lam4 = bc[:, B_LAM:B_LAM + 256].rearrange("p (m s n) -> p m s n", m=2, s=2)
            prod = lam_p.rearrange("p (m n) -> p m n", m=2)
            d(dve.tensor_tensor(prod, lam4[:, :, 0, :], lam4[:, :, 1, :], ALU.mult))
            d(dve.tensor_reduce(lam_s, prod, AX_X, ALU.add), lam_arg)
            d(dve.tensor_scalar(sub_w, cols[:, R_SUBLN:R_SUBLN + 1], 1.0 - LAM_INIT, None, ALU.mult))
            dve.wait_ge(lam_exp, 1)
            d(dve.tensor_tensor(lam_neg, lam_e[:, 1:2], lam_e[:, 0:1], ALU.subtract))
            d(dve.tensor_scalar(lam_neg, lam_neg, -LAM_INIT, None, ALU.add))

            def df_mask(n):
                i = n // DIFF_H
                dve.wait_ge(df_score, n + 1)
                own = slice(P * i, P * i + P)
                for m in range(2):
                    s, ps, v = df_s[:, n % 2, m, :], bank[2 * (n % 2) + m], 2 * (n % 2) + m
                    d(dve.scalar_tensor_tensor(s[:, own], ps[:, own], 0.125, causal[:], ALU.mult, ALU.add))
                    if i:
                        d(dve.tensor_scalar(s[:, 0:P * i], ps[:, 0:P * i], 0.125, None, ALU.mult))
                    d(dve.tensor_reduce(df_nmax[:, v:v + 1], s[:, 0:P * (i + 1)], AX_X, ALU.max, negate=True), df_masked)

            df_mask(0)
            for n in range(NT * DIFF_H):
                i, h = n // DIFF_H, n % DIFF_H
                if n + 1 < NT * DIFF_H:
                    df_mask(n + 1)
                w, v = P * (i + 1), 2 * (n % 2)
                dve.wait_ge(df_prob, 2 * n + 2)
                if n >= 2:
                    dve.wait_ge(df_turned, n - 1)
                d(dve.reciprocal(df_r[:, v:v + 2], df_den[:, v:v + 2]))
                d(dve.tensor_tensor(df_r[:, v + 1:v + 2], df_r[:, v + 1:v + 2], lam_neg, ALU.mult))
                d(dve.tensor_scalar(df_attn[:, n % 2, 0:w], df_s[:, n % 2, 1, 0:w], df_r[:, v + 1:v + 2], None, ALU.mult))
                d(dve.scalar_tensor_tensor(df_attn[:, n % 2, 0:w], df_s[:, n % 2, 0, 0:w], df_r[:, v:v + 1],
                                           df_attn[:, n % 2, 0:w], ALU.mult, ALU.add), df_mixed)
                if h == DIFF_H - 1:
                    hd = lambda ap: ap.rearrange("p (h n) -> p h n", h=DIFF_H)
                    dve.wait_ge(squared, 2 * NT + i + 1)
                    d(dve.tensor_reduce(df_sq, hd(df_tmp), AX_X, ALU.add))
                    d(dve.tensor_scalar(df_var, df_sq, 1.0 / P, EPS, ALU.mult, ALU.add), var_ready)
                    dve.wait_ge(std_ready, 1 + 2 * NT + i + 1)
                    d(dve.reciprocal(df_rstd, df_std))
                    d(dve.tensor_tensor(hd(df_o), hd(bank[5][:]), along(df_rstd, P), ALU.mult), df_ready)
                    dve.wait_ge(df_oT, i + 1)
                    d(dve.tensor_scalar(branchT[:, 2 * KB:3 * KB, P * i:P * i + P],
                                        bank[4][:].rearrange("p (j t) -> p j t", j=KB), sub_w, None, ALU.mult), df_out)

            d(dve.tensor_tensor(causal_4th[:], causal_4th[:], causal[:], ALU.min))

            scale = DIL_D ** -0.5
            for n, (g, j, b0, tiles, prev) in enumerate(DIL_SCORES):
                dve.wait_ge(dl_score, n + 1)
                c_ = len(tiles)
                mask = (band_prev if prev else (causal, causal, causal_4th)[g])[:]
                dst = dl_p[:, j, b0:b0 + c_, :]
                own, before = dl_stat[g][:, :, j], dl_prev[:, 1:NT, j]
                d(dve.scalar_tensor_tensor(dst, bank[n % 4][:, 0:P * c_].rearrange("p (a k) -> p a k", k=P), scale,
                                           over(mask, c_), ALU.mult, ALU.add))
                d(dve.tensor_reduce(before if prev else own, dst, AX_X, ALU.max, negate=True),
                  None if prev else dl_masked)
                if prev:
                    d(dve.tensor_tensor(own[:, 1:NT], own[:, 1:NT], before, ALU.min), dl_masked)
            dve.wait_ge(dl_prob, len(DIL_SCORES))
            d(dve.tensor_tensor(dl_stat[0][:, 1:NT, 4:8], dl_stat[0][:, 1:NT, 4:8], dl_prev[:, 1:NT, 4:8], ALU.add))
            dve.wait_ge(dl_back, 32)
            nat = [dl_stat[0], dl_nat[0], dl_nat[1]]
            d(dve.tensor_tensor(dl_low, nat[0][:, :, 0:4], nat[1][:, :, 0:4], ALU.min))
            d(dve.tensor_tensor(dl_low, dl_low, nat[2][:, :, 0:4], ALU.min))
            for g in range(3):
                d(dve.tensor_tensor(dl_w[g], dl_low, nat[g][:, :, 0:4], ALU.subtract), dl_warg)
            dve.wait_ge(dl_wexp, 3)
            d(dve.tensor_tensor(dl_z, dl_w[0], nat[0][:, :, 4:8], ALU.mult))
            for g in (1, 2):
                d(dve.tensor_tensor(dl_t, dl_w[g], nat[g][:, :, 4:8], ALU.mult))
                d(dve.tensor_tensor(dl_z, dl_z, dl_t, ALU.add))
            d(dve.reciprocal(dl_z, dl_z))
            for g in range(3):
                d(dve.tensor_tensor(dl_w[g], dl_w[g], dl_z, ALU.mult), dl_weighed)
            dve.wait_ge(dl_wback, 32)
            for j in range(DIL_H):
                for b0, n, w in ((0, 4, dl_w[0][:, :, j]), (4, 3, dl_w[0][:, 1:NT, j]), (7, 4, dl_wg[0][:, :, j]),
                                 (11, 4, dl_wg[1][:, :, j])):
                    d(dve.tensor_tensor(dl_p[:, j, b0:b0 + n, :], dl_p[:, j, b0:b0 + n, :], along(w, P), ALU.mult), dl_scaled)
            for j in range(DIL_H):
                dve.wait_ge(dl_y, j + 1)
                d(dve.tensor_copy(branchT[:, KB + j, :], bank[4 + j % 2][:]), dl_out)
            dve.wait_ge(w_used, ADA)
            d(dve.tensor_tensor(mod[:, 16:48], proj_ps[0][:, 0:32], cols[:, 16:48], ALU.add), mod_copied)
            d(dve.scalar_tensor_tensor(scale_ffn[:], mod[:, 32:40], 1.0, cols[:, R_NFFN:R_NFFN + KD], ALU.add, ALU.mult), scale2_ready)
            d(dve.memset(merged, 0.0))

            def merge(b, half):
                for m in range(4):
                    t = 8 * b + 4 * half + m
                    dve.wait_ge(gate_out, t + 1)
                    dve.wait_ge(merge_done, t + 1)
                    dve.tensor_tensor(gate_sb[:, m % 2, :], gate_sb[:, m % 2, :], bank[m % 2][:], ALU.mult).then_inc(merge_mul, 1)
                    dve.wait_ge(merge_mul, t + 1)
                    dve.tensor_tensor(merged[:, 4 * half + m, :], merged[:, 4 * half + m, :], gate_sb[:, m % 2, :], ALU.add)\
                       .then_inc(merge_out, 1)

            for half in range(2):
                merge(0, half)
            with dve.Fori(1, 4) as b:
                for half in range(2):
                    merge(b, half)
            dve.wait_ge(x2_loaded, 16)
            dve.wait_ge(row_ready, 10)
            for o in range(2 * NT):
                s = slice(512 * (o // NT), 512 * (o // NT) + 512)
                dve.wait_ge(o_done, o + 1)
                tmp = gate_sb[:, o % 2, :]
                d(dve.tensor_tensor(tmp, bank[4 + o % 2][:], bc_gate1[:, s], ALU.mult))
                d(dve.tensor_tensor(x2[:, o % NT, s], x2[:, o % NT, s], tmp, ALU.add), o_out)
            dve.wait_ge(squared, 3 * NT + NT)
            d(dve.tensor_scalar(f_var[:, 0:NT], f_sq[:, 0:NT], 1.0 / D, EPS, ALU.mult, ALU.add), var_ready)
            dve.wait_ge(std_ready, 1 + 3 * NT + 1)
            d(dve.reciprocal(f_rstd[:, 0:NT], f_std[:, 0:NT]))
            for i in range(NT):
                d(dve.scalar_tensor_tensor(h2[:, i, :], x2[:, i, :], f_rstd[:, i:i + 1], bc_scale2, ALU.mult, ALU.mult))
                d(dve.tensor_tensor(h2[:, i, :], h2[:, i, :], bc_shift2, ALU.add), h2_ready)
            for k in range(KD):
                dve.wait_ge(h2_turned, k + 1)
                d(dve.tensor_copy(h2T[:, k, :], bank[k % 2][:]), h2T_ready)

            dve.wait_ge(scored, 1)
            d(dve.tensor_tensor(sel, scores, over(bc[:, B_RB:B_RB + N_EXP], NT), ALU.add))
            for i in range(NT):
                for g in range(GROUPS):
                    d(dve.max(best8[:, GROUPS * i + g, :], sel[:, i, 8 * g:8 * g + 8]))
            best = best8[:].rearrange("p (i g) m -> p i g m", i=NT)
            d(dve.tensor_tensor(grp_score, best[:, :, :, 0], best[:, :, :, 1], ALU.add))
            for i in range(NT):
                d(dve.max(top8[:, i, :], grp_score[:, i, :]))
                d(dve.max_index(top_i[:, i, :], top8[:, i, :], grp_score[:, i, :]))
            d(dve.tensor_copy(top_f[:], top_i[:]))
            d(dve.tensor_tensor(grp_pen, over(iota_grp[:], NT), along(top_f[:, :, 0], GROUPS), ALU.not_equal))
            d(dve.tensor_scalar(grp_pen, grp_pen, NEG, None, ALU.mult))
            for i in range(NT):
                d(dve.tensor_tensor(sel[:, i, :].rearrange("p (g e) -> p g e", g=GROUPS), sel[:, i, :].rearrange("p (g e) -> p g e", g=GROUPS),
                                    along(grp_pen[:, i, :], 8), ALU.add))
                d(dve.max(top8[:, i, :], sel[:, i, :]))
                d(dve.max_index(top_i[:, i, :], top8[:, i, :], sel[:, i, :]))
            d(dve.tensor_copy(top_f[:], top_i[:]))
            for s in range(2):
                d(dve.tensor_tensor(hot[s], over(iota_exp[:], NT), along(top_f[:, :, s], N_EXP), ALU.is_equal))
                d(dve.tensor_tensor(picked[:], hot[s], scores, ALU.mult))
                d(dve.tensor_reduce(pair_s[:, :, s], picked[:], AX_X, ALU.add))
            d(dve.tensor_tensor(both_hot[:], hot[0], hot[1], ALU.add))
            d(dve.tensor_reduce(pair_z, pair_s, AX_X, ALU.add), hot_ready)
            d(dve.reciprocal(pair_z, pair_z), hot_ready)
            d(dve.tensor_tensor(pair_s, pair_s, along(pair_z, 2), ALU.mult), hot_ready)
            d(dve.memset(endc[:], 0.0), hot_ready)
            dve.wait_ge(ranked, 1)
            for dst, cnt in ((nbc[:, 0:1], bank[5][0:N_EXP, 0:1]), (n_blk_e[:], bank[4][:, 0:N_EXP])):
                d(dve.tensor_scalar(dst, cnt, 0.0, None, ALU.is_gt))
                for j in range(1, T // BLK):
                    d(dve.scalar_tensor_tensor(dst, cnt, float(BLK * j), dst, ALU.is_gt, ALU.add),
                      nbc_ready if j == T // BLK - 1 else None)
            d(dve.tensor_tensor_scan(blk_end[:], ones[:, 0:N_EXP], n_blk_e[:], 0.0, ALU.mult, ALU.add))
            d(dve.tensor_copy(n_blocks[:], blk_end[0:1, N_EXP - 1:N_EXP]), plan_ready)
            d(dve.tensor_tensor(n_blk_e[:], blk_end[:], n_blk_e[:], ALU.subtract))
            d(dve.scalar_tensor_tensor(rank[:], over(n_blk_e[:], NT), float(BLK), bank[3][:, 0:NT * N_EXP].rearrange("p (i e) -> p i e", i=NT),
                                       ALU.mult, ALU.add))
            for s in range(2):
                d(dve.tensor_tensor(picked[:], hot[s], rank[:], ALU.mult))
                d(dve.tensor_reduce(pair_row[:, :, s], picked[:], AX_X, ALU.add))
            d(dve.tensor_copy(row_id[:], pair_row), rows_ready)
            dve.wait_ge(ends_done, 1)
            d(dve.tensor_copy(endc[:], bank[5][0:N_EXP, 0:1]))
            d(dve.tensor_scalar(ended[:], iota_blk[:], endc[:, 0:1], None, ALU.is_ge), ended_ready)
            dve.wait_ge(owners_done, 1)
            d(dve.tensor_scalar(blk_exp[:], bank[4][0:1, 0:N_BLK], float(N_EXP - 1), None, ALU.min), plan_ready)

            n_valid = dve.value_load(n_blocks[0:1, 0:1], min_val=MIN_BLOCKS, max_val=MAX_BLOCKS)

            def expert_dve(b, s, first):
                dve.wait_ge(gu_act, b + 1)
                dve.tensor_tensor(e_hid, e_act, bank[2 + s % 2][:, 2 * BLK:4 * BLK].rearrange("p (j t) -> p j t", j=2), ALU.mult)\
                   .then_inc(hid_ready, 1)
                dve.wait_ge(down_done, b + 1)
                if not first:
                    dve.wait_ge(y_stored[s], 8 * (b - s))
                dve.tensor_copy(yb[s][0:BLK, 512:1024], proj_ps[0][0:BLK, :]).then_inc(y_dve, 1)

            for s in range(2):
                expert_dve(s, s, True)
            with dve.Fori(1, N_BLK // 2) as it:
                for s in range(2):
                    b = 2 * it + s
                    with dve.If(b < n_valid):
                        expert_dve(b, s, False)
            for i in range(NT):
                a, b = yg[2 * (i % 2)], yg[2 * (i % 2) + 1]
                dve.wait_ge(yg_loaded[i % 2], 32 * (i // 2 + 1))
                d(dve.tensor_scalar(a, a, pair_s[:, i, 0:1], None, ALU.mult))
                d(dve.scalar_tensor_tensor(a, b, pair_s[:, i, 1:2], a, ALU.mult, ALU.add))
                d(dve.tensor_tensor(a, a, bc_gate2, ALU.mult))
                d(dve.tensor_tensor(x2[:, i, :], x2[:, i, :], a, ALU.add), x3_ready)
                dve.wait_ge(squared, 3 * NT + NT + i + 1)
                d(dve.tensor_scalar(f_var[:, NT + i:NT + i + 1], f_sq[:, NT + i:NT + i + 1], 1.0 / D, EPS, ALU.mult, ALU.add), var_ready)
                dve.wait_ge(std_ready, 1 + 3 * NT + i + 2)
                d(dve.reciprocal(f_rstd[:, NT + i:NT + i + 1], f_std[:, NT + i:NT + i + 1]))
                d(dve.scalar_tensor_tensor(out_ring[i], x2[:, i, :], f_rstd[:, NT + i:NT + i + 1], bc_final, ALU.mult, ALU.mult),
                  out_ready_)


_INS = ["x", "c", "w_ada", "b_ada", "norm_mix_w", "norm_ffn_w", "w_in", "conv_w", "conv_b", "ssd_dt_bias",
        "ssd_a_log", "ssd_d", "ssd_norm_w", "diff_lambda", "diff_subln_w", "hgrn_lb_logits", "hgrn_norm_w",
        "w_merge", "w_out", "w_router", "router_bias", "w_expert_gate", "w_expert_up", "w_expert_down",
        "final_norm_w"]


def kernel(**inputs):
    import numpy as np
    import concourse.bacc as bacc
    from concourse.bass_utils import run_bass_kernel_spmd

    nc = bacc.Bacc("TRN2", target_bir_lowering=False, num_devices=1)
    arrays, args = {}, []
    for name in _INS:
        a = np.ascontiguousarray(inputs[name])
        arrays[f"in_{name}"] = a
        args.append(nc.dram_tensor(f"in_{name}", a.shape, mybir.dt.from_np(a.dtype), kind="ExternalInput").ap())
    for name, shape, dt in (("row_list", (LIST, 2), U32), ("h2_rows", (T, D), F32),
                            ("y_rows", (2 * T, D), F32), ("dil_stats", (2, T, 8), F32),
                            ("dil_weights", (2, T, 4), F32)):
        args.append(nc.dram_tensor(name, shape, dt, kind="Internal").ap())
    args.append(nc.dram_tensor("out", (1, T, D), F32, kind="ExternalOutput").ap())
    build(nc, *args)
    r = run_bass_kernel_spmd(nc, [arrays], core_ids=[0])
    return r.results[0]["out"]
```

```python
from contextlib import ExitStack

import concourse.bass as bass
from concourse import mybir

F32 = mybir.dt.float32
U32 = mybir.dt.uint32
ALU = mybir.AluOpType
ACT = mybir.ActivationFunctionType
AX_X = mybir.AxisListType.X

P = 128
T = 512
NT = T // P
D = 1024
KD = D // P
BW = 512
KB = BW // P
EPS = 1e-6
NEG = -1e30
SSD_H, SSD_P = 8, 64
CONV_CH, CONV_K = 768, 4
DIL_H, DIL_D = 4, 128
DIL_BLOCKS = 15
DIFF_H = 4
HG_H = 8
LEVELS = [1, 2, 4, 8, 16, 32, 64]
LAM_INIT = 0.8 - 0.6
N_EXP, GROUPS, F_EXP = 64, 8, 256
BLK = 64
MAX_BLOCKS = N_EXP + (2 * T - N_EXP) // BLK
E_SLOTS = 4
N_BLK = -(-MAX_BLOCKS // E_SLOTS) * E_SLOTS
MIN_BLOCKS = 2 * T // BLK
AHEAD = 4
LIST_BLK = N_BLK + AHEAD
LIST = LIST_BLK * BLK

C_Z, C_XBC, C_DT = 0, 512, 1280
C_QB, C_KB, C_VB = 1288, 2824, 4360
C_QC, C_KC, C_VC = 5896, 6408, 6920
C_QD, C_FD, C_ID, C_GD = 7432, 7944, 8456, 8968
C_GATE = 9480

R_BADA, R_NMIX, R_NFFN, R_FIN, R_CONVB, R_CONVW, R_SSDN, R_SUBLN, R_HGN, R_LB = 0, 48, 56, 64, 72, 78, 102, 106, 107, 108
N_ROWS = 112
B_DTB, B_ALOG, B_DSK, B_LAM, B_RB = 0, 8, 16, 24, 280
N_BC = 344

ARENA = 27136
PLACES = {"open": (0, 11264), "merge": (0, 5120), "ssd": (0, 11264), "ssd_more": (17408, ARENA), "diff": (11264, 22528),
          "hg_in": (5120, 11264), "hg": (11264, ARENA), "dil": (5120, ARENA), "late": (5120, ARENA)}


class Order:

    def __init__(self, eng, own):
        self.eng, self.own, self.count = eng, own, {}

    def __call__(self, ins, sem=None):
        sem = self.own if sem is None else sem
        ins.then_inc(sem, 1)
        self.count[sem.name] = self.count.get(sem.name, 0) + 1
        self.eng.wait_ge(sem, self.count[sem.name])


def tokens_of(view, g, a):
    return view[:, P * a:P * a + P] if g == 0 else view.rearrange("p (i r) -> p r i", r=4)[:, a, :]


def build(nc, x, c, w_ada, b_ada, norm_mix_w, norm_ffn_w, w_in, conv_w, conv_b, ssd_dt_bias, ssd_a_log,
          ssd_d, ssd_norm_w, diff_lambda, diff_subln_w, hgrn_lb_logits, hgrn_norm_w, w_merge, w_out,
          w_router, router_bias, w_expert_gate, w_expert_up, w_expert_down, final_norm_w,
          list_dram, h2_dram, y_dram, stat_dram, weight_dram, out):
    x_dram = x.rearrange("a (i p) d -> p (a i) d", p=P)
    out_dram = out.rearrange("a (i p) d -> p (a i) d", p=P)
    ada_dram = w_ada[0].rearrange("(p k) n -> p k n", p=P)
    in_dram = w_in[0].rearrange("(k p) n -> p k n", p=P)

    with ExitStack() as ctx:
        def sb(name, shape, dt=F32):
            return ctx.enter_context(nc.sbuf_tensor(name, shape, dt))

        def sem(name):
            return ctx.enter_context(nc.semaphore(name))

        proj_ps = [ctx.enter_context(nc.psum_tensor(f"proj_ps{i}", [P, 512], F32)) for i in range(2)]
        bank = [ctx.enter_context(nc.psum_tensor(f"bank{i}", [P, 512], F32)) for i in range(6)]

        ident = sb("ident", [P, P])
        ones = sb("ones", [P, P])
        upper = sb("upper", [P, P])
        upper_strict = sb("upper_strict", [P, P])
        causal = sb("causal", [P, P])
        band_prev = sb("band_prev", [P, P])
        apart = sb("apart", [P, P], U32)
        causal_4th = sb("causal_4th", [P, P])
        level_mask = sb("level_mask", [P, len(LEVELS), P])
        two_heads = sb("two_heads", [P, P])
        iota_exp = sb("iota_exp", [P, N_EXP])
        iota_grp = sb("iota_grp", [P, GROUPS])
        iota_blk = sb("iota_blk", [N_EXP, N_BLK])
        entry = sb("entry", [P, NT, 2, 2], U32)
        rows = sb("rows", [N_ROWS, P])
        cols = sb("cols", [P, N_ROWS])
        bc_row = sb("bc_row", [1, N_BC])
        bc = sb("bc", [P, N_BC])
        mod = sb("mod", [P, 48])
        c_raw = sb("c_raw", [P, KD])
        c_act = sb("c_act", [P, KD])
        scale_mix = sb("scale_mix", [P, KD])
        ada_acc = [sb(f"ada_acc{i}", [P, 512]) for i in range(2)]
        scale_ffn = sb("scale_ffn", [P, KD])
        hT = sb("hT", [P, KD, T])
        branchT = sb("branchT", [P, 4 * KB, T])
        w_ring = [sb(f"w_ring{i}", [P, KD * 512]) for i in range(2)]
        small = sb("small", [P, 1024])
        arena = sb("arena", [P, ARENA])
        taken = {who: at for who, (at, _) in PLACES.items()}

        def place(who, n):
            at = taken[who]
            taken[who] = at + n
            assert taken[who] <= PLACES[who][1], (who, taken[who])
            return arena[:, at:at + n]

        w_slot = [w[:].rearrange("p (k n) -> p k n", k=KD) for w in w_ring]

        dve_order, act_order, pool_order = sem("dve_order"), sem("act_order"), sem("pool_order")
        consts_ready, apart_ready = sem("consts_ready"), sem("apart_ready")
        x_loaded, vec_loaded = sem("x_loaded"), sem("vec_loaded")
        w_loaded = [sem(f"w_loaded{i}") for i in range(2)]
        w_used, ada_done, ada_summed = sem("w_used"), sem("ada_done"), sem("ada_summed")
        ada_loaded = [sem(f"ada_loaded{i}") for i in range(2)]
        cols_turned, bc_spread = sem("cols_turned"), sem("bc_spread")
        c_ready = sem("c_ready")
        mod_copied = sem("mod_copied")
        xn_ready = sem("xn_ready")
        x_turned, h_ready = sem("x_turned"), sem("h_ready")
        proj_done, proj_out = sem("proj_done"), sem("proj_out")
        ssd_conv, ssd_act = sem("ssd_conv"), sem("ssd_act")
        ssd_turned, ssd_tok = sem("ssd_turned"), sem("ssd_tok")
        dt_abs, dt_exp, dt_arg, dt_ln = sem("dt_abs"), sem("dt_exp"), sem("dt_arg"), sem("dt_ln")
        adt_ready, acs_done, acs_ready = sem("adt_ready"), sem("acs_done"), sem("acs_ready")
        acs_exp = sem("acs_exp")
        ssd_score, ssd_diff, ssd_decay, ssd_m = sem("ssd_score"), sem("ssd_diff"), sem("ssd_decay"), sem("ssd_m")
        ssd_y, ssd_state, ssd_gated, squared = sem("ssd_y"), sem("ssd_state"), sem("ssd_gated"), sem("squared")
        z_act, var_ready, std_ready = sem("z_act"), sem("var_ready"), sem("std_ready")
        ssd_o, ssd_oT, ssd_out = sem("ssd_o"), sem("ssd_oT"), sem("ssd_out")

        ADA_FIRST, ADA = 4, 12
        x_tok = place("open", NT * D).rearrange("p (i d) -> p i d", i=NT)
        x_nrm = place("open", NT * D).rearrange("p (i d) -> p i d", i=NT)
        junk = place("open", D)
        ada_slot = [w_slot[0], w_slot[1]] + [branchT[:].rearrange("p c t -> p (c t)")[:, KD * 512 * i:KD * 512 * (i + 1)]
                                             .rearrange("p (k n) -> p k n", k=KD) for i in range(2)]
        ada_first = [place("open", 512) for _ in range(ADA_FIRST)]
        at = [0]

        def sm(n):
            at[0] += n
            assert at[0] <= 1024
            return small[:, at[0] - n:at[0]]

        x_sq, x_var, x_std, x_rstd = sm(NT), sm(NT), sm(NT), sm(NT)

        def over(ap, n):
            return ap.unsqueeze(1).to_broadcast([ap.shape[0], n, ap.shape[1]])

        def along(ap, n):
            return ap.unsqueeze(2).to_broadcast([ap.shape[0], ap.shape[1], n])

        PROJ = [("z", C_Z, 512, 4), ("xbc_a", C_XBC, 512, 4), ("xbc_b", C_XBC + 512, 264, 3),
                ("q_c", C_QC, 512, 4), ("ada4", 512 * 4, 512, 1), ("k_c", C_KC, 512, 4), ("ada5", 512 * 5, 512, 1),
                ("v_c", C_VC, 512, 4), ("ada6", 512 * 6, 512, 1), ("g_d", C_GD, 512, 4), ("ada7", 512 * 7, 512, 1),
                ("q_d", C_QD, 512, 4), ("ada8", 512 * 8, 512, 1), ("f_d", C_FD, 512, 4), ("ada9", 512 * 9, 512, 1),
                ("i_d", C_ID, 512, 4), ("ada10", 512 * 10, 512, 1), ("ada11", 512 * 11, 512, 1)]
        N_BEFORE = len(PROJ)
        for g in range(3):
            PROJ += [(f"q_b{g}", C_QB + 512 * g, 512, 4), (f"k_b{g}", C_KB + 512 * g, 512, 4),
                     (f"v_b{g}", C_VB + 512 * g, 512, 4)]
        first_out = {name: sum(o for _, _, _, o in PROJ[:i]) for i, (name, _, _, _) in enumerate(PROJ)}
        outs_of = {name: o for name, _, _, o in PROJ}
        MERGE_ORDER = [0, 2, 3, 1]
        MERGE_UNITS = 4 * KD // 2
        UNITS = ["ada0", "ada1"] + [p[0] for p in PROJ[:N_BEFORE]]
        UNITS += [f"merge{u}" for u in range(MERGE_UNITS // 2)] + [p[0] for p in PROJ[N_BEFORE:]]
        UNITS += [f"merge{u}" for u in range(MERGE_UNITS // 2, MERGE_UNITS)] + ["out0", "out1"]
        unit_of = {name: n for n, name in enumerate(UNITS)}

        def in_slot(name):
            n = unit_of[name]
            return 16 * sum(2 if u.startswith("merge") else 1 for u in UNITS[n % 2:n + 1:2])

        def out_ready(name):
            return first_out[name] + outs_of[name]

        def outputs(*names):
            return [(name, m) for name in names for m in range(outs_of[name])]

        merges = [("merge", t) for t in range(4 * KD)]
        work = outputs(*(p[0] for p in PROJ[3:N_BEFORE]))
        FILL = {"ssd": [work[a:b] for a, b in ((0, 4), (4, 6), (6, 8), (8, 10), (10, 12), (12, 14), (14, 16), (16, 18), (18, 19), (19, 20))],
                "diff": [[w] for w in work[20:]],
                "hg": [merges[0:5]] + [merges[t:t + 1] for t in range(5, 16)],
                "dil": [merges[16:20]] + [merges[t:t + 1] for t in range(20, 24)]}

        def drained(points):
            taken_out, under_way = [], []
            for items in points:
                under_way = under_way + items
                taken_out.append(under_way[:-1])
                under_way = under_way[-1:]
            return taken_out + [under_way]

        DRAIN = {who: drained(points) for who, points in FILL.items()}

        xbc_raw = place("ssd", 6 * (T + 3)).rearrange("p (c t) -> p c t", c=6)
        xbcT = place("ssd", 6 * T).rearrange("p (c t) -> p c t", c=6)
        z_tok = place("ssd", NT * BW).rearrange("p (i n) -> p i n", i=NT)
        xs_tok = place("ssd", NT * BW).rearrange("p (i n) -> p i n", i=NT)
        xs_dt = place("ssd_more", 2 * BW).rearrange("p (i n) -> p i n", i=2)
        xs_dec = place("ssd_more", 2 * BW).rearrange("p (i n) -> p i n", i=2)
        b_tok = place("ssd_more", NT * P).rearrange("p (i n) -> p i n", i=NT)
        ssd_l = place("ssd_more", SSD_H * P).rearrange("p (h l) -> p h l", h=SSD_H)
        ssd_cb = place("ssd_more", 2 * P).rearrange("p (g l) -> p g l", g=2)
        ssd_r = place("ssd_more", BW)
        ssd_tmp = place("ssd_more", BW)
        ssd_yt = place("ssd_more", BW)
        dt_raw, dt_a, dt_e, dt, adt = sm(32), sm(32), sm(32), sm(32), sm(32)
        a_neg = sm(8)
        acs, eacs, dec = sm(64), sm(64), sm(32)
        y_sq, y_var, y_std, y_rstd = sm(NT), sm(NT), sm(NT), sm(NT)

        def hg_tiles(who="hg"):
            return place(who, NT * T).rearrange("p (n t) -> p n t", n=NT)

        hg_q, hg_k, hg_v = (hg_tiles("hg_in") for _ in range(3))
        hg_g = branchT[:, KB:2 * KB, :]
        hg_log, hg_cum = (hg_tiles() for _ in range(2))
        hg_qk = [hg_tiles() for _ in range(2)]
        hg_ktok = hg_tiles()
        hg_qg = hg_log
        hg_attn = place("hg", NT * 2 * NT * P).rearrange("p (i s n q) -> p i s n q", i=NT, s=2, n=NT)
        hg_r = place("hg", BW).rearrange("p (n v) -> p n v", n=NT)
        hg_tmp, hg_o = place("hg", BW), place("hg", BW)
        lb_e, lb_r, lb, lb_rest = sm(4), sm(4), sm(4), sm(4)
        hg_last = sm(16)
        hg_sq, hg_var, hg_std, hg_rstd = sm(8), sm(8), sm(8), sm(8)
        exp_arg, exp_out = sem("exp_arg"), sem("exp_out")
        hg_sig, hg_f, hg_ln, hg_scan = sem("hg_sig"), sem("hg_f"), sem("hg_ln"), sem("hg_scan")
        hg_silu, hg_expq, hg_expk, hg_expl = sem("hg_silu"), sem("hg_expq"), sem("hg_expk"), sem("hg_expl")
        hg_kgarg, hg_kg, hg_qgr = sem("hg_kgarg"), sem("hg_kg"), sem("hg_qgr")
        hg_kturned, hg_kcopied, hg_zeroed = sem("hg_kturned"), sem("hg_kcopied"), sem("hg_zeroed")
        hg_dist, hg_decay, hg_scaled = sem("hg_dist"), sem("hg_decay"), sem("hg_scaled")
        hg_score, hg_pick, hg_y, hg_state = sem("hg_score"), sem("hg_pick"), sem("hg_y"), sem("hg_state")
        hg_ready, hg_oT, hg_out = sem("hg_ready"), sem("hg_oT"), sem("hg_out")

        df_q, df_k, df_v = (place("diff", NT * T).rearrange("p (n t) -> p n t", n=NT) for _ in range(3))
        df_s = place("diff", 4 * T).rearrange("p (b m t) -> p b m t", b=2, m=2)
        df_attn = place("diff", 2 * T).rearrange("p (b t) -> p b t", b=2)
        df_attnT = place("diff", 2 * T).rearrange("p (b t) -> p b t", b=2)
        df_tmp, df_o = place("diff", BW), place("diff", BW)
        lam_p, lam_s, lam_e, lam_neg, sub_w = sm(128), sm(2), sm(2), sm(1), sm(1)
        df_nmax, df_den, df_r = sm(4), sm(4), sm(4)
        df_sq, df_var, df_std, df_rstd = sm(4), sm(4), sm(4), sm(4)
        df_score, df_masked, df_prob, df_mixed = sem("df_score"), sem("df_masked"), sem("df_prob"), sem("df_mixed")
        df_turned, df_copied, df_y = sem("df_turned"), sem("df_copied"), sem("df_y")
        df_ready, df_oT, df_out = sem("df_ready"), sem("df_oT"), sem("df_out")

        dl_q, dl_k = (place("dil", NT * T).rearrange("p (n t) -> p n t", n=NT) for _ in range(2))
        dl_v = [place("dil", NT * BW).rearrange("p (i n) -> p i n", i=NT) for _ in range(3)]
        dl_p = place("dil", DIL_H * DIL_BLOCKS * P).rearrange("p (j b k) -> p j b k", j=DIL_H, b=DIL_BLOCKS)
        dl_pT = place("dil", DIL_BLOCKS * P).rearrange("p (b k) -> p b k", b=DIL_BLOCKS)
        dl_stat = [sm(32).rearrange("p (a v) -> p a v", v=8) for _ in range(3)]
        dl_prev = sm(32).rearrange("p (a v) -> p a v", v=8)
        dl_nat = [sm(32).rearrange("p (a v) -> p a v", v=8) for _ in range(2)]
        dl_w = [sm(16).rearrange("p (a j) -> p a j", j=4) for _ in range(3)]
        dl_wg = [sm(16).rearrange("p (a j) -> p a j", j=4) for _ in range(2)]
        dl_low, dl_z, dl_t = (sm(16).rearrange("p (a j) -> p a j", j=4) for _ in range(3))
        dl_score, dl_masked, dl_prob = sem("dl_score"), sem("dl_masked"), sem("dl_prob")
        dl_stored, dl_back = sem("dl_stored"), sem("dl_back")
        dl_warg, dl_wexp, dl_weighed, dl_scaled = sem("dl_warg"), sem("dl_wexp"), sem("dl_weighed"), sem("dl_scaled")
        dl_turned, dl_copied, dl_y, dl_out = sem("dl_turned"), sem("dl_copied"), sem("dl_y"), sem("dl_out")
        DIL_SCORES = []
        for g in range(3):
            for j in range(DIL_H):
                DIL_SCORES.append((g, j, (0, 7, 11)[g], range(NT), False))
                if g == 0:
                    DIL_SCORES.append((g, j, 4, range(1, NT), True))

        gate_sb = place("merge", 2 * T).rearrange("p (b t) -> p b t", b=2)
        merged = place("merge", KD * T).rearrange("p (k t) -> p k t", k=KD)
        m_ring = [place("late", KB * 512).rearrange("p (k n) -> p k n", k=KB) for _ in range(2)]
        x2 = place("late", NT * D).rearrange("p (i d) -> p i d", i=NT)
        bc_gate1, bc_scale2, bc_shift2, bc_gate2, bc_final = (place("late", D) for _ in range(5))
        xg = [merged[:, 2 * s:2 * s + 2, :].rearrange("p k t -> p (k t)") for s in range(AHEAD)]
        xgT = [place("late", KD * BLK).rearrange("p (k t) -> p k t", k=KD) for _ in range(2)]
        e_act, e_hid = (place("late", 2 * BLK).rearrange("p (j t) -> p j t", j=2) for _ in range(2))
        yb = [place("late", D) for _ in range(2)]
        h2T = hT
        old_branches = branchT[:].rearrange("p c t -> p (c t)")
        h2 = old_branches[:, 0:NT * D].rearrange("p (i d) -> p i d", i=NT)
        w_wide = [w_ring[0][:], w_ring[1][:], hT[:].rearrange("p k t -> p (k t)"), old_branches[:, 0:2 * KD * F_EXP]]
        w_wide = [w.rearrange("p (g k f) -> p g k f", g=2, k=KD) for w in w_wide]
        w_down = [m.rearrange("p k n -> p (k n)") for m in m_ring] + [old_branches[:, KD * 512 + 2 * D * i:KD * 512 + 2 * D * i + 2 * D] for i in range(2)]
        w_down = [w.rearrange("p (j d) -> p j d", j=2) for w in w_down]
        scores = gate_sb[:, 0, 0:256].rearrange("p (i e) -> p i e", i=NT)
        sel = gate_sb[:, 0, 256:512].rearrange("p (i e) -> p i e", i=NT)
        hot = [gate_sb[:, 1, 256 * s:256 * s + 256].rearrange("p (i e) -> p i e", i=NT) for s in range(2)]
        both_hot = place("late", NT * N_EXP).rearrange("p (i e) -> p i e", i=NT)
        rank = place("late", NT * N_EXP).rearrange("p (i e) -> p i e", i=NT)
        picked = place("late", NT * N_EXP).rearrange("p (i e) -> p i e", i=NT)
        best8 = place("late", NT * GROUPS * 8).rearrange("p (i m) -> p i m", m=8)
        grp_score = sm(32).rearrange("p (i g) -> p i g", i=NT)
        grp_pen = sm(32).rearrange("p (i g) -> p i g", i=NT)
        top8 = place("late", NT * 8).rearrange("p (i e) -> p i e", i=NT)
        top_i = sb("top_i", [P, NT, 8], U32)
        top_f = place("late", NT * 8).rearrange("p (i e) -> p i e", i=NT)
        n_blk_e, blk_end = place("late", N_EXP), place("late", N_EXP)
        pair_s = sm(8).rearrange("p (i s) -> p i s", i=NT)
        pair_z = sm(4)
        pair_row = sm(8).rearrange("p (i s) -> p i s", i=NT)
        row_id = sb("row_id", [P, NT, 2], U32)
        nbc, endc = sb("nbc", [N_EXP, 2]), sb("endc", [N_EXP, 1])
        ended = place("late", N_BLK)[0:N_EXP]
        blk_exp = place("late", N_BLK)[0:1].bitcast(U32)
        n_blocks = sb("n_blocks", [1, 1], U32)
        no_entry = sb("no_entry", [P, LIST // P, 2], U32)
        blk_list = place("late", 2 * LIST_BLK)[0:BLK].bitcast(U32).rearrange("p (b a) -> p b a", a=2)
        blk_tok = [sb(f"blk_tok{i}", [BLK, 1], U32) for i in range(AHEAD)]
        blk_dst = [sb(f"blk_dst{i}", [BLK, 1], U32) for i in range(2)]
        row_in = sb("row_in", [P, NT, 2], U32)
        f_sq, f_var, f_std, f_rstd = sm(8), sm(8), sm(8), sm(8)
        out_ring = [w_ring[1][:, D * i:D * i + D] for i in range(NT)]
        yg = [w_ring[0][:, D * i:D * i + D] for i in range(4)]

        gate_done, gate_out, merge_done, merge_out = sem("gate_done"), sem("gate_out"), sem("merge_done"), sem("merge_out")
        merge_mul = sem("merge_mul")
        x2_loaded, scale2_ready = sem("x2_loaded"), sem("scale2_ready")
        row_spread, row_ready = sem("row_spread"), sem("row_ready")
        o_done, o_out = sem("o_done"), sem("o_out")
        h2_ready, h2_stored, h2_turned, h2T_ready = sem("h2_ready"), sem("h2_stored"), sem("h2_turned"), sem("h2T_ready")
        router_loaded, routed, scored = sem("router_loaded"), sem("routed"), sem("scored")
        hot_ready, ranked, nbc_ready, ends_done, ended_ready, owners_done = (
            sem("hot_ready"), sem("ranked"), sem("nbc_ready"), sem("ends_done"), sem("ended_ready"), sem("owners_done"))
        plan_ready, rows_ready, list_stored = sem("plan_ready"), sem("rows_ready"), sem("list_stored")
        passed = sem("passed")

        e_loaded = [sem(f"e_loaded{i}") for i in range(E_SLOTS)]
        down_loaded = [sem(f"down_loaded{i}") for i in range(E_SLOTS)]
        ids_loaded, ids_ready, xg_loaded = sem("ids_loaded"), sem("ids_ready"), [sem(f"xg_loaded{i}") for i in range(AHEAD)]
        xg_turned, xgT_ready = sem("xg_turned"), sem("xgT_ready")
        gu_done, gu_act, hid_ready = sem("gu_done"), sem("gu_act"), sem("hid_ready")
        down_done, y_act, y_dve = sem("down_done"), sem("y_act"), sem("y_dve")
        y_stored = [sem(f"y_stored{i}") for i in range(2)]
        yg_loaded, x3_ready = [sem(f"yg_loaded{i}") for i in range(2)], sem("x3_ready")
        out_ready_, out_stored, y_weighed = sem("out_ready"), sem("out_stored"), sem("y_weighed")

        TOKEN_MAJOR = {"z": 0, "v_c": 0, "i_d": 0, "g_d": 0, "v_b0": 0, "v_b1": 1, "v_b2": 2}
        tiles4 = lambda ap: [ap[:, n, :] for n in range(NT)]
        DEST = {"z": tiles4(z_tok), "xbc_a": [xbc_raw[:, i, 3:3 + T] for i in range(4)],
                "xbc_b": [xbc_raw[:, 4, 3:3 + T], xbc_raw[:, 5, 3:3 + T], dt_raw],
                "q_c": tiles4(df_q), "k_c": tiles4(df_k), "v_c": tiles4(df_v),
                "q_d": tiles4(hg_q), "f_d": tiles4(hg_k), "i_d": tiles4(hg_v), "g_d": tiles4(hg_g)}
        for g in range(3):
            DEST.update({f"q_b{g}": tiles4(dl_q), f"k_b{g}": tiles4(dl_k), f"v_b{g}": tiles4(dl_v[g])})
        for u in range(ADA_FIRST, ADA):
            DEST[f"ada{u}"] = [mod[:, 4 * u:4 * u + 4]]
        BRANCH_DONE = {0: ssd_out, KD: df_out, 2 * KD: hg_out, 3 * KD: dl_out}
        OUT_ORDER = [(0, 0), (1, 0), (0, 1), (1, 1), (2, 0), (2, 1), (3, 0), (3, 1)]
        m_slot = [w[:, KD * 256:KD * 256 + KB * 256].rearrange("p (k n) -> p k n", k=KB) for w in w_ring]
        g_slot = [w[:, 0:KD * 256].rearrange("p (k n) -> p k n", k=KD) for w in w_ring]

        block = ctx.enter_context(nc.Block())

        @block.sync
        def _(sp):
            def load_vec(row, src, n):
                sp.dma_start(rows[row:row + n, :], src).then_inc(vec_loaded, 16)

            for i in range(NT):
                sp.dma_start(x_tok[:, i, :], x_dram[:, i, :]).then_inc(x_loaded, 16)
            sp.dma_start(c_raw[:], c.rearrange("a (p k) -> (a p) k", k=KD)).then_inc(vec_loaded, 16)
            load_vec(R_BADA, b_ada.rearrange("a (j q) -> (a j) q", q=P), 48)
            load_vec(R_NMIX, norm_mix_w.rearrange("a (j q) -> (a j) q", q=P), KD)
            load_vec(R_NFFN, norm_ffn_w.rearrange("a (j q) -> (a j) q", q=P), KD)
            load_vec(R_FIN, final_norm_w.rearrange("(j q) -> j q", q=P), KD)
            load_vec(R_CONVB, conv_b.rearrange("a (j q) -> (a j) q", q=P), 6)
            load_vec(R_CONVW, conv_w.rearrange("a k (j q) -> (a k j) q", q=P), 24)
            load_vec(R_SSDN, ssd_norm_w.rearrange("a (j q) -> (a j) q", q=P), KB)
            load_vec(R_SUBLN, diff_subln_w, 1)
            for half in range(2):
                sp.dma_start(rows[R_HGN:R_HGN + 1, 64 * half:64 * half + 64], hgrn_norm_w).then_inc(vec_loaded, 16)
            load_vec(R_LB, hgrn_lb_logits.rearrange("a (j q) -> (a j) q", q=P), KB)
            for at_, src in ((B_DTB, ssd_dt_bias), (B_ALOG, ssd_a_log), (B_DSK, ssd_d),
                             (B_LAM, diff_lambda.rearrange("a i n -> a (i n)")),
                             (B_RB, router_bias.rearrange("(a n) -> a n", a=1))):
                n = src.shape[1]
                sp.dma_start(bc_row[:, at_:at_ + n], src).then_inc(vec_loaded, 16)

            for u in range(ADA_FIRST):
                sp.dma_start(ada_slot[u], ada_dram[:, :, 512 * u:512 * u + 512]).then_inc(w_loaded[u] if u < 2 else ada_loaded[u - 2], 16)

            def slot_free(n):
                before = UNITS[n - 2]
                if n - 2 < 2:
                    sp.wait_ge(w_used, n - 1)
                elif before.startswith("ada"):
                    sp.wait_ge(ada_summed, int(before[3:]) - ADA_FIRST + 1)
                elif before.startswith("merge"):
                    sp.wait_ge(merge_done, 2 * int(before[5:]) + 2)
                else:
                    sp.wait_ge(proj_done, out_ready(before))

            columns = {name: (c0, width) for name, c0, width, _ in PROJ}
            for n, name in enumerate(UNITS[2:], 2):
                if name == f"merge{3 * MERGE_UNITS // 4 + 2}":
                    sp.wait_ge(dl_out, NT)
                    sp.dma_start(x2, x_dram).then_inc(x2_loaded, 16)
                slot_free(n)
                if name.startswith("merge"):
                    u = int(name[5:])
                    b, c0 = MERGE_ORDER[u // 4], 256 * (u % 4)
                    sp.dma_start(g_slot[n % 2], in_dram[:, :, C_GATE + b * D + c0:C_GATE + b * D + c0 + 256]).then_inc(w_loaded[n % 2], 16)
                    sp.dma_start(m_slot[n % 2], w_merge[0][b].rearrange("(k p) n -> p k n", p=P)[:, :, c0:c0 + 256]).then_inc(w_loaded[n % 2], 16)
                elif name.startswith("out"):
                    c0 = 512 * int(name[3:])
                    sp.dma_start(w_slot[n % 2], w_out[0].rearrange("(k p) n -> p k n", p=P)[:, :, c0:c0 + 512]).then_inc(w_loaded[n % 2], 16)
                elif name.startswith("ada"):
                    c0 = 512 * int(name[3:])
                    sp.dma_start(w_slot[n % 2], ada_dram[:, :, c0:c0 + 512]).then_inc(w_loaded[n % 2], 16)
                else:
                    c0, width = columns[name]
                    sp.dma_start(w_slot[n % 2][:, :, 0:width], in_dram[:, :, c0:c0 + width]).then_inc(w_loaded[n % 2], 16)
            sp.dma_start(m_ring[0].rearrange("p k n -> p (k n)")[:, 0:KD * N_EXP].rearrange("p (k e) -> p k e", k=KD),
                         w_router.rearrange("(k p) e -> p k e", p=P)).then_inc(router_loaded, 16)
            for i in range(NT):
                sp.wait_ge(h2_ready, i + 1)
                sp.dma_start(h2_dram.rearrange("(i p) d -> p i d", p=P)[:, i, :], h2[:, i, :]).then_inc(h2_stored, 16)

            sp.wait_ge(o_done, 8)
            sp.wait_ge(routed, 1)
            sp.wait_ge(h2_stored, 16 * NT)
            sp.wait_ge(plan_ready, 2)
            n_valid = sp.value_load(n_blocks[0:1, 0:1], min_val=MIN_BLOCKS, max_val=MAX_BLOCKS)

            def expert_weights(b, s, first):
                e = sp.value_load(blk_exp[0:1, bass.ds(b, 1)], min_val=0, max_val=N_EXP - 1)
                if not first:
                    sp.wait_ge(gu_done, b - (E_SLOTS - 1))
                for half, w in enumerate((w_expert_gate, w_expert_up)):
                    sp.dma_start(w_wide[s][:, half],
                                 w[0][bass.ds(e, 1)].rearrange("a (p k) f -> (a p) k f", k=KD)).then_inc(e_loaded[s], 16)
                if not first:
                    sp.wait_ge(down_done, b - (E_SLOTS - 1))
                sp.dma_start(w_down[s], w_expert_down[0][bass.ds(e, 1)].rearrange("a (p j) d -> (a p) j d", j=2))\
                  .then_inc(down_loaded[s], 16)

            for s in range(E_SLOTS):
                expert_weights(s, s, True)
                if s == 0:
                    sp.wait_ge(xg_loaded[0], 16)
            with sp.Fori(1, N_BLK // E_SLOTS) as it:
                for s in range(E_SLOTS):
                    b = E_SLOTS * it + s
                    with sp.If(b < n_valid):
                        expert_weights(b, s, False)
            for s in range(2):
                sp.wait_ge(y_stored[s], 16 * ((n_valid + 1 - s) // 2))
            for i in range(NT):
                for s in range(2):
                    if i >= 2:
                        sp.wait_ge(x3_ready, i - 1)
                    sp.dma_start(yg[2 * (i % 2) + s], y_dram[T * s + P * i:T * s + P * i + P, :]).then_inc(yg_loaded[i % 2], 16)

        @block.gpsimd
        def _(pool):
            p = Order(pool, pool_order)
            p(pool.memset(ones[:], 1.0))
            for m in (ident, causal, band_prev, level_mask):
                p(pool.memset(m[:], 0.0))
            p(pool.affine_select(out=ident[:], in_=ident[:], compare_op=ALU.not_equal, fill=1.0, base=0,
                                 pattern=[[-1, P]], channel_multiplier=1))
            p(pool.affine_select(out=upper[:], in_=ones[:], compare_op=ALU.is_ge, fill=0.0, base=0,
                                 pattern=[[1, P]], channel_multiplier=-1))
            p(pool.affine_select(out=upper_strict[:], in_=ones[:], compare_op=ALU.is_gt, fill=0.0, base=0,
                                 pattern=[[1, P]], channel_multiplier=-1))
            p(pool.affine_select(out=causal[:], in_=causal[:], compare_op=ALU.is_ge, fill=NEG, base=0,
                                 pattern=[[-1, P]], channel_multiplier=1))
            p(pool.affine_select(out=band_prev[:], in_=band_prev[:], compare_op=ALU.is_ge, fill=NEG, base=0,
                                 pattern=[[1, P]], channel_multiplier=-1))
            p(pool.iota(apart[:], pattern=[[-1, P]], base=P, channel_multiplier=1), apart_ready)
            for n, b in enumerate(LEVELS):
                m = level_mask[:, n, :].rearrange("p (k s i) -> p k s i", s=2, i=b)[:, :, 1, :]
                one = ones[:].rearrange("p (k s i) -> p k s i", s=2, i=b)[:, :, 1, :]
                p(pool.affine_select(out=m, in_=one, compare_op=ALU.is_ge, fill=0.0, base=0,
                                     pattern=[[-2 * b, P // (2 * b)], [0, b]], channel_multiplier=1))
                p(pool.affine_select(out=m, in_=m, compare_op=ALU.is_ge, fill=0.0, base=b - 1,
                                     pattern=[[2 * b, P // (2 * b)], [0, b]], channel_multiplier=-1))
            h2 = two_heads[:].rearrange("p (h n) -> p h n", h=2)
            p(pool.affine_select(out=h2, in_=ones[:].rearrange("p (h n) -> p h n", h=2), compare_op=ALU.is_ge,
                                 fill=0.0, base=0, pattern=[[-64, 2], [0, 64]], channel_multiplier=1))
            p(pool.affine_select(out=h2, in_=h2, compare_op=ALU.is_ge, fill=0.0, base=63,
                                 pattern=[[64, 2], [0, 64]], channel_multiplier=-1))
            pool.iota(iota_exp[:], pattern=[[1, N_EXP]], base=0, channel_multiplier=0,
                      allow_small_or_imprecise_dtypes=True).then_inc(consts_ready, 1)
            pool.iota(iota_grp[:], pattern=[[1, GROUPS]], base=0, channel_multiplier=0,
                      allow_small_or_imprecise_dtypes=True).then_inc(consts_ready, 1)
            pool.iota(iota_blk[:], pattern=[[1, N_BLK]], base=0, channel_multiplier=0,
                      allow_small_or_imprecise_dtypes=True).then_inc(consts_ready, 1)
            pool.iota(entry[:, :, :, 0], pattern=[[P, NT], [0, 2]], base=0, channel_multiplier=1).then_inc(consts_ready, 1)
            pool.iota(entry[:, :, :, 1], pattern=[[P, NT], [T, 2]], base=0, channel_multiplier=1).then_inc(consts_ready, 1)
            for i in range(ADA - ADA_FIRST):
                name, acc = f"ada{ADA_FIRST + i}", ada_acc[i % 2]
                slot = unit_of[name] % 2
                pool.wait_ge(w_loaded[slot], in_slot(name))
                if i == 0:
                    pool.wait_ge(c_ready, 1)
                if i >= 2:
                    pool.wait_ge(proj_done, out_ready(f"ada{ADA_FIRST + i - 2}"))
                w = w_slot[slot]
                p(pool.tensor_tensor(w, w, along(c_act[:], 512), ALU.mult))
                p(pool.tensor_tensor(w[:, 0:4, :], w[:, 0:4, :], w[:, 4:8, :], ALU.add))
                p(pool.tensor_tensor(w[:, 0:2, :], w[:, 0:2, :], w[:, 2:4, :], ALU.add))
                p(pool.tensor_tensor(acc[:], w[:, 0, :], w[:, 1, :], ALU.add), ada_summed)
            pool.wait_ge(df_out, NT)
            pool.memset(hg_attn, 0.0).then_inc(hg_zeroed, 1)
            pool.wait_ge(dl_prob, len(DIL_SCORES))
            for g in range(2):
                pool.dma_start(stat_dram[g].rearrange("(p a) v -> p a v", a=4), dl_stat[g + 1]).then_inc(dl_stored, 16)
            pool.wait_ge(dl_stored, 32)
            for g in range(2):
                pool.dma_start(dl_nat[g], stat_dram[g].rearrange("(a p) v -> p a v", p=P)).then_inc(dl_back, 16)
            pool.wait_ge(dl_weighed, 3)
            for g in range(2):
                pool.dma_start(weight_dram[g].rearrange("(a p) v -> p a v", p=P), dl_w[g + 1]).then_inc(dl_stored, 16)
            pool.wait_ge(dl_stored, 64)
            for g in range(2):
                pool.dma_start(dl_wg[g], weight_dram[g].rearrange("(p a) v -> p a v", a=4)).then_inc(dl_back, 16)
            p(pool.memset(no_entry[:, :, 0], 0))
            p(pool.memset(no_entry[:, :, 1], 2 * T))
            pool.dma_start(list_dram.rearrange("(p n) a -> p n a", p=P), no_entry[:]).then_inc(list_stored, 16)
            pool.wait_ge(list_stored, 16)
            pool.wait_ge(rows_ready, 1)
            for i in range(NT):
                for s in range(2):
                    pool.indirect_dma_start(out=list_dram, out_offset=bass.IndirectOffsetOnAxis(ap=row_id[:, i, s:s + 1], axis=0),
                                            in_=entry[:, i, s, :], in_offset=None).then_inc(list_stored, 16)
            pool.wait_ge(list_stored, 16 + 16 * 2 * NT)
            pool.wait_ge(h2_stored, 16 * NT)
            pool.wait_ge(plan_ready, 2)
            n_valid = pool.value_load(n_blocks[0:1, 0:1], min_val=MIN_BLOCKS, max_val=MAX_BLOCKS)

            pool.dma_start(blk_list, list_dram.rearrange("(r b) a -> r b a", b=LIST_BLK)).then_inc(ids_loaded, 16)
            pool.wait_ge(ids_loaded, 16)

            blk_ids = blk_list.rearrange("p b a -> p (b a)")

            def gather(b, s, n):
                pool.tensor_copy(blk_tok[s][:], blk_ids[:, bass.ds(2 * b, 1)]).then_inc(ids_ready, 1)
                pool.wait_ge(ids_ready, n + 1)
                pool.sem_inc(passed)
                pool.indirect_dma_start(out=xg[s][0:BLK, :], out_offset=None, in_=h2_dram,
                                        in_offset=bass.IndirectOffsetOnAxis(ap=blk_tok[s][:], axis=0)).then_inc(xg_loaded[s], 16)

            def scatter(b, s, n):
                pool.wait_ge(y_act, b + 1)
                pool.wait_ge(y_dve, b + 1)
                pool.tensor_copy(blk_dst[s][:], blk_ids[:, bass.ds(2 * b + 1, 1)]).then_inc(ids_ready, 1)
                pool.wait_ge(ids_ready, n + 1)
                pool.sem_inc(passed)
                pool.indirect_dma_start(out=y_dram, out_offset=bass.IndirectOffsetOnAxis(ap=blk_dst[s][:], axis=0),
                                        in_=yb[s][0:BLK, :], in_offset=None, bounds_check=2 * T - 1, oob_is_err=False)\
                    .then_inc(y_stored[s], 16)

            for s in range(AHEAD):
                gather(s, s, s)
            for s in range(AHEAD):
                pool.wait_ge(xg_turned, s + 1)
                gather(s + AHEAD, s, AHEAD + 2 * s)
                scatter(s, s % 2, AHEAD + 2 * s + 1)
            with pool.Fori(1, N_BLK // AHEAD) as it:
                for s in range(AHEAD):
                    b = AHEAD * it + s
                    with pool.If(b < n_valid):
                        pool.wait_ge(xg_turned, b + 1)
                        gather(b + AHEAD, s, 2 * b + AHEAD)
                        scatter(b, s % 2, 2 * b + AHEAD + 1)

        @block.tensor
        def _(pe):
            pe.wait_ge(consts_ready, 5)
            pe.wait_ge(vec_loaded, 16 * 17)
            pe.transpose(bank[2][:, 0:N_ROWS], rows[:], ident[0:N_ROWS, 0:N_ROWS]).then_inc(cols_turned, 1)
            pe.matmul(bank[3][:, 0:N_BC], ones[0:1, :], bc_row[:], start=True, stop=True).then_inc(bc_spread, 1)

            def sum_partitions(ps, c0, acc):
                for j in range(4):
                    mm = pe.matmul(ps[:, c0 + j:c0 + j + 1], acc[:, P * j:P * j + P], ones[:, 0:1], start=True, stop=True)
                return mm

            for u in range(ADA_FIRST):
                pe.wait_ge(w_used, u + 1)
                sum_partitions(bank[4], 4 * u, ada_first[u]).then_inc(ada_done, 1)

            pe.wait_ge(xn_ready, NT)
            for k in range(KD):
                if k >= 2:
                    pe.wait_ge(h_ready, k - 1)
                for i in range(NT):
                    mm = pe.transpose(bank[k % 2][:, P * i:P * i + P], x_nrm[:, i, P * k:P * k + P], ident[:])
                mm.then_inc(x_turned, 1)
            pe.wait_ge(h_ready, KD)

            def at_unit(name):
                n = unit_of[name]
                pe.wait_ge(w_loaded[n % 2], in_slot(name))
                return n % 2

            def project(name, m):
                o, slot = first_out[name] + m, unit_of[name] % 2
                w, ps = w_slot[slot], proj_ps[o % 2]
                if name.startswith("ada"):
                    pe.wait_ge(ada_summed, int(name[3:]) - ADA_FIRST + 1)
                elif m == 0:
                    at_unit(name)
                if o >= 2:
                    pe.wait_ge(proj_out, o - 1)
                if name.startswith("ada"):
                    mm = sum_partitions(ps, 0, ada_acc[int(name[3:]) % 2])
                elif (name, m) == ("xbc_b", 2):
                    for a in range(NT):
                        for k in range(KD):
                            mm = pe.matmul(ps[:, 8 * a:8 * a + 8], hT[:, k, P * a:P * a + P], w[:, k, 256:264],
                                           start=(k == 0), stop=(k == KD - 1))
                elif name in TOKEN_MAJOR:
                    for k in range(KD):
                        mm = pe.matmul(ps[:], tokens_of(hT[:, k, :], TOKEN_MAJOR[name], m), w[:, k, :], start=(k == 0), stop=(k == KD - 1))
                else:
                    for k in range(KD):
                        mm = pe.matmul(ps[:], w[:, k, P * m:P * m + P], hT[:, k, :], start=(k == 0), stop=(k == KD - 1))
                mm.then_inc(proj_done, 1)

            def merge(t):
                b, name = MERGE_ORDER[t // KD], f"merge{t // 2}"
                slot = unit_of[name] % 2
                if t in BRANCH_DONE:
                    pe.wait_ge(BRANCH_DONE[t], NT)
                    pe.wait_ge(proj_out, out_ready(PROJ[N_BEFORE - 1][0]) if t < 2 * KD else out_ready("v_b2"))
                if t % 2 == 0:
                    at_unit(name)
                if t:
                    pe.wait_ge(gate_out, t)
                c0 = P * (t % 2)
                for k in range(KD):
                    mm = pe.matmul(proj_ps[0][:], g_slot[slot][:, k, c0:c0 + P], hT[:, k, :], start=(k == 0), stop=(k == KD - 1))
                mm.then_inc(gate_done, 1)
                if t:
                    pe.wait_ge(merge_mul, t)
                for k in range(KB):
                    mm = pe.matmul(proj_ps[1][:], m_slot[slot][:, k, c0:c0 + P], branchT[:, b * KB + k, :], start=(k == 0), stop=(k == KB - 1))
                mm.then_inc(merge_done, 1)

            def emit(items):
                for name, m in items:
                    if name == "merge":
                        merge(m)
                    else:
                        project(name, m)

            emit(outputs("z", "xbc_a", "xbc_b"))
            emit(FILL["ssd"][0])
            pe.wait_ge(ssd_act, 6)
            for i in range(NT):
                if i >= 2:
                    pe.wait_ge(ssd_tok, i - 1)
                for t in range(4):
                    mm = pe.transpose(bank[i % 2][:, P * t:P * t + P], xbcT[:, t, P * i:P * i + P], ident[:])
                mm.then_inc(ssd_turned, 1)
            for i in range(NT):
                mm = pe.transpose(bank[2][:, P * i:P * i + P], xbcT[:, 4, P * i:P * i + P], ident[:])
            mm.then_inc(ssd_turned, 1)
            pe.wait_ge(adt_ready, 1)
            pe.matmul(bank[3][:, 0:32], upper[:], adt, start=True, stop=True)
            pe.matmul(bank[3][:, 32:64], ones[:], adt, start=True, stop=True).then_inc(acs_done, 1)
            emit(FILL["ssd"][1])
            pe.wait_ge(acs_ready, 1)
            pe.wait_ge(ssd_tok, NT + 1)
            for i in range(NT):
                s = slice(P * i, P * i + P)
                if i:
                    pe.wait_ge(ssd_m, i)
                    pe.wait_ge(ssd_state, i)
                for g in range(2):
                    pe.matmul(bank[5 * g][:, 0:P], xbcT[64 * g:64 * g + 64, 4, s], xbcT[64 * g:64 * g + 64, 5, s],
                              start=True, stop=True)
                for h in range(SSD_H):
                    mm = pe.matmul(bank[1 + h // 4][:, P * (h % 4):P * (h % 4) + P],
                                   adt[:, 8 * i + h:8 * i + h + 1].to_broadcast([P, P]), upper[:], start=True, stop=True)
                mm.then_inc(ssd_score, 1)
                emit(FILL["ssd"][2 + 2 * i])
                pe.wait_ge(ssd_m, i + 1)
                if i:
                    pe.wait_ge(ssd_out, i)
                for h in range(SSD_H):
                    mm = pe.matmul(bank[3][:, 64 * h:64 * h + 64], ssd_l[:, h, :], xs_dt[:, i % 2, 64 * h:64 * h + 64],
                                   start=True, stop=True)
                if i:
                    pe.wait_ge(ssd_state, i)
                    mm = pe.matmul(bank[4][:], xbcT[:, 5, s], ssd_r, start=True, stop=True)
                if i < NT - 1:
                    mm = pe.matmul(bank[5][:], b_tok[:, i, :], xs_dec[:, i % 2, :], start=True, stop=True)
                mm.then_inc(ssd_y, 1)
                emit(FILL["ssd"][3 + 2 * i])
                pe.wait_ge(ssd_o, i + 1)
                for j in range(KB):
                    mm = pe.transpose(bank[4][:, P * j:P * j + P], ssd_yt[:, P * j:P * j + P], ident[:])
                mm.then_inc(ssd_oT, 1)
            DF_STEPS = [(i, h) for i in range(NT) for h in range(DIFF_H)]
            pe.wait_ge(proj_out, out_ready("v_c"))
            pe.wait_ge(ssd_out, NT)

            def df_scores(n):
                i, h = DF_STEPS[n]
                if n >= 2:
                    pe.wait_ge(df_masked, 2 * n - 2)
                for m in range(2):
                    s = slice(64 * m, 64 * m + 64)
                    mm = pe.matmul(bank[2 * (n % 2) + m][:, 0:P * (i + 1)], df_q[s, h, P * i:P * i + P],
                                   df_k[s, h, 0:P * (i + 1)], start=True, stop=True)
                mm.then_inc(df_score, 1)

            df_scores(0)
            for n, (i, h) in enumerate(DF_STEPS):
                if n + 1 < len(DF_STEPS):
                    df_scores(n + 1)
                emit(FILL["diff"][n])
                pe.wait_ge(df_mixed, n + 1)
                if n:
                    pe.wait_ge(df_copied, n)
                if h == 0 and i:
                    pe.wait_ge(df_out, i)
                for b in range(i + 1):
                    mm = pe.transpose(bank[4][:, P * b:P * b + P], df_attn[:, n % 2, P * b:P * b + P], ident[:])
                mm.then_inc(df_turned, 1)
                pe.wait_ge(df_copied, n + 1)
                for b in range(i + 1):
                    mm = pe.matmul(bank[5][:, P * h:P * h + P], df_attnT[:, n % 2, P * b:P * b + P],
                                   df_v[:, b, P * h:P * h + P], start=(b == 0), stop=(b == i))
                mm.then_inc(df_y, 1)
                if h == DIFF_H - 1:
                    pe.wait_ge(df_ready, i + 1)
                    for j in range(KB):
                        mm = pe.transpose(bank[4][:, P * j:P * j + P], df_o[:, P * j:P * j + P], ident[:])
                    mm.then_inc(df_oT, 1)

            emit(FILL["hg"][0])
            pe.wait_ge(df_out, NT)
            pe.wait_ge(hg_kg, 1)
            for i in range(NT):
                if i >= 2:
                    pe.wait_ge(hg_kcopied, i - 1)
                for n in range(NT):
                    mm = pe.transpose(bank[i % 2][:, P * n:P * n + P], hg_qk[0][:, n, P * i:P * i + P], ident[:])
                mm.then_inc(hg_kturned, 1)
            pe.wait_ge(hg_kcopied, NT)
            for lv in range(len(LEVELS) + 1):
                keys, queries = (hg_k, hg_q) if lv == 0 else (hg_qk[(lv - 1) % 2],) * 2
                if lv:
                    emit(FILL["hg"][lv])
                    pe.wait_ge(hg_scaled, lv)
                for i in range(NT):
                    for s in range(2):
                        q = 8 * lv + 2 * i + s
                        if q >= 6:
                            pe.wait_ge(hg_pick, q - 5)
                        for n in range(NT):
                            mm = pe.matmul(bank[q % 6][:, P * n:P * n + P], keys[64 * s:64 * s + 64, n, P * i:P * i + P],
                                           queries[64 * s:64 * s + 64, n, P * i:P * i + P], start=True, stop=True)
                        mm.then_inc(hg_score, 1)
            emit(FILL["hg"][len(LEVELS) + 1])
            pe.wait_ge(hg_pick, 8 * (len(LEVELS) + 1))
            pe.wait_ge(hg_qgr, 1)
            for i in range(NT):
                if i:
                    pe.wait_ge(hg_state, i)
                    pe.wait_ge(hg_ready, i)
                    for n in range(NT):
                        pe.matmul(bank[0][:, P * n:P * n + P], hg_qg[:, n, P * i:P * i + P], hg_r[:, n, :],
                                  start=(n == 0), stop=False, skip_group_check=True)
                for h in range(HG_H):
                    mm = pe.matmul(bank[0][:, 64 * h:64 * h + 64], hg_attn[:, i, h % 2, h // 2, :],
                                   hg_v[:, i, 64 * h:64 * h + 64], start=(i == 0 and h == 0), stop=(h == HG_H - 1),
                                   skip_group_check=True)
                if i < NT - 1:
                    for n in range(NT):
                        mm = pe.matmul(bank[1][:, P * n:P * n + P], hg_ktok[:, i, P * n:P * n + P],
                                       hg_v[:, i, P * n:P * n + P], start=True, stop=True)
                mm.then_inc(hg_y, 1)
                if i < NT - 1:
                    emit(FILL["hg"][len(LEVELS) + 2 + i])
                pe.wait_ge(hg_ready, i + 1)
                if i:
                    pe.wait_ge(hg_out, i)
                for j in range(KB):
                    mm = pe.transpose(bank[2][:, P * j:P * j + P], hg_o[:, P * j:P * j + P], ident[:])
                mm.then_inc(hg_oT, 1)

            for g in range(3):
                if g == 0:
                    pe.wait_ge(gate_out, 2 * KD)
                    pe.wait_ge(merge_mul, 2 * KD)
                emit(outputs(f"q_b{g}", f"k_b{g}", f"v_b{g}"))
                pe.wait_ge(proj_out, out_ready(f"v_b{g}"))
                if g == 0:
                    pe.wait_ge(hg_out, NT)
                for n, (gg, j, _, tiles, prev) in enumerate(DIL_SCORES):
                    if gg != g:
                        continue
                    if n >= 4:
                        pe.wait_ge(dl_masked, n - 3)
                    for c_, a in enumerate(tiles):
                        mm = pe.matmul(bank[n % 4][:, P * c_:P * c_ + P], tokens_of(dl_q[:, j, :], g, a),
                                       tokens_of(dl_k[:, j, :], g, a - 1 if prev else a), start=True, stop=True)
                    mm.then_inc(dl_score, 1)
            emit(FILL["dil"][0])
            for j in range(DIL_H):
                pe.wait_ge(dl_scaled, 4 * j + 4)
                if j:
                    pe.wait_ge(dl_copied, 4 * j)
                for b in range(DIL_BLOCKS):
                    mm = pe.transpose(bank[b // 4][:, P * (b % 4):P * (b % 4) + P], dl_p[:, j, b, :], ident[:])
                    if b % 4 == 3 or b == DIL_BLOCKS - 1:
                        mm.then_inc(dl_turned, 1)
                emit(FILL["dil"][1 + j])
                pe.wait_ge(dl_copied, 4 * j + 4)
                if j >= 2:
                    pe.wait_ge(dl_out, j - 1)
                y = bank[4 + j % 2][:]
                s = slice(P * j, P * j + P)
                for b in range(DIL_BLOCKS):
                    g, a, key = ((0, b, b) if b < 4 else (0, b - 3, b - 4) if b < 7 else
                                 (1, b - 7, b - 7) if b < 11 else (2, b - 11, b - 11))
                    mm = pe.matmul(tokens_of(y, g, a), dl_v[g][:, key, s], dl_pT[:, b, :],
                                   start=(b == 0), stop=(b == DIL_BLOCKS - 1), skip_group_check=True)
                mm.then_inc(dl_y, 1)
            emit(merges[3 * KD:])
            pe.wait_ge(mod_copied, 2)
            for v, (src, c0) in enumerate(((mod, 16), (scale_ffn, 0), (mod, 24), (mod, 40), (cols, R_FIN))):
                if v == 1:
                    pe.wait_ge(scale2_ready, 1)
                for half in range(2):
                    q = 2 * v + half
                    if q >= 2:
                        pe.wait_ge(row_ready, q - 1)
                    for j in range(4):
                        at_ = c0 + 4 * half + j
                        mm = pe.matmul(bank[2 + q % 2][:, P * j:P * j + P], src[:, at_:at_ + 1].to_broadcast([P, P]), ident[:],
                                       start=True, stop=True)
                    mm.then_inc(row_spread, 1)
            pe.wait_ge(merge_out, 32)
            for o, (i, half) in enumerate(OUT_ORDER):
                    n = unit_of[f"out{half}"]
                    if i == 0:
                        at_unit(f"out{half}")
                    if o >= 2:
                        pe.wait_ge(o_out, o - 1)
                    for k in range(KD):
                        mm = pe.matmul(bank[4 + o % 2][:], merged[:, k, P * i:P * i + P], w_slot[n % 2][:, k, :],
                                       start=(k == 0), stop=(k == KD - 1))
                    mm.then_inc(o_done, 1)
            pe.wait_ge(h2_ready, NT)
            for k in range(KD):
                if k >= 2:
                    pe.wait_ge(h2T_ready, k - 1)
                for i in range(NT):
                    mm = pe.transpose(bank[k % 2][:, P * i:P * i + P], h2[:, i, P * k:P * k + P], ident[:])
                mm.then_inc(h2_turned, 1)
            pe.wait_ge(h2T_ready, KD)
            pe.wait_ge(router_loaded, 16)
            w_r = m_ring[0].rearrange("p k n -> p (k n)")[:, 0:KD * N_EXP].rearrange("p (k e) -> p k e", k=KD)
            for i in range(NT):
                for k in range(KD):
                    mm = pe.matmul(bank[2][:, N_EXP * i:N_EXP * i + N_EXP], h2T[:, k, P * i:P * i + P], w_r[:, k, :],
                                   start=(k == 0), stop=(k == KD - 1))
            mm.then_inc(routed, 1)
            pe.wait_ge(hot_ready, NT)
            for i in range(NT):
                r = bank[3][:, N_EXP * i:N_EXP * i + N_EXP]
                for j in range(i):
                    pe.matmul(r, ones[:], both_hot[:, j, :], start=(j == 0), stop=False)
                pe.matmul(r, upper_strict[:], both_hot[:, i, :], start=(i == 0), stop=True)
            for i in range(NT):
                pe.matmul(bank[4][:, 0:N_EXP], ones[:], both_hot[:, i, :], start=(i == 0), stop=(i == NT - 1))
            for i in range(NT):
                mm = pe.matmul(bank[5][0:N_EXP, 0:1], both_hot[:, i, :], ones[:, 0:1], start=(i == 0), stop=(i == NT - 1))
            mm.then_inc(ranked, 1)
            pe.wait_ge(nbc_ready, 1)
            pe.matmul(bank[5][0:N_EXP, 0:1], upper[0:N_EXP, 0:N_EXP], nbc[:, 0:1], start=True, stop=True).then_inc(ends_done, 1)
            pe.wait_ge(ended_ready, 1)
            pe.matmul(bank[4][0:1, 0:N_BLK], ones[0:N_EXP, 0:1], ended, start=True, stop=True).then_inc(owners_done, 1)

            pe.wait_ge(plan_ready, 2)
            n_valid = pe.value_load(n_blocks[0:1, 0:1], min_val=MIN_BLOCKS, max_val=MAX_BLOCKS)

            def turn_rows(b, s, first=False):
                pe.wait_ge(xg_loaded[s], 4 * (b - s) + 16)
                if not first:
                    pe.wait_ge(xgT_ready, b)
                pe.sem_inc(passed)
                for k in range(KD):
                    mm = pe.transpose(bank[0][:, BLK * k:BLK * k + BLK], xg[s][0:BLK, :].rearrange("p (q k) -> p k q", k=KD)[:, k, :],
                                      ident[0:BLK, 0:BLK])
                mm.then_inc(xg_turned, 1)

            def expert(b, s):
                pe.wait_ge(e_loaded[s], 8 * (b - s) + 32)
                pe.wait_ge(xgT_ready, b + 1)
                gu = bank[2 + s % 2]
                for m in range(4):
                    for k in range(KD):
                        mm = pe.matmul(gu[:, BLK * m:BLK * m + BLK], w_wide[s][:, m // 2, k, m % 2:F_EXP:2], xgT[s % 2][:, k, :],
                                       start=(k == 0), stop=(k == KD - 1))
                mm.then_inc(gu_done, 1)
                turn_rows(b + 1, (s + 1) % AHEAD)
                pe.wait_ge(down_loaded[s], 4 * (b - s) + 16)
                pe.wait_ge(hid_ready, b + 1)
                if not (isinstance(b, int) and b == 0):
                    pe.wait_ge(y_act, b)
                    pe.wait_ge(y_dve, b)
                for half in range(2):
                    for j in range(2):
                        mm = pe.matmul((bank[5], proj_ps[0])[half][0:BLK, :], e_hid[:, j, :],
                                       w_down[s][:, j, 512 * half:512 * half + 512], start=(j == 0), stop=(j == 1))
                mm.then_inc(down_done, 1)

            assert AHEAD == E_SLOTS
            turn_rows(0, 0, True)
            for s in range(E_SLOTS):
                expert(s, s)
            with pe.Fori(1, N_BLK // E_SLOTS) as it:
                for s in range(E_SLOTS):
                    b = E_SLOTS * it + s
                    with pe.If(b < n_valid):
                        expert(b, s)

        @block.scalar
        def _(act):
            a_ = Order(act, act_order)
            act.wait_ge(vec_loaded, 16 * 17)
            act.activation(c_act[:], c_raw[:], ACT.Silu).then_inc(c_ready, 1)
            act.wait_ge(x_loaded, 16 * NT)
            for i in range(NT):
                a_(act.activation(junk, x_tok[:, i, :], ACT.Square, accum_out=x_sq[:, i:i + 1]))
            act.wait_ge(var_ready, 1)
            a_(act.activation(x_std, x_var, ACT.Sqrt), std_ready)

            def drain(items):
                for name, m in items:
                    if name == "merge":
                        act.wait_ge(gate_done, m + 1)
                        if m >= 2:
                            act.wait_ge(merge_out, m - 1)
                        act.activation(gate_sb[:, m % 2, :], proj_ps[0][:], ACT.Sigmoid).then_inc(gate_out, 1)
                    else:
                        o, dst = first_out[name] + m, DEST[name][m]
                        act.wait_ge(proj_done, o + 1)
                        act.activation(dst, proj_ps[o % 2][:, 0:dst.shape[-1]], ACT.Copy).then_inc(proj_out, 1)

            act.wait_ge(h_ready, KD)
            drain(outputs("z", "xbc_a", "xbc_b"))
            for t in range(6):
                act.wait_ge(ssd_conv, t + 1)
                act.activation(xbcT[:, t, :], xbcT[:, t, :], ACT.Silu, bias=cols[:, R_CONVB + t:R_CONVB + t + 1])\
                   .then_inc(ssd_act, 1)
                if t % 2:
                    drain(DRAIN["ssd"][0][t // 2:t // 2 + 1])
            act.activation(z_tok, z_tok, ACT.Silu).then_inc(z_act, 1)
            act.wait_ge(dt_abs, 1)
            act.activation(dt_e, dt_a, ACT.Exp).then_inc(dt_exp, 1)
            act.activation(a_neg, bc[:, B_ALOG:B_ALOG + 8], ACT.Exp).then_inc(dt_exp, 1)
            act.wait_ge(dt_arg, 1)
            act.activation(dt_e, dt_e, ACT.Ln).then_inc(dt_ln, 1)
            for i in range(NT + 1):
                act.wait_ge(ssd_turned, i + 1)
                dst = xs_tok[:, i, :] if i < NT else b_tok
                act.activation(dst, bank[i % 2 if i < NT else 2][:], ACT.Copy).then_inc(ssd_tok, 1)
            drain(DRAIN["ssd"][1])
            act.wait_ge(acs_ready, 1)
            act.activation(eacs, acs, ACT.Exp).then_inc(acs_exp, 1)
            act.wait_ge(acs_ready, 2)
            act.activation(dec, dec, ACT.Exp).then_inc(acs_exp, 1)
            for i in range(NT):
                drain(DRAIN["ssd"][2 + 2 * i])
                act.wait_ge(ssd_diff, i + 1)
                act.activation(ssd_l, ssd_l, ACT.Exp).then_inc(ssd_decay, 1)
                drain(DRAIN["ssd"][3 + 2 * i])
                act.wait_ge(ssd_gated, i + 1)
                act.activation(ssd_tmp, ssd_yt, ACT.Square, accum_out=y_sq[:, i:i + 1]).then_inc(squared, 1)
                act.wait_ge(var_ready, i + 2)
                act.activation(y_std[:, i:i + 1], y_var[:, i:i + 1], ACT.Sqrt).then_inc(std_ready, 1)
            act.wait_ge(exp_arg, 1)
            act.activation(lam_e, lam_s, ACT.Exp).then_inc(exp_out, 1)
            drain(DRAIN["ssd"][-1])
            act.wait_ge(ssd_out, NT)

            def df_exp(n):
                i = n // DIFF_H
                act.wait_ge(df_masked, 2 * n + 2)
                if n >= 2:
                    act.wait_ge(df_mixed, n - 1)
                for m in range(2):
                    v = 2 * (n % 2) + m
                    act.activation(df_s[:, n % 2, m, 0:P * (i + 1)], df_s[:, n % 2, m, 0:P * (i + 1)], ACT.Exp,
                                   bias=df_nmax[:, v:v + 1], accum_out=df_den[:, v:v + 1]).then_inc(df_prob, 1)

            df_exp(0)
            for n in range(NT * DIFF_H):
                if n + 1 < NT * DIFF_H:
                    df_exp(n + 1)
                drain(DRAIN["diff"][n])
                act.wait_ge(df_turned, n + 1)
                if n >= 2:
                    act.wait_ge(df_y, n - 1)
                w = P * (n // DIFF_H + 1)
                act.activation(df_attnT[:, n % 2, 0:w], bank[4][:, 0:w], ACT.Copy).then_inc(df_copied, 1)
                if n % DIFF_H == DIFF_H - 1:
                    act.wait_ge(df_y, n + 1)
                    act.activation(df_tmp, bank[5][:], ACT.Square).then_inc(squared, 1)
                    act.wait_ge(var_ready, 1 + NT + n // DIFF_H + 1)
                    act.activation(df_std, df_var, ACT.Sqrt).then_inc(std_ready, 1)
            drain(DRAIN["diff"][-1])
            act.wait_ge(exp_arg, 2)
            act.activation(lb_e, lb_e, ACT.Exp).then_inc(exp_out, 1)
            act.wait_ge(proj_out, out_ready(PROJ[N_BEFORE - 1][0]))
            act.activation(hg_k, hg_k, ACT.Sigmoid).then_inc(hg_sig, 1)
            act.activation(hg_q, hg_q, ACT.Silu).then_inc(hg_silu, 1)
            act.activation(hg_g, hg_g, ACT.Silu).then_inc(hg_silu, 1)
            drain(DRAIN["hg"][0][0:1])
            act.wait_ge(hg_f, NT)
            act.wait_ge(df_out, NT)
            act.activation(hg_log, hg_k, ACT.Ln).then_inc(hg_ln, 1)
            drain(DRAIN["hg"][0][1:2])
            act.wait_ge(hg_scan, 16)
            act.activation(hg_last, hg_cum.rearrange("p n (i t) -> p (n i) t", t=P)[:, :, P - 1], ACT.Exp).then_inc(hg_expl, 1)
            act.wait_ge(hg_kgarg, 1)
            act.activation(hg_qk[0], hg_qk[0], ACT.Exp).then_inc(hg_expk, 1)
            act.activation(hg_qg, hg_cum, ACT.Exp).then_inc(hg_expq, 1)
            drain(DRAIN["hg"][0][2:])
            for i in range(NT):
                act.wait_ge(hg_kturned, i + 1)
                act.activation(hg_ktok[:, i, :], bank[i % 2][:], ACT.Copy).then_inc(hg_kcopied, 1)
            for lv in range(1, len(LEVELS) + 1):
                drain(DRAIN["hg"][lv])
                act.wait_ge(hg_dist, lv)
                act.activation(hg_qk[(lv - 1) % 2], hg_qk[(lv - 1) % 2], ACT.Exp).then_inc(hg_decay, 1)
            drain(DRAIN["hg"][len(LEVELS) + 1])
            for i in range(NT):
                drain(DRAIN["hg"][len(LEVELS) + 2 + i])
                act.wait_ge(hg_y, i + 1)
                act.activation(hg_tmp, bank[0][:], ACT.Square).then_inc(squared, 1)
                act.wait_ge(var_ready, 1 + 2 * NT + i + 1)
                act.activation(hg_std, hg_var, ACT.Sqrt).then_inc(std_ready, 1)
            act.wait_ge(hg_out, NT)
            for g in range(3):
                if g:
                    act.wait_ge(dl_score, 4 + 4 * g)
                drain(outputs(f"q_b{g}", f"k_b{g}", f"v_b{g}"))
                for n, (gg, j, b0, tiles, prev) in enumerate(DIL_SCORES):
                    if gg == g and (g or prev):
                        act.wait_ge(dl_masked, n + 1)
                        for part, (first, who) in enumerate(((0, range(NT)), (4, range(1, NT))) if g == 0 else ((b0, tiles),)):
                            stat = dl_prev if part else dl_stat[g]
                            for c_, a in enumerate(who):
                                e = act.activation(dl_p[:, j, first + c_, :], dl_p[:, j, first + c_, :], ACT.Exp,
                                                   bias=dl_stat[g][:, a, j:j + 1], accum_out=stat[:, a, 4 + j:5 + j])
                            e.then_inc(dl_prob, 1)
            drain(DRAIN["dil"][0][0:1])
            act.wait_ge(dl_warg, 3)
            for g in range(3):
                act.activation(dl_w[g], dl_w[g], ACT.Exp).then_inc(dl_wexp, 1)
            drain(DRAIN["dil"][0][1:])
            for j in range(DIL_H):
                drain(DRAIN["dil"][1 + j])
                if j:
                    act.wait_ge(dl_y, j)
                for q in range(4):
                    n = min(4, DIL_BLOCKS - 4 * q)
                    act.wait_ge(dl_turned, 4 * j + q + 1)
                    act.activation(dl_pT[:, 4 * q:4 * q + n, :], bank[q][:, 0:P * n].rearrange("p (b k) -> p b k", k=P), ACT.Copy)\
                       .then_inc(dl_copied, 1)
            drain(DRAIN["dil"][-1] + merges[3 * KD:])
            act.wait_ge(dl_out, NT)
            for v, dst in enumerate((bc_gate1, bc_scale2, bc_shift2, bc_gate2, bc_final)):
                for half in range(2):
                    q = 2 * v + half
                    act.wait_ge(row_spread, q + 1)
                    act.activation(dst[:, 512 * half:512 * half + 512], bank[2 + q % 2][:], ACT.Copy).then_inc(row_ready, 1)
            for i in range(NT):
                act.wait_ge(o_out, OUT_ORDER.index((i, 1)) + 1)
                act.wait_ge(squared, 3 * NT + i)
                act.activation(yb[0], x2[:, i, :], ACT.Square, accum_out=f_sq[:, i:i + 1]).then_inc(squared, 1)
                act.wait_ge(var_ready, 1 + 3 * NT + i + 1)
                act.activation(f_std[:, i:i + 1], f_var[:, i:i + 1], ACT.Sqrt).then_inc(std_ready, 1)
            act.wait_ge(routed, 1)
            act.activation(scores, bank[2][:, 0:NT * N_EXP].rearrange("p (i e) -> p i e", i=NT), ACT.Sigmoid).then_inc(scored, 1)

            act.wait_ge(plan_ready, 2)
            n_valid = act.value_load(n_blocks[0:1, 0:1], min_val=MIN_BLOCKS, max_val=MAX_BLOCKS)

            def rows_out(b, s):
                act.wait_ge(xg_turned, b + 1)
                act.activation(xgT[s], bank[0][:].rearrange("p (k t) -> p k t", k=KD), ACT.Copy).then_inc(xgT_ready, 1)

            def expert_act(b, s, first):
                act.wait_ge(gu_done, b + 1)
                act.activation(e_act, bank[2 + s % 2][:, 0:2 * BLK].rearrange("p (j t) -> p j t", j=2), ACT.Silu).then_inc(gu_act, 1)
                rows_out(b + 1, 1 - s)
                act.wait_ge(down_done, b + 1)
                if not first:
                    act.wait_ge(y_stored[s], 8 * (b - s))
                act.activation(yb[s][0:BLK, 0:512], bank[5][0:BLK, :], ACT.Copy).then_inc(y_act, 1)

            rows_out(0, 0)
            for s in range(2):
                expert_act(s, s, True)
            with act.Fori(1, N_BLK // 2) as it:
                for s in range(2):
                    b = 2 * it + s
                    with act.If(b < n_valid):
                        expert_act(b, s, False)
            def store(i):
                act.wait_ge(out_ready_, i + 1)
                act.dma_start(out_dram[:, i, :], out_ring[i]).then_inc(out_stored, 16)

            def weigh(i):
                act.wait_ge(yg_loaded[i % 2], 32 * (i // 2 + 1))
                act.activation(yg[2 * (i % 2)], yg[2 * (i % 2)], ACT.Copy, scale=pair_s[:, i, 0:1]).then_inc(y_weighed, 1)

            weigh(0)
            for i in range(NT):
                if i + 1 < NT:
                    weigh(i + 1)
                act.wait_ge(x3_ready, i + 1)
                act.activation(out_ring[i], x2[:, i, :], ACT.Square, accum_out=f_sq[:, NT + i:NT + i + 1]).then_inc(squared, 1)
                act.wait_ge(var_ready, 1 + 4 * NT + i + 1)
                act.activation(f_std[:, NT + i:NT + i + 1], f_var[:, NT + i:NT + i + 1], ACT.Sqrt).then_inc(std_ready, 1)
                if i:
                    store(i - 1)
            store(NT - 1)
            act.wait_ge(out_stored, 16 * NT)

        @block.vector
        def _(dve):
            d = Order(dve, dve_order)
            dve.wait_ge(apart_ready, 1)
            d(dve.tensor_scalar(apart[:], apart[:], 3, None, ALU.bitwise_and))
            d(dve.tensor_scalar(causal_4th[:], apart[:], 0.0, NEG, ALU.is_gt, ALU.mult))
            dve.wait_ge(cols_turned, 1)
            d(dve.tensor_copy(cols[:], bank[2][:, 0:N_ROWS]))
            dve.wait_ge(bc_spread, 1)
            d(dve.tensor_copy(bc[:], bank[3][:, 0:N_BC]))
            dve.wait_ge(act_order, NT)
            d(dve.tensor_scalar(x_var, x_sq, 1.0 / D, EPS, ALU.mult, ALU.add), var_ready)
            dve.wait_ge(std_ready, 1)
            d(dve.reciprocal(x_rstd, x_std))
            for i in range(NT):
                d(dve.tensor_scalar(x_nrm[:, i, :], x_tok[:, i, :], x_rstd[:, i:i + 1], None, ALU.mult), xn_ready)
            dve.wait_ge(c_ready, 1)
            for u in range(ADA_FIRST):
                w, acc = ada_slot[u], ada_first[u]
                dve.wait_ge(w_loaded[u] if u < 2 else ada_loaded[u - 2], 16)
                d(dve.tensor_scalar(acc, w[:, 0, :], c_act[:, 0:1], None, ALU.mult))
                for k in range(1, KD):
                    d(dve.scalar_tensor_tensor(acc, w[:, k, :], c_act[:, k:k + 1], acc, ALU.mult, ALU.add),
                      w_used if k == KD - 1 else None)
            dve.wait_ge(ada_done, ADA_FIRST)
            d(dve.tensor_tensor(mod[:, 0:16], bank[4][:, 0:16], cols[:, 0:16], ALU.add), mod_copied)
            d(dve.scalar_tensor_tensor(scale_mix[:], mod[:, 8:16], 1.0, cols[:, R_NMIX:R_NMIX + KD], ALU.add, ALU.mult))
            for k in range(KD):
                dve.wait_ge(x_turned, k + 1)
                d(dve.tensor_scalar(hT[:, k, :], bank[k % 2][:], scale_mix[:, k:k + 1], mod[:, k:k + 1],
                                    ALU.mult, ALU.add), h_ready)
            dve.wait_ge(proj_out, out_ready("xbc_b"))
            d(dve.memset(xbc_raw[:, :, 0:3], 0.0))
            for t in range(6):
                for k in range(CONV_K):
                    w = cols[:, R_CONVW + 6 * k + t:R_CONVW + 6 * k + t + 1]
                    if k == 0:
                        d(dve.tensor_scalar(xbcT[:, t, :], xbc_raw[:, t, 0:T], w, None, ALU.mult))
                    else:
                        d(dve.scalar_tensor_tensor(xbcT[:, t, :], xbc_raw[:, t, k:k + T], w, xbcT[:, t, :], ALU.mult, ALU.add),
                          ssd_conv if k == CONV_K - 1 else None)
            d(dve.tensor_tensor(dt_raw.rearrange("p (i h) -> p i h", h=8), dt_raw.rearrange("p (i h) -> p i h", h=8),
                                over(bc[:, B_DTB:B_DTB + 8], NT), ALU.add))
            d(dve.scalar_tensor_tensor(dt_a, dt_raw, -1.0, dt_raw, ALU.mult, ALU.min), dt_abs)
            dve.wait_ge(dt_exp, 2)
            d(dve.tensor_scalar(dt_e, dt_e, 1.0, None, ALU.add), dt_arg)
            dve.wait_ge(dt_ln, 1)
            d(dve.scalar_tensor_tensor(dt, dt_raw, 0.0, dt_e, ALU.max, ALU.add))
            d(dve.scalar_tensor_tensor(adt.rearrange("p (i h) -> p i h", h=8), dt.rearrange("p (i h) -> p i h", h=8), -1.0,
                                       over(a_neg, NT), ALU.mult, ALU.mult), adt_ready)
            dve.wait_ge(acs_done, 1)
            d(dve.tensor_copy(acs, bank[3][:, 0:64]), acs_ready)
            d(dve.tensor_tensor(dec, acs[:, 32:64], acs[:, 0:32], ALU.subtract), acs_ready)
            dve.wait_ge(acs_exp, 2)
            d(dve.tensor_tensor(dec, dec, dt, ALU.mult))
            heads = lambda ap: ap.rearrange("p (h n) -> p h n", n=64)
            for i in range(NT):
                e = slice(8 * i, 8 * i + 8)
                dve.wait_ge(ssd_score, i + 1)
                if i:
                    dve.wait_ge(ssd_y, i)
                for h in range(SSD_H):
                    d(dve.tensor_scalar(ssd_l[:, h, :], bank[1 + h // 4][:, P * (h % 4):P * (h % 4) + P],
                                        acs[:, 8 * i + h:8 * i + h + 1], 0.0, ALU.subtract, ALU.min),
                      ssd_diff if h == SSD_H - 1 else None)
                for g in range(2):
                    d(dve.tensor_tensor(ssd_cb[:, g, :], bank[5 * g][:, 0:P], upper[:], ALU.mult))
                dve.wait_ge(ssd_tok, i + 1)
                d(dve.tensor_tensor(heads(xs_dt[:, i % 2, :]), heads(xs_tok[:, i, :]), along(dt[:, e], 64), ALU.mult))
                d(dve.tensor_tensor(heads(xs_dec[:, i % 2, :]), heads(xs_tok[:, i, :]), along(dec[:, e], 64), ALU.mult))
                dve.wait_ge(ssd_decay, i + 1)
                for g in range(2):
                    d(dve.tensor_tensor(ssd_l[:, 4 * g:4 * g + 4, :], ssd_l[:, 4 * g:4 * g + 4, :], over(ssd_cb[:, g, :], 4), ALU.mult),
                      ssd_m if g else None)
                dve.wait_ge(ssd_y, i + 1)
                d(dve.tensor_tensor(heads(ssd_yt), heads(xs_tok[:, i, :]), along(bc[:, B_DSK:B_DSK + 8], 64), ALU.mult))
                d(dve.tensor_tensor(ssd_yt, ssd_yt, bank[3][:], ALU.add))
                if i:
                    d(dve.tensor_tensor(heads(ssd_tmp), heads(bank[4][:]), along(eacs[:, e], 64), ALU.mult))
                    d(dve.tensor_tensor(ssd_yt, ssd_yt, ssd_tmp, ALU.add))
                if i < NT - 1:
                    mask = along(two_heads[:, 0:P:64], 256)
                    grp = lambda ap: ap.rearrange("p (g n) -> p g n", g=2)
                    if i == 0:
                        d(dve.tensor_tensor(grp(ssd_r), grp(bank[5][:]), mask, ALU.mult), ssd_state)
                    else:
                        d(dve.tensor_tensor(heads(ssd_r), heads(ssd_r), along(eacs[:, 32 + 8 * i:40 + 8 * i], 64), ALU.mult))
                        d(dve.tensor_tensor(grp(ssd_tmp), grp(bank[5][:]), mask, ALU.mult))
                        d(dve.tensor_tensor(ssd_r, ssd_r, ssd_tmp, ALU.add), ssd_state)
                dve.wait_ge(z_act, 1)
                d(dve.tensor_tensor(ssd_yt, ssd_yt, z_tok[:, i, :], ALU.mult), ssd_gated)
                dve.wait_ge(squared, i + 1)
                d(dve.tensor_scalar(y_var[:, i:i + 1], y_sq[:, i:i + 1], 1.0 / BW, EPS, ALU.mult, ALU.add), var_ready)
                dve.wait_ge(std_ready, i + 2)
                d(dve.reciprocal(y_rstd[:, i:i + 1], y_std[:, i:i + 1]))
                d(dve.tensor_scalar(ssd_yt, ssd_yt, y_rstd[:, i:i + 1], None, ALU.mult), ssd_o)
                dve.wait_ge(ssd_oT, i + 1)
                d(dve.tensor_tensor(branchT[:, 0:KB, P * i:P * i + P], bank[4][:].rearrange("p (j t) -> p j t", j=KB),
                                    along(cols[:, R_SSDN:R_SSDN + KB], P), ALU.mult), ssd_out)
            lam4 = bc[:, B_LAM:B_LAM + 256].rearrange("p (m s n) -> p m s n", m=2, s=2)
            prod = lam_p.rearrange("p (m n) -> p m n", m=2)
            d(dve.tensor_tensor(prod, lam4[:, :, 0, :], lam4[:, :, 1, :], ALU.mult))
            d(dve.tensor_reduce(lam_s, prod, AX_X, ALU.add), exp_arg)
            d(dve.tensor_scalar(sub_w, cols[:, R_SUBLN:R_SUBLN + 1], 1.0 - LAM_INIT, None, ALU.mult))
            dve.wait_ge(exp_out, 1)
            d(dve.tensor_tensor(lam_neg, lam_e[:, 1:2], lam_e[:, 0:1], ALU.subtract))
            d(dve.tensor_scalar(lam_neg, lam_neg, -LAM_INIT, None, ALU.add))

            def df_mask(n):
                i = n // DIFF_H
                dve.wait_ge(df_score, n + 1)
                own = slice(P * i, P * i + P)
                for m in range(2):
                    s, ps, v = df_s[:, n % 2, m, :], bank[2 * (n % 2) + m], 2 * (n % 2) + m
                    d(dve.scalar_tensor_tensor(s[:, own], ps[:, own], 0.125, causal[:], ALU.mult, ALU.add))
                    if i:
                        d(dve.tensor_scalar(s[:, 0:P * i], ps[:, 0:P * i], 0.125, None, ALU.mult))
                    d(dve.tensor_reduce(df_nmax[:, v:v + 1], s[:, 0:P * (i + 1)], AX_X, ALU.max, negate=True), df_masked)

            df_mask(0)
            for n in range(NT * DIFF_H):
                i, h = n // DIFF_H, n % DIFF_H
                if n + 1 < NT * DIFF_H:
                    df_mask(n + 1)
                w, v = P * (i + 1), 2 * (n % 2)
                dve.wait_ge(df_prob, 2 * n + 2)
                if n >= 2:
                    dve.wait_ge(df_turned, n - 1)
                d(dve.reciprocal(df_r[:, v:v + 2], df_den[:, v:v + 2]))
                d(dve.tensor_tensor(df_r[:, v + 1:v + 2], df_r[:, v + 1:v + 2], lam_neg, ALU.mult))
                d(dve.tensor_scalar(df_attn[:, n % 2, 0:w], df_s[:, n % 2, 1, 0:w], df_r[:, v + 1:v + 2], None, ALU.mult))
                d(dve.scalar_tensor_tensor(df_attn[:, n % 2, 0:w], df_s[:, n % 2, 0, 0:w], df_r[:, v:v + 1],
                                           df_attn[:, n % 2, 0:w], ALU.mult, ALU.add), df_mixed)
                if h == DIFF_H - 1:
                    hd = lambda ap: ap.rearrange("p (h n) -> p h n", h=DIFF_H)
                    dve.wait_ge(squared, NT + i + 1)
                    d(dve.tensor_reduce(df_sq, hd(df_tmp), AX_X, ALU.add))
                    d(dve.tensor_scalar(df_var, df_sq, 1.0 / P, EPS, ALU.mult, ALU.add), var_ready)
                    dve.wait_ge(std_ready, 1 + NT + i + 1)
                    d(dve.reciprocal(df_rstd, df_std))
                    d(dve.tensor_tensor(hd(df_o), hd(bank[5][:]), along(df_rstd, P), ALU.mult), df_ready)
                    dve.wait_ge(df_oT, i + 1)
                    d(dve.tensor_scalar(branchT[:, 2 * KB:3 * KB, P * i:P * i + P],
                                        bank[4][:].rearrange("p (j t) -> p j t", j=KB), sub_w, None, ALU.mult), df_out)

            def add_in(items):
                for _, t in items:
                    dve.wait_ge(gate_out, t + 1)
                    dve.wait_ge(merge_done, t + 1)
                    d(dve.tensor_tensor(gate_sb[:, t % 2, :], gate_sb[:, t % 2, :], proj_ps[1][:], ALU.mult), merge_mul)
                    dst = merged[:, t % KD, :]
                    if t < KD:
                        d(dve.tensor_copy(dst, gate_sb[:, t % 2, :]), merge_out)
                    else:
                        d(dve.tensor_tensor(dst, dst, gate_sb[:, t % 2, :], ALU.add), merge_out)

            lbl = cols[:, R_LB:R_LB + KB]
            d(dve.tensor_tensor(lb_e, lbl, lbl, ALU.subtract), exp_arg)
            dve.wait_ge(exp_out, 2)
            d(dve.reciprocal(lb_r, lb_e))
            d(dve.tensor_tensor(lb_r, lb_r, lb_e, ALU.mult))
            d(dve.tensor_tensor(lb, lb_r, lb_r, ALU.subtract))
            d(dve.tensor_scalar(lb_rest, lb, -1.0, 1.0, ALU.mult, ALU.add))
            dve.wait_ge(hg_sig, 1)
            for n in range(NT):
                d(dve.tensor_scalar(hg_k[:, n, :], hg_k[:, n, :], lb_rest[:, n:n + 1], lb[:, n:n + 1], ALU.mult, ALU.add), hg_f)
            add_in(DRAIN["hg"][0][0:1])
            dve.wait_ge(hg_ln, 1)
            d(dve.tensor_scalar(hg_k, hg_k, -1.0, 1.0, ALU.mult, ALU.add))
            for n in range(NT):
                for i in range(NT):
                    s = slice(P * i, P * i + P)
                    d(dve.tensor_tensor_scan(hg_cum[:, n, s], ones[:], hg_log[:, n, s], 0.0, ALU.mult, ALU.add), hg_scan)
            add_in(DRAIN["hg"][0][1:2])
            cum16 = hg_cum.rearrange("p n (i t) -> p (n i) t", t=P)
            as16 = lambda ap: ap.rearrange("p n (i t) -> p (n i) t", t=P)
            d(dve.tensor_tensor(as16(hg_qk[0]), along(cum16[:, :, P - 1], P), cum16, ALU.subtract), hg_kgarg)
            dve.wait_ge(hg_expk, 1)
            d(dve.tensor_tensor(hg_qk[0], hg_qk[0], hg_k, ALU.mult), hg_kg)
            dve.wait_ge(hg_expq, 1)
            dve.wait_ge(hg_silu, 2)
            d(dve.tensor_tensor(hg_qg, hg_qg, hg_q, ALU.mult), hg_qgr)
            add_in(DRAIN["hg"][0][2:])
            dve.wait_ge(hg_zeroed, 1)

            def pick(lv):
                mask = ident[:] if lv == 0 else level_mask[:, lv - 1, :]
                for i in range(NT):
                    for s in range(2):
                        q = 8 * lv + 2 * i + s
                        dve.wait_ge(hg_score, q + 1)
                        d(dve.copy_predicated(hg_attn[:, i, s], over(mask.bitcast(U32), NT),
                                              bank[q % 6][:].rearrange("p (n q) -> p n q", n=NT)), hg_pick)

            for lv in range(1, len(LEVELS) + 1):
                b, buf = LEVELS[lv - 1], hg_qk[(lv - 1) % 2]
                if lv == 1:
                    dve.wait_ge(hg_kturned, NT)
                if lv > 2:
                    dve.wait_ge(hg_score, 8 * (lv - 1))
                halves = lambda ap: ap.rearrange("p n (k s j) -> p (n k) s j", s=2, j=b)
                cum, dst = halves(hg_cum), halves(buf)
                edge = along(cum[:, :, 0, b - 1], b)
                d(dve.tensor_tensor(dst[:, :, 0, :], edge, cum[:, :, 0, :], ALU.subtract))
                d(dve.tensor_tensor(dst[:, :, 1, :], cum[:, :, 1, :], edge, ALU.subtract), hg_dist)
                add_in(DRAIN["hg"][lv])
                pick(lv - 1)
                dve.wait_ge(hg_decay, lv)
                d(dve.tensor_tensor(dst[:, :, 0, :], dst[:, :, 0, :], halves(hg_k)[:, :, 0, :], ALU.mult))
                d(dve.tensor_tensor(dst[:, :, 1, :], dst[:, :, 1, :], halves(hg_q)[:, :, 1, :], ALU.mult), hg_scaled)
            add_in(DRAIN["hg"][len(LEVELS) + 1])
            pick(len(LEVELS))
            for i in range(NT):
                add_in(DRAIN["hg"][len(LEVELS) + 2 + i])
                dve.wait_ge(hg_y, i + 1)
                if i < NT - 1:
                    grp = bank[1][:].rearrange("p (n v) -> p n v", n=NT)
                    if i == 0:
                        d(dve.tensor_tensor(hg_r, grp, over(two_heads[:], NT), ALU.mult), hg_state)
                    else:
                        dve.wait_ge(hg_expl, 1)
                        d(dve.tensor_tensor(hg_r, hg_r, along(hg_last[:, i:16:4], P), ALU.mult))
                        d(dve.tensor_tensor(hg_o.rearrange("p (n v) -> p n v", n=NT), grp, over(two_heads[:], NT), ALU.mult))
                        d(dve.tensor_tensor(hg_r, hg_r, hg_o.rearrange("p (n v) -> p n v", n=NT), ALU.add), hg_state)
                dve.wait_ge(squared, 2 * NT + i + 1)
                d(dve.tensor_reduce(hg_sq, hg_tmp.rearrange("p (h v) -> p h v", v=64), AX_X, ALU.add))
                d(dve.tensor_scalar(hg_var, hg_sq, 1.0 / 64, EPS, ALU.mult, ALU.add), var_ready)
                dve.wait_ge(std_ready, 1 + 2 * NT + i + 1)
                d(dve.reciprocal(hg_rstd, hg_std))
                d(dve.tensor_tensor(heads(hg_o), heads(bank[0][:]), along(hg_rstd, 64), ALU.mult))
                d(dve.tensor_tensor(hg_o, hg_o, hg_g[:, i, :], ALU.mult), hg_ready)
                dve.wait_ge(hg_oT, i + 1)
                d(dve.tensor_scalar(branchT[:, 3 * KB:4 * KB, P * i:P * i + P], bank[2][:].rearrange("p (j t) -> p j t", j=KB),
                                    cols[:, R_HGN:R_HGN + 1], None, ALU.mult), hg_out)
            d(dve.tensor_tensor(causal_4th[:], causal_4th[:], causal[:], ALU.min))

            scale = DIL_D ** -0.5
            for n, (g, j, b0, tiles, prev) in enumerate(DIL_SCORES):
                dve.wait_ge(dl_score, n + 1)
                c_ = len(tiles)
                mask = (band_prev if prev else (causal, causal, causal_4th)[g])[:]
                dst = dl_p[:, j, b0:b0 + c_, :]
                own, before = dl_stat[g][:, :, j], dl_prev[:, 1:NT, j]
                d(dve.scalar_tensor_tensor(dst, bank[n % 4][:, 0:P * c_].rearrange("p (a k) -> p a k", k=P), scale,
                                           over(mask, c_), ALU.mult, ALU.add))
                d(dve.tensor_reduce(before if prev else own, dst, AX_X, ALU.max, negate=True),
                  None if prev else dl_masked)
                if prev:
                    d(dve.tensor_tensor(own[:, 1:NT], own[:, 1:NT], before, ALU.min), dl_masked)
            add_in(DRAIN["dil"][0][0:1])
            dve.wait_ge(dl_prob, len(DIL_SCORES))
            d(dve.tensor_tensor(dl_stat[0][:, 1:NT, 4:8], dl_stat[0][:, 1:NT, 4:8], dl_prev[:, 1:NT, 4:8], ALU.add))
            dve.wait_ge(dl_back, 32)
            nat = [dl_stat[0], dl_nat[0], dl_nat[1]]
            d(dve.tensor_tensor(dl_low, nat[0][:, :, 0:4], nat[1][:, :, 0:4], ALU.min))
            d(dve.tensor_tensor(dl_low, dl_low, nat[2][:, :, 0:4], ALU.min))
            for g in range(3):
                d(dve.tensor_tensor(dl_w[g], dl_low, nat[g][:, :, 0:4], ALU.subtract), dl_warg)
            dve.wait_ge(dl_wexp, 3)
            d(dve.tensor_tensor(dl_z, dl_w[0], nat[0][:, :, 4:8], ALU.mult))
            for g in (1, 2):
                d(dve.tensor_tensor(dl_t, dl_w[g], nat[g][:, :, 4:8], ALU.mult))
                d(dve.tensor_tensor(dl_z, dl_z, dl_t, ALU.add))
            d(dve.reciprocal(dl_z, dl_z))
            for g in range(3):
                d(dve.tensor_tensor(dl_w[g], dl_w[g], dl_z, ALU.mult), dl_weighed)
            add_in(DRAIN["dil"][0][1:])
            dve.wait_ge(dl_back, 64)
            for j in range(DIL_H):
                for b0, n, w in ((0, 4, dl_w[0][:, :, j]), (4, 3, dl_w[0][:, 1:NT, j]), (7, 4, dl_wg[0][:, :, j]),
                                 (11, 4, dl_wg[1][:, :, j])):
                    d(dve.tensor_tensor(dl_p[:, j, b0:b0 + n, :], dl_p[:, j, b0:b0 + n, :], along(w, P), ALU.mult), dl_scaled)
            for j in range(DIL_H):
                add_in(DRAIN["dil"][1 + j])
                dve.wait_ge(dl_y, j + 1)
                d(dve.tensor_copy(branchT[:, KB + j, :], bank[4 + j % 2][:]), dl_out)
            dve.wait_ge(proj_out, out_ready(f"ada{ADA - 1}"))
            d(dve.tensor_tensor(mod[:, 16:48], mod[:, 16:48], cols[:, 16:48], ALU.add), mod_copied)
            d(dve.scalar_tensor_tensor(scale_ffn[:], mod[:, 32:40], 1.0, cols[:, R_NFFN:R_NFFN + KD], ALU.add, ALU.mult), scale2_ready)
            add_in(DRAIN["dil"][-1] + merges[3 * KD:])
            dve.wait_ge(x2_loaded, 16)
            dve.wait_ge(row_ready, 10)
            def out_tile(o):
                i, half = OUT_ORDER[o]
                s = slice(512 * half, 512 * half + 512)
                dve.wait_ge(o_done, o + 1)
                tmp = gate_sb[:, o % 2, :]
                d(dve.tensor_tensor(tmp, bank[4 + o % 2][:], bc_gate1[:, s], ALU.mult))
                d(dve.tensor_tensor(x2[:, i, s], x2[:, i, s], tmp, ALU.add), o_out)

            def norm_tile(i):
                v = slice(i, i + 1)
                dve.wait_ge(squared, 3 * NT + i + 1)
                d(dve.tensor_scalar(f_var[:, v], f_sq[:, v], 1.0 / D, EPS, ALU.mult, ALU.add), var_ready)
                dve.wait_ge(std_ready, 1 + 3 * NT + i + 1)
                d(dve.reciprocal(f_rstd[:, v], f_std[:, v]))
                d(dve.scalar_tensor_tensor(h2[:, i, :], x2[:, i, :], f_rstd[:, v], bc_scale2, ALU.mult, ALU.mult))
                d(dve.tensor_tensor(h2[:, i, :], h2[:, i, :], bc_shift2, ALU.add), h2_ready)

            for o, (i, half) in enumerate(OUT_ORDER):
                out_tile(o)
                if half and i:
                    norm_tile(i - 1)
            norm_tile(NT - 1)
            for k in range(KD):
                dve.wait_ge(h2_turned, k + 1)
                d(dve.tensor_copy(h2T[:, k, :], bank[k % 2][:]), h2T_ready)

            dve.wait_ge(scored, 1)
            d(dve.tensor_tensor(sel, scores, over(bc[:, B_RB:B_RB + N_EXP], NT), ALU.add))
            for i in range(NT):
                for g in range(GROUPS):
                    d(dve.max(best8[:, GROUPS * i + g, :], sel[:, i, 8 * g:8 * g + 8]))
            best = best8[:].rearrange("p (i g) m -> p i g m", i=NT)
            d(dve.tensor_tensor(grp_score, best[:, :, :, 0], best[:, :, :, 1], ALU.add))
            for i in range(NT):
                d(dve.max(top8[:, i, :], grp_score[:, i, :]))
                d(dve.max_index(top_i[:, i, :], top8[:, i, :], grp_score[:, i, :]))
            d(dve.tensor_copy(top_f[:], top_i[:]))
            d(dve.tensor_tensor(grp_pen, over(iota_grp[:], NT), along(top_f[:, :, 0], GROUPS), ALU.not_equal))
            d(dve.tensor_scalar(grp_pen, grp_pen, NEG, None, ALU.mult))
            for i in range(NT):
                d(dve.tensor_tensor(sel[:, i, :].rearrange("p (g e) -> p g e", g=GROUPS), sel[:, i, :].rearrange("p (g e) -> p g e", g=GROUPS),
                                    along(grp_pen[:, i, :], 8), ALU.add))
                d(dve.max(top8[:, i, :], sel[:, i, :]))
                d(dve.max_index(top_i[:, i, :], top8[:, i, :], sel[:, i, :]))
            d(dve.tensor_copy(top_f[:], top_i[:]))
            for s in range(2):
                d(dve.tensor_tensor(hot[s], over(iota_exp[:], NT), along(top_f[:, :, s], N_EXP), ALU.is_equal))
                d(dve.tensor_tensor(picked[:], hot[s], scores, ALU.mult))
                d(dve.tensor_reduce(pair_s[:, :, s], picked[:], AX_X, ALU.add))
            d(dve.tensor_tensor(both_hot[:], hot[0], hot[1], ALU.add))
            d(dve.tensor_reduce(pair_z, pair_s, AX_X, ALU.add), hot_ready)
            d(dve.reciprocal(pair_z, pair_z), hot_ready)
            d(dve.tensor_tensor(pair_s, pair_s, along(pair_z, 2), ALU.mult), hot_ready)
            d(dve.memset(endc[:], 0.0), hot_ready)
            dve.wait_ge(ranked, 1)
            for dst, cnt in ((nbc[:, 0:1], bank[5][0:N_EXP, 0:1]), (n_blk_e[:], bank[4][:, 0:N_EXP])):
                d(dve.tensor_scalar(dst, cnt, 0.0, None, ALU.is_gt))
                for j in range(1, T // BLK):
                    d(dve.scalar_tensor_tensor(dst, cnt, float(BLK * j), dst, ALU.is_gt, ALU.add),
                      nbc_ready if j == T // BLK - 1 else None)
            d(dve.tensor_tensor_scan(blk_end[:], ones[:, 0:N_EXP], n_blk_e[:], 0.0, ALU.mult, ALU.add))
            d(dve.tensor_copy(n_blocks[:], blk_end[0:1, N_EXP - 1:N_EXP]), plan_ready)
            d(dve.tensor_tensor(n_blk_e[:], blk_end[:], n_blk_e[:], ALU.subtract))
            d(dve.scalar_tensor_tensor(rank[:], over(n_blk_e[:], NT), float(BLK), bank[3][:, 0:NT * N_EXP].rearrange("p (i e) -> p i e", i=NT),
                                       ALU.mult, ALU.add))
            for s in range(2):
                d(dve.tensor_tensor(picked[:], hot[s], rank[:], ALU.mult))
                d(dve.tensor_reduce(pair_row[:, :, s], picked[:], AX_X, ALU.add))
            d(dve.tensor_copy(row_in[:], pair_row))
            d(dve.tensor_scalar(row_id[:], row_in[:], BLK.bit_length() - 1, None, ALU.logical_shift_right))
            d(dve.tensor_scalar(row_in[:], row_in[:], BLK - 1, None, ALU.bitwise_and))
            d(dve.scalar_tensor_tensor(row_id[:], row_in[:], float(LIST_BLK), row_id[:], ALU.mult, ALU.add), rows_ready)
            dve.wait_ge(ends_done, 1)
            d(dve.tensor_copy(endc[:], bank[5][0:N_EXP, 0:1]))
            d(dve.tensor_scalar(ended, iota_blk[:], endc[:, 0:1], None, ALU.is_ge), ended_ready)
            dve.wait_ge(owners_done, 1)
            d(dve.tensor_scalar(blk_exp[:], bank[4][0:1, 0:N_BLK], float(N_EXP - 1), None, ALU.min), plan_ready)

            n_valid = dve.value_load(n_blocks[0:1, 0:1], min_val=MIN_BLOCKS, max_val=MAX_BLOCKS)

            def expert_dve(b, s, first):
                dve.wait_ge(gu_act, b + 1)
                dve.tensor_tensor(e_hid, e_act, bank[2 + s % 2][:, 2 * BLK:4 * BLK].rearrange("p (j t) -> p j t", j=2), ALU.mult)\
                   .then_inc(hid_ready, 1)
                dve.wait_ge(down_done, b + 1)
                if not first:
                    dve.wait_ge(y_stored[s], 8 * (b - s))
                dve.tensor_copy(yb[s][0:BLK, 512:1024], proj_ps[0][0:BLK, :]).then_inc(y_dve, 1)

            for s in range(2):
                expert_dve(s, s, True)
            with dve.Fori(1, N_BLK // 2) as it:
                for s in range(2):
                    b = 2 * it + s
                    with dve.If(b < n_valid):
                        expert_dve(b, s, False)
            def last_norm(i):
                v = slice(NT + i, NT + i + 1)
                dve.wait_ge(squared, 4 * NT + i + 1)
                d(dve.tensor_scalar(f_var[:, v], f_sq[:, v], 1.0 / D, EPS, ALU.mult, ALU.add), var_ready)
                dve.wait_ge(std_ready, 1 + 4 * NT + i + 1)
                d(dve.reciprocal(f_rstd[:, v], f_std[:, v]))
                d(dve.scalar_tensor_tensor(out_ring[i], x2[:, i, :], f_rstd[:, v], bc_final, ALU.mult, ALU.mult), out_ready_)

            for i in range(NT):
                a, b = yg[2 * (i % 2)], yg[2 * (i % 2) + 1]
                dve.wait_ge(y_weighed, i + 1)
                d(dve.scalar_tensor_tensor(a, b, pair_s[:, i, 1:2], a, ALU.mult, ALU.add))
                d(dve.tensor_tensor(a, a, bc_gate2, ALU.mult))
                d(dve.tensor_tensor(x2[:, i, :], x2[:, i, :], a, ALU.add), x3_ready)
                if i:
                    last_norm(i - 1)
            last_norm(NT - 1)


_INS = ["x", "c", "w_ada", "b_ada", "norm_mix_w", "norm_ffn_w", "w_in", "conv_w", "conv_b", "ssd_dt_bias",
        "ssd_a_log", "ssd_d", "ssd_norm_w", "diff_lambda", "diff_subln_w", "hgrn_lb_logits", "hgrn_norm_w",
        "w_merge", "w_out", "w_router", "router_bias", "w_expert_gate", "w_expert_up", "w_expert_down",
        "final_norm_w"]


def kernel(**inputs):
    import numpy as np
    import concourse.bacc as bacc
    from concourse.bass_utils import run_bass_kernel_spmd

    nc = bacc.Bacc("TRN2", target_bir_lowering=False, num_devices=1)
    arrays, args = {}, []
    for name in _INS:
        a = np.ascontiguousarray(inputs[name])
        arrays[f"in_{name}"] = a
        args.append(nc.dram_tensor(f"in_{name}", a.shape, mybir.dt.from_np(a.dtype), kind="ExternalInput").ap())
    for name, shape, dt in (("row_list", (LIST, 2), U32), ("h2_rows", (T, D), F32),
                            ("y_rows", (2 * T, D), F32), ("dil_stats", (2, T, 8), F32),
                            ("dil_weights", (2, T, 4), F32)):
        args.append(nc.dram_tensor(name, shape, dt, kind="Internal").ap())
    args.append(nc.dram_tensor("out", (1, T, D), F32, kind="ExternalOutput").ap())
    build(nc, *args)
    r = run_bass_kernel_spmd(nc, [arrays], core_ids=[0])
    return r.results[0]["out"]
```

```python
from contextlib import ExitStack

import concourse.bass as bass
from concourse import mybir

F32 = mybir.dt.float32
U32 = mybir.dt.uint32
ALU = mybir.AluOpType
ACT = mybir.ActivationFunctionType
AX_X = mybir.AxisListType.X

P = 128
T = 512
NT = T // P
D = 1024
KD = D // P
BW = 512
KB = BW // P
EPS = 1e-6
NEG = -1e30
SSD_H, SSD_P = 8, 64
CONV_CH, CONV_K = 768, 4
DIL_H, DIL_D = 4, 128
DIL_BLOCKS = 15
DIFF_H = 4
HG_H = 8
LEVELS = [1, 2, 4, 8, 16, 32, 64]
LAM_INIT = 0.8 - 0.6
N_EXP, GROUPS, F_EXP = 64, 8, 256
BLK = 96
MAX_BLOCKS = N_EXP + (2 * T - N_EXP) // BLK
E_SLOTS = 4
N_BLK = -(-MAX_BLOCKS // E_SLOTS) * E_SLOTS
MIN_BLOCKS = -(-2 * T // BLK)
AHEAD = 4
LIST_BLK = N_BLK + AHEAD

C_Z, C_XBC, C_DT = 0, 512, 1280
C_QB, C_KB, C_VB = 1288, 2824, 4360
C_QC, C_KC, C_VC = 5896, 6408, 6920
C_QD, C_FD, C_ID, C_GD = 7432, 7944, 8456, 8968
C_GATE = 9480

R_BADA, R_NMIX, R_NFFN, R_FIN, R_CONVB, R_CONVW, R_SSDN, R_SUBLN, R_HGN, R_LB = 0, 48, 56, 64, 72, 78, 102, 106, 107, 108
N_ROWS = 112
B_DTB, B_ALOG, B_DSK, B_LAM, B_RB = 0, 8, 16, 24, 280
N_BC = 344

ARENA = 27136
PLACES = {"open": (0, 11264), "merge": (0, 5120), "ssd": (0, 11264), "ssd_more": (17408, ARENA), "diff": (11264, 22528),
          "hg_in": (5120, 11264), "hg": (11264, ARENA), "dil": (5120, ARENA), "late": (5120, ARENA)}


class Order:

    def __init__(self, eng, own):
        self.eng, self.own, self.count = eng, own, {}

    def __call__(self, ins, sem=None):
        sem = self.own if sem is None else sem
        ins.then_inc(sem, 1)
        self.count[sem.name] = self.count.get(sem.name, 0) + 1
        self.eng.wait_ge(sem, self.count[sem.name])

    def free(self, ins, sem=None):
        sem = self.own if sem is None else sem
        ins.then_inc(sem, 1)
        self.count[sem.name] = self.count.get(sem.name, 0) + 1


def tokens_of(view, g, a):
    return view[:, P * a:P * a + P] if g == 0 else view.rearrange("p (i r) -> p r i", r=4)[:, a, :]


def build(nc, x, c, w_ada, b_ada, norm_mix_w, norm_ffn_w, w_in, conv_w, conv_b, ssd_dt_bias, ssd_a_log,
          ssd_d, ssd_norm_w, diff_lambda, diff_subln_w, hgrn_lb_logits, hgrn_norm_w, w_merge, w_out,
          w_router, router_bias, w_expert_gate, w_expert_up, w_expert_down, final_norm_w,
          h2_dram, y_dram, stat_dram, weight_dram, out):
    x_dram = x.rearrange("a (i p) d -> p (a i) d", p=P)
    out_dram = out.rearrange("a (i p) d -> p (a i) d", p=P)
    ada_dram = w_ada[0].rearrange("(p k) n -> p k n", p=P)
    in_dram = w_in[0].rearrange("(k p) n -> p k n", p=P)

    with ExitStack() as ctx:
        def sb(name, shape, dt=F32):
            return ctx.enter_context(nc.sbuf_tensor(name, shape, dt))

        def sem(name):
            return ctx.enter_context(nc.semaphore(name))

        proj_ps = [ctx.enter_context(nc.psum_tensor(f"proj_ps{i}", [P, 512], F32)) for i in range(2)]
        bank = [ctx.enter_context(nc.psum_tensor(f"bank{i}", [P, 512], F32)) for i in range(6)]

        MOD_BANK = (bank[4], proj_ps[1])
        X_BANK = [bank[0], bank[1], bank[2], bank[3], bank[5], proj_ps[0], bank[0], bank[1]]

        ident = sb("ident", [P, P])
        ones = sb("ones", [P, P])
        upper = sb("upper", [P, P])
        upper_strict = sb("upper_strict", [P, P])
        causal = sb("causal", [P, P])
        band_prev = sb("band_prev", [P, P])
        apart = sb("apart", [P, P], U32)
        causal_4th = sb("causal_4th", [P, P])
        level_mask = sb("level_mask", [P, len(LEVELS), P])
        two_heads = sb("two_heads", [P, P])
        iota_exp = sb("iota_exp", [P, N_EXP])
        iota_grp = sb("iota_grp", [P, GROUPS])
        iota_blk = sb("iota_blk", [P, LIST_BLK])
        iota_row = sb("iota_row", [P, BLK])
        entry = sb("entry", [P, 2, 2, NT])
        rows = sb("rows", [N_ROWS, P])
        cols = sb("cols", [P, N_ROWS])
        bc_row = sb("bc_row", [1, N_BC])
        bc = sb("bc", [P, N_BC])
        mod = sb("mod", [P, 48])
        c_raw = sb("c_raw", [P, KD])
        c_act = sb("c_act", [P, KD])
        scale_mix = sb("scale_mix", [P, KD])
        ada_acc = [sb(f"ada_acc{i}", [P, 512]) for i in range(2)]
        scale_ffn = sb("scale_ffn", [P, KD])
        hT = sb("hT", [P, KD, T])
        branchT = sb("branchT", [P, 4 * KB, T])
        w_ring = [sb(f"w_ring{i}", [P, KD * 512]) for i in range(2)]
        small = sb("small", [P, 1024])
        arena = sb("arena", [P, ARENA])
        taken = {who: at for who, (at, _) in PLACES.items()}

        def place(who, n):
            at = taken[who]
            taken[who] = at + n
            assert taken[who] <= PLACES[who][1], (who, taken[who])
            return arena[:, at:at + n]

        w_slot = [w[:].rearrange("p (k n) -> p k n", k=KD) for w in w_ring]

        dve_order, act_order, pool_order = sem("dve_order"), sem("act_order"), sem("pool_order")
        consts_ready, apart_ready = sem("consts_ready"), sem("apart_ready")
        x_loaded, vec_loaded = sem("x_loaded"), sem("vec_loaded")
        w_loaded = [sem(f"w_loaded{i}") for i in range(2)]
        w_used, ada_done, ada_summed, scale1_ready = sem("w_used"), sem("ada_done"), sem("ada_summed"), sem("scale1_ready")
        ada_loaded = [sem(f"ada_loaded{i}") for i in range(2)]
        cols_turned, bc_spread = sem("cols_turned"), sem("bc_spread")
        c_ready = sem("c_ready")
        mod_copied = sem("mod_copied")
        xn_ready = sem("xn_ready")
        x_turned, h_ready = sem("x_turned"), sem("h_ready")
        proj_done, proj_out = sem("proj_done"), sem("proj_out")
        ssd_conv, ssd_act = sem("ssd_conv"), sem("ssd_act")
        ssd_turned, ssd_tok = sem("ssd_turned"), sem("ssd_tok")
        dt_abs, dt_exp, dt_arg, dt_ln = sem("dt_abs"), sem("dt_exp"), sem("dt_arg"), sem("dt_ln")
        adt_ready, acs_done, acs_ready = sem("adt_ready"), sem("acs_done"), sem("acs_ready")
        acs_exp = sem("acs_exp")
        ssd_score, ssd_diff, ssd_decay, ssd_m = sem("ssd_score"), sem("ssd_diff"), sem("ssd_decay"), sem("ssd_m")
        ssd_y, ssd_state, ssd_gated, squared = sem("ssd_y"), sem("ssd_state"), sem("ssd_gated"), sem("squared")
        z_act, var_ready, std_ready = sem("z_act"), sem("var_ready"), sem("std_ready")
        ssd_o, ssd_oT, ssd_out = sem("ssd_o"), sem("ssd_oT"), sem("ssd_out")

        ADA_FIRST, ADA = 4, 12
        ADA_HEAD = [0, 2, 1, 3]
        x_tok = place("open", NT * D).rearrange("p (i d) -> p i d", i=NT)
        x_nrm = place("open", NT * D).rearrange("p (i d) -> p i d", i=NT)
        junk = place("open", D)
        ada_slot = [w_slot[0], w_slot[1]] + [branchT[:].rearrange("p c t -> p (c t)")[:, KD * 512 * i:KD * 512 * (i + 1)]
                                             .rearrange("p (k n) -> p k n", k=KD) for i in range(2)]
        ada_first = [place("open", 512) for _ in range(ADA_FIRST)]
        at = [0]

        def sm(n):
            at[0] += n
            assert at[0] <= 1024
            return small[:, at[0] - n:at[0]]

        x_sq, x_var, x_std, x_rstd = sm(NT), sm(NT), sm(NT), sm(NT)

        def over(ap, n):
            return ap.unsqueeze(1).to_broadcast([ap.shape[0], n, ap.shape[1]])

        def along(ap, n):
            return ap.unsqueeze(2).to_broadcast([ap.shape[0], ap.shape[1], n])

        PROJ = [("z", C_Z, 512, 4), ("xbc_a", C_XBC, 512, 4), ("xbc_b", C_XBC + 512, 264, 3),
                ("q_c", C_QC, 512, 4), ("ada4", 512 * 4, 512, 1), ("k_c", C_KC, 512, 4), ("ada5", 512 * 5, 512, 1),
                ("v_c", C_VC, 512, 4), ("ada6", 512 * 6, 512, 1), ("g_d", C_GD, 512, 4), ("ada7", 512 * 7, 512, 1),
                ("q_d", C_QD, 512, 4), ("ada8", 512 * 8, 512, 1), ("f_d", C_FD, 512, 4), ("ada9", 512 * 9, 512, 1),
                ("i_d", C_ID, 512, 4), ("ada10", 512 * 10, 512, 1), ("ada11", 512 * 11, 512, 1)]
        N_BEFORE = len(PROJ)
        for g in range(3):
            PROJ += [(f"q_b{g}", C_QB + 512 * g, 512, 4), (f"k_b{g}", C_KB + 512 * g, 512, 4),
                     (f"v_b{g}", C_VB + 512 * g, 512, 4)]
        first_out = {name: sum(o for _, _, _, o in PROJ[:i]) for i, (name, _, _, _) in enumerate(PROJ)}
        outs_of = {name: o for name, _, _, o in PROJ}
        MERGE_ORDER = [0, 2, 3, 1]
        MERGE_UNITS = 4 * KD // 2
        UNITS = ["ada0", "ada1"] + [p[0] for p in PROJ[:N_BEFORE]]
        UNITS.remove(f"ada{ADA - 1}")
        UNITS += [f"merge{u}" for u in range(MERGE_UNITS // 2)] + [p[0] for p in PROJ[N_BEFORE:]]
        UNITS += [f"merge{u}" for u in range(MERGE_UNITS // 2, MERGE_UNITS)] + ["out0", "out1"]
        unit_of = {name: n for n, name in enumerate(UNITS)}

        def in_slot(name):
            n = unit_of[name]
            return 16 * sum(2 if u.startswith("merge") else 1 for u in UNITS[n % 2:n + 1:2])

        def out_ready(name):
            return first_out[name] + outs_of[name]

        def outputs(*names):
            return [(name, m) for name in names for m in range(outs_of[name])]

        merges = [("merge", t) for t in range(4 * KD)]
        work = outputs(*(p[0] for p in PROJ[3:N_BEFORE]))
        FILL = {"ssd": [work[a:b] for a, b in ((0, 4), (4, 6), (6, 8), (8, 10), (10, 12), (12, 14), (14, 16), (16, 18), (18, 19), (19, 20))],
                "diff": [[w] for w in work[20:]],
                "hg": [merges[0:5]] + [merges[t:t + 1] for t in range(5, 16)],
                "dil": [merges[16:20]] + [merges[t:t + 1] for t in range(20, 24)]}

        def drained(points):
            taken_out, under_way = [], []
            for items in points:
                under_way = under_way + items
                taken_out.append(under_way[:-1])
                under_way = under_way[-1:]
            return taken_out + [under_way]

        DRAIN = {who: drained(points) for who, points in FILL.items()}

        xbc_raw = place("ssd", 6 * (T + 3)).rearrange("p (c t) -> p c t", c=6)
        xbcT = place("ssd", 6 * T).rearrange("p (c t) -> p c t", c=6)
        z_tok = place("ssd", NT * BW).rearrange("p (i n) -> p i n", i=NT)
        xs_tok = place("ssd", NT * BW).rearrange("p (i n) -> p i n", i=NT)
        xs_dt = place("ssd_more", 2 * BW).rearrange("p (i n) -> p i n", i=2)
        xs_dec = place("ssd_more", 2 * BW).rearrange("p (i n) -> p i n", i=2)
        b_tok = place("ssd_more", NT * P).rearrange("p (i n) -> p i n", i=NT)
        ssd_l = place("ssd_more", SSD_H * P).rearrange("p (h l) -> p h l", h=SSD_H)
        ssd_cb = place("ssd_more", 2 * P).rearrange("p (g l) -> p g l", g=2)
        ssd_r = place("ssd_more", BW)
        ssd_tmp = place("ssd_more", BW)
        ssd_yt = place("ssd_more", BW)
        dt_raw, dt_a, dt_e, dt, adt = sm(32), sm(32), sm(32), sm(32), sm(32)
        a_neg = sm(8)
        acs, eacs, dec = sm(64), sm(64), sm(32)
        y_sq, y_var, y_std, y_rstd = sm(NT), sm(NT), sm(NT), sm(NT)

        def hg_tiles(who="hg"):
            return place(who, NT * T).rearrange("p (n t) -> p n t", n=NT)

        hg_q, hg_k, hg_v = (hg_tiles("hg_in") for _ in range(3))
        hg_g = branchT[:, KB:2 * KB, :]
        hg_log, hg_cum = (hg_tiles() for _ in range(2))
        hg_qk = [hg_tiles() for _ in range(2)]
        hg_ktok = hg_tiles()
        hg_qg = hg_log
        hg_attn = place("hg", NT * 2 * NT * P).rearrange("p (i s n q) -> p i s n q", i=NT, s=2, n=NT)
        hg_r = place("hg", BW).rearrange("p (n v) -> p n v", n=NT)
        hg_tmp, hg_o = place("hg", BW), place("hg", BW)
        lb_e, lb_r, lb, lb_rest = sm(4), sm(4), sm(4), sm(4)
        hg_last = sm(16)
        hg_sq, hg_var, hg_std, hg_rstd = sm(8), sm(8), sm(8), sm(8)
        exp_arg, exp_out = sem("exp_arg"), sem("exp_out")
        hg_sig, hg_f, hg_ln, hg_scan = sem("hg_sig"), sem("hg_f"), sem("hg_ln"), sem("hg_scan")
        hg_silu, hg_expq, hg_expk, hg_expl = sem("hg_silu"), sem("hg_expq"), sem("hg_expk"), sem("hg_expl")
        hg_kgarg, hg_kg, hg_qgr = sem("hg_kgarg"), sem("hg_kg"), sem("hg_qgr")
        hg_kturned, hg_kcopied, hg_zeroed = sem("hg_kturned"), sem("hg_kcopied"), sem("hg_zeroed")
        hg_dist, hg_decay, hg_scaled = sem("hg_dist"), sem("hg_decay"), sem("hg_scaled")
        hg_score, hg_pick, hg_y, hg_state = sem("hg_score"), sem("hg_pick"), sem("hg_y"), sem("hg_state")
        hg_ready, hg_oT, hg_out = sem("hg_ready"), sem("hg_oT"), sem("hg_out")

        df_q, df_k, df_v = (place("diff", NT * T).rearrange("p (n t) -> p n t", n=NT) for _ in range(3))
        df_s = place("diff", 4 * T).rearrange("p (b m t) -> p b m t", b=2, m=2)
        df_attn = place("diff", 2 * T).rearrange("p (b t) -> p b t", b=2)
        df_attnT = place("diff", 2 * T).rearrange("p (b t) -> p b t", b=2)
        df_tmp, df_o = place("diff", BW), place("diff", BW)
        lam_p, lam_s, lam_e, lam_neg, sub_w = sm(128), sm(2), sm(2), sm(1), sm(1)
        df_nmax, df_den, df_r = sm(4), sm(4), sm(4)
        df_sq, df_var, df_std, df_rstd = sm(4), sm(4), sm(4), sm(4)
        df_score, df_masked, df_prob, df_mixed = sem("df_score"), sem("df_masked"), sem("df_prob"), sem("df_mixed")
        df_turned, df_copied, df_y = sem("df_turned"), sem("df_copied"), sem("df_y")
        df_ready, df_oT, df_out = sem("df_ready"), sem("df_oT"), sem("df_out")

        dl_q, dl_k = (place("dil", NT * T).rearrange("p (n t) -> p n t", n=NT) for _ in range(2))
        dl_v = [place("dil", NT * BW).rearrange("p (i n) -> p i n", i=NT) for _ in range(3)]
        dl_p = place("dil", DIL_H * DIL_BLOCKS * P).rearrange("p (j b k) -> p j b k", j=DIL_H, b=DIL_BLOCKS)
        dl_pT = place("dil", DIL_BLOCKS * P).rearrange("p (b k) -> p b k", b=DIL_BLOCKS)
        dl_stat = [sm(32).rearrange("p (a v) -> p a v", v=8) for _ in range(3)]
        dl_prev = sm(32).rearrange("p (a v) -> p a v", v=8)
        dl_nat = [sm(32).rearrange("p (a v) -> p a v", v=8) for _ in range(2)]
        dl_w = [sm(16).rearrange("p (a j) -> p a j", j=4) for _ in range(3)]
        dl_wg = [sm(16).rearrange("p (a j) -> p a j", j=4) for _ in range(2)]
        dl_low, dl_z, dl_t = (sm(16).rearrange("p (a j) -> p a j", j=4) for _ in range(3))
        dl_score, dl_masked, dl_prob = sem("dl_score"), sem("dl_masked"), sem("dl_prob")
        dl_stored, dl_back = sem("dl_stored"), sem("dl_back")
        dl_warg, dl_wexp, dl_weighed, dl_scaled = sem("dl_warg"), sem("dl_wexp"), sem("dl_weighed"), sem("dl_scaled")
        dl_turned, dl_copied, dl_y, dl_out = sem("dl_turned"), sem("dl_copied"), sem("dl_y"), sem("dl_out")
        DIL_SCORES = []
        for g in range(3):
            for j in range(DIL_H):
                DIL_SCORES.append((g, j, (0, 7, 11)[g], range(NT), False))
                if g == 0:
                    DIL_SCORES.append((g, j, 4, range(1, NT), True))

        gate_sb = place("merge", 2 * T).rearrange("p (b t) -> p b t", b=2)
        merged = place("merge", KD * T).rearrange("p (k t) -> p k t", k=KD)
        down_place = [place("late", 2 * D) for _ in range(2)]
        x2 = place("late", NT * D).rearrange("p (i d) -> p i d", i=NT)
        bc_gate1, bc_scale2, bc_shift2, bc_gate2, bc_final = (place("late", D) for _ in range(5))
        xg = [merged[:, 2 * s:2 * s + 2, :].rearrange("p k t -> p (k t)") for s in range(AHEAD)]
        xgT = [place("late", KD * BLK).rearrange("p (k t) -> p k t", k=KD) for _ in range(2)]
        e_act, e_hid = (place("late", 2 * BLK).rearrange("p (j t) -> p j t", j=2) for _ in range(2))
        yb = [place("late", D) for _ in range(2)]
        h2T = hT
        old_branches = branchT[:].rearrange("p c t -> p (c t)")
        h2 = old_branches[:, 0:NT * D].rearrange("p (i d) -> p i d", i=NT)
        w_wide = [w_ring[0][:], w_ring[1][:], hT[:].rearrange("p k t -> p (k t)"), old_branches[:, 0:2 * KD * F_EXP]]
        w_wide = [w.rearrange("p (g k f) -> p g k f", g=2, k=KD) for w in w_wide]
        w_down = down_place + [old_branches[:, KD * 512 + 2 * D * i:KD * 512 + 2 * D * i + 2 * D] for i in range(2)]
        w_down = [w.rearrange("p (j d) -> p j d", j=2) for w in w_down]
        scores = gate_sb[:, 0, 0:256].rearrange("p (i e) -> p i e", i=NT)
        sel = gate_sb[:, 0, 256:512].rearrange("p (i e) -> p i e", i=NT)
        hot = [gate_sb[:, 1, 256 * s:256 * s + 256].rearrange("p (i e) -> p i e", i=NT) for s in range(2)]
        both_hot = place("late", NT * N_EXP).rearrange("p (i e) -> p i e", i=NT)
        rank = place("late", NT * N_EXP).rearrange("p (i e) -> p i e", i=NT)
        hot_sum = place("late", NT * N_EXP).rearrange("p (i e) -> p i e", i=NT)
        picked = place("late", NT * N_EXP).rearrange("p (i e) -> p i e", i=NT)
        best8 = place("late", NT * GROUPS * 8).rearrange("p (i m) -> p i m", m=8)
        grp_score = sm(32).rearrange("p (i g) -> p i g", i=NT)
        grp_pen = sm(32).rearrange("p (i g) -> p i g", i=NT)
        top8 = place("late", NT * 8).rearrange("p (i e) -> p i e", i=NT)
        top_i = sb("top_i", [P, NT, 8], U32)
        top_f = place("late", NT * 8).rearrange("p (i e) -> p i e", i=NT)
        n_blk_e, blk_end = place("late", N_EXP), place("late", N_EXP)
        pair_s = sm(8).rearrange("p (i s) -> p i s", i=NT)
        pair_z = sm(4)
        nbc, endc = sb("nbc", [N_EXP, 2]), sb("endc", [N_EXP, 1])
        ended = place("late", N_BLK)[0:N_EXP]
        blk_exp = place("late", N_BLK)[0:1].bitcast(U32)
        n_blocks = sb("n_blocks", [1, 1], U32)
        blk_list = place("late", 2 * LIST_BLK)[0:BLK].bitcast(U32)
        in_row = xgT[1].rearrange("p k t -> p (k t)").rearrange("p (s i r) -> p s i r", s=2, i=NT)
        in_blk = place("late", 2 * NT * LIST_BLK).rearrange("p (s i b) -> p s i b", s=2, i=NT)
        list_term = place("late", 2 * NT * 2 * LIST_BLK).rearrange("p (s i v b) -> p s i v b", s=2, i=NT, v=2)
        blk_tok = [sb(f"blk_tok{i}", [BLK, 1], U32) for i in range(AHEAD)]
        blk_dst = [sb(f"blk_dst{i}", [BLK, 1], U32) for i in range(2)]
        blk_in = sb("blk_in", [P, 2, NT])
        blk_of, row_of = sb("blk_of", [P, 2, NT]), sb("row_of", [P, 2, NT])
        f_sq, f_var, f_std, f_rstd = sm(8), sm(8), sm(8), sm(8)
        UP_BANK = (bank[4], proj_ps[1])
        out_ring = [w_ring[1][:, D * i:D * i + D] for i in range(NT)]
        yg = [w_ring[0][:, D * i:D * i + D] for i in range(4)]

        gate_done, gate_out, merge_done, merge_out = sem("gate_done"), sem("gate_out"), sem("merge_done"), sem("merge_out")
        merge_mul = sem("merge_mul")
        x2_loaded, scale2_ready = sem("x2_loaded"), sem("scale2_ready")
        row_spread, row_ready = sem("row_spread"), sem("row_ready")
        o_done, o_out = sem("o_done"), sem("o_out")
        h2_ready, h2_stored, h2_turned, h2T_ready = sem("h2_ready"), sem("h2_stored"), sem("h2_turned"), sem("h2T_ready")
        router_loaded, routed, scored = sem("router_loaded"), sem("routed"), sem("scored")
        hot_ready, ranked, nbc_ready, ends_done, ended_ready, owners_done = (
            sem("hot_ready"), sem("ranked"), sem("nbc_ready"), sem("ends_done"), sem("ended_ready"), sem("owners_done"))
        plan_ready, list_terms, list_added, list_ready = sem("plan_ready"), sem("list_terms"), sem("list_added"), sem("list_ready")
        passed = sem("passed")

        e_loaded = [sem(f"e_loaded{i}") for i in range(E_SLOTS)]
        down_loaded = [sem(f"down_loaded{i}") for i in range(E_SLOTS)]
        ids_ready, xg_loaded = sem("ids_ready"), [sem(f"xg_loaded{i}") for i in range(AHEAD)]
        xg_turned, xgT_ready = sem("xg_turned"), sem("xgT_ready")
        gu_done, gu_act, hid_ready = sem("gu_done"), sem("gu_act"), sem("hid_ready")
        down_done, y_ready = sem("down_done"), sem("y_ready")
        y_stored = [sem(f"y_stored{i}") for i in range(2)]
        yg_loaded, x3_ready = [sem(f"yg_loaded{i}") for i in range(2)], sem("x3_ready")
        out_ready_, out_stored = sem("out_ready"), sem("out_stored")

        TOKEN_MAJOR = {"z": 0, "v_c": 0, "i_d": 0, "g_d": 0, "v_b0": 0, "v_b1": 1, "v_b2": 2}
        tiles4 = lambda ap: [ap[:, n, :] for n in range(NT)]
        DEST = {"z": tiles4(z_tok), "xbc_a": [xbc_raw[:, i, 3:3 + T] for i in range(4)],
                "xbc_b": [xbc_raw[:, 4, 3:3 + T], xbc_raw[:, 5, 3:3 + T], dt_raw],
                "q_c": tiles4(df_q), "k_c": tiles4(df_k), "v_c": tiles4(df_v),
                "q_d": tiles4(hg_q), "f_d": tiles4(hg_k), "i_d": tiles4(hg_v), "g_d": tiles4(hg_g)}
        for g in range(3):
            DEST.update({f"q_b{g}": tiles4(dl_q), f"k_b{g}": tiles4(dl_k), f"v_b{g}": tiles4(dl_v[g])})
        for u in range(ADA_FIRST, ADA):
            DEST[f"ada{u}"] = [mod[:, 4 * u:4 * u + 4]]
        BRANCH_DONE = {0: ssd_out, KD: df_out, 2 * KD: hg_out, 3 * KD: dl_out}
        OUT_ORDER = [(0, 0), (1, 0), (0, 1), (1, 1), (2, 0), (2, 1), (3, 0), (3, 1)]
        last_ada = merged.rearrange("p k t -> p (k t)").rearrange("p (k n) -> p k n", k=KD)
        m_slot = [w[:, KD * 256:KD * 256 + KB * 256].rearrange("p (k n) -> p k n", k=KB) for w in w_ring]
        g_slot = [w[:, 0:KD * 256].rearrange("p (k n) -> p k n", k=KD) for w in w_ring]

        block = ctx.enter_context(nc.Block())

        @block.sync
        def _(sp):
            def load_vec(row, src, n):
                sp.dma_start(rows[row:row + n, :], src).then_inc(vec_loaded, 16)

            for i in range(NT):
                sp.dma_start(x_tok[:, i, :], x_dram[:, i, :]).then_inc(x_loaded, 16)
            sp.dma_start(c_raw[:], c.rearrange("a (p k) -> (a p) k", k=KD)).then_inc(vec_loaded, 16)
            load_vec(R_BADA, b_ada.rearrange("a (j q) -> (a j) q", q=P), 48)
            load_vec(R_NMIX, norm_mix_w.rearrange("a (j q) -> (a j) q", q=P), KD)
            load_vec(R_NFFN, norm_ffn_w.rearrange("a (j q) -> (a j) q", q=P), KD)
            load_vec(R_FIN, final_norm_w.rearrange("(j q) -> j q", q=P), KD)
            load_vec(R_CONVB, conv_b.rearrange("a (j q) -> (a j) q", q=P), 6)
            load_vec(R_CONVW, conv_w.rearrange("a k (j q) -> (a k j) q", q=P), 24)
            load_vec(R_SSDN, ssd_norm_w.rearrange("a (j q) -> (a j) q", q=P), KB)
            load_vec(R_SUBLN, diff_subln_w, 1)
            for half in range(2):
                sp.dma_start(rows[R_HGN:R_HGN + 1, 64 * half:64 * half + 64], hgrn_norm_w).then_inc(vec_loaded, 16)
            load_vec(R_LB, hgrn_lb_logits.rearrange("a (j q) -> (a j) q", q=P), KB)
            for at_, src in ((B_DTB, ssd_dt_bias), (B_ALOG, ssd_a_log), (B_DSK, ssd_d),
                             (B_LAM, diff_lambda.rearrange("a i n -> a (i n)")),
                             (B_RB, router_bias.rearrange("(a n) -> a n", a=1))):
                n = src.shape[1]
                sp.dma_start(bc_row[:, at_:at_ + n], src).then_inc(vec_loaded, 16)

            for q, u in enumerate(ADA_HEAD):
                sp.dma_start(ada_slot[q], ada_dram[:, :, 512 * u:512 * u + 512]).then_inc(w_loaded[q] if q < 2 else ada_loaded[q - 2], 16)

            def slot_free(n):
                before = UNITS[n - 2]
                if n - 2 < 2:
                    sp.wait_ge(w_used, n - 1)
                elif before.startswith("ada"):
                    sp.wait_ge(ada_summed, int(before[3:]) - ADA_FIRST + 1)
                elif before.startswith("merge"):
                    sp.wait_ge(merge_done, 2 * int(before[5:]) + 2)
                else:
                    sp.wait_ge(proj_done, out_ready(before))

            columns = {name: (c0, width) for name, c0, width, _ in PROJ}
            for n, name in enumerate(UNITS[2:], 2):
                if name == "f_d":
                    sp.wait_ge(ssd_out, NT)
                    sp.dma_start(last_ada, ada_dram[:, :, 512 * (ADA - 1):512 * ADA]).then_inc(ada_loaded[0], 16)
                if name == f"merge{3 * MERGE_UNITS // 4 + 2}":
                    sp.wait_ge(dl_out, NT)
                    sp.dma_start(x2, x_dram).then_inc(x2_loaded, 16)
                slot_free(n)
                if name.startswith("merge"):
                    u = int(name[5:])
                    b, c0 = MERGE_ORDER[u // 4], 256 * (u % 4)
                    sp.dma_start(g_slot[n % 2], in_dram[:, :, C_GATE + b * D + c0:C_GATE + b * D + c0 + 256]).then_inc(w_loaded[n % 2], 16)
                    sp.dma_start(m_slot[n % 2], w_merge[0][b].rearrange("(k p) n -> p k n", p=P)[:, :, c0:c0 + 256]).then_inc(w_loaded[n % 2], 16)
                elif name.startswith("out"):
                    c0 = 512 * int(name[3:])
                    sp.dma_start(w_slot[n % 2], w_out[0].rearrange("(k p) n -> p k n", p=P)[:, :, c0:c0 + 512]).then_inc(w_loaded[n % 2], 16)
                elif name.startswith("ada"):
                    c0 = 512 * int(name[3:])
                    sp.dma_start(w_slot[n % 2], ada_dram[:, :, c0:c0 + 512]).then_inc(w_loaded[n % 2], 16)
                else:
                    c0, width = columns[name]
                    sp.dma_start(w_slot[n % 2][:, :, 0:width], in_dram[:, :, c0:c0 + width]).then_inc(w_loaded[n % 2], 16)
            sp.dma_start(down_place[0][:, 0:KD * N_EXP].rearrange("p (k e) -> p k e", k=KD),
                         w_router.rearrange("(k p) e -> p k e", p=P)).then_inc(router_loaded, 16)
            for i in range(NT):
                sp.wait_ge(h2_ready, i + 1)
                sp.dma_start(h2_dram.rearrange("(i p) d -> p i d", p=P)[:, i, :], h2[:, i, :]).then_inc(h2_stored, 16)

            sp.wait_ge(o_done, 8)
            sp.wait_ge(routed, NT)
            sp.wait_ge(h2_stored, 16 * NT)
            sp.wait_ge(plan_ready, 2)
            n_valid = sp.value_load(n_blocks[0:1, 0:1], min_val=MIN_BLOCKS, max_val=MAX_BLOCKS)

            def expert_weights(b, s, first):
                e = sp.value_load(blk_exp[0:1, bass.ds(b, 1)], min_val=0, max_val=N_EXP - 1)
                if not first:
                    sp.wait_ge(gu_done, 2 * b - 2 * (E_SLOTS - 1))
                for half, w in enumerate((w_expert_gate, w_expert_up)):
                    sp.dma_start(w_wide[s][:, half],
                                 w[0][bass.ds(e, 1)].rearrange("a (p k) f -> (a p) k f", k=KD)).then_inc(e_loaded[s], 16)
                if not first:
                    sp.wait_ge(down_done, b - (E_SLOTS - 1))
                sp.dma_start(w_down[s], w_expert_down[0][bass.ds(e, 1)].rearrange("a (p j) d -> (a p) j d", j=2))\
                  .then_inc(down_loaded[s], 16)

            for s in range(E_SLOTS):
                expert_weights(s, s, True)
                if s == 0:
                    sp.wait_ge(xg_loaded[0], 16)
            with sp.Fori(1, N_BLK // E_SLOTS) as it:
                for s in range(E_SLOTS):
                    b = E_SLOTS * it + s
                    with sp.If(b < n_valid):
                        expert_weights(b, s, False)
            for s in range(2):
                sp.wait_ge(y_stored[s], 16 * ((n_valid + 1 - s) // 2))
            for i in range(NT):
                for s in range(2):
                    if i >= 2:
                        sp.wait_ge(x3_ready, i - 1)
                    sp.dma_start(yg[2 * (i % 2) + s], y_dram[T * s + P * i:T * s + P * i + P, :]).then_inc(yg_loaded[i % 2], 16)

        @block.gpsimd
        def _(pool):
            p = Order(pool, pool_order)
            p(pool.memset(ones[:], 1.0))
            for m in (ident, causal, band_prev, level_mask):
                p(pool.memset(m[:], 0.0))
            p(pool.affine_select(out=ident[:], in_=ident[:], compare_op=ALU.not_equal, fill=1.0, base=0,
                                 pattern=[[-1, P]], channel_multiplier=1))
            p(pool.affine_select(out=upper[:], in_=ones[:], compare_op=ALU.is_ge, fill=0.0, base=0,
                                 pattern=[[1, P]], channel_multiplier=-1))
            p(pool.affine_select(out=upper_strict[:], in_=ones[:], compare_op=ALU.is_gt, fill=0.0, base=0,
                                 pattern=[[1, P]], channel_multiplier=-1))
            p(pool.affine_select(out=causal[:], in_=causal[:], compare_op=ALU.is_ge, fill=NEG, base=0,
                                 pattern=[[-1, P]], channel_multiplier=1))
            p(pool.affine_select(out=band_prev[:], in_=band_prev[:], compare_op=ALU.is_ge, fill=NEG, base=0,
                                 pattern=[[1, P]], channel_multiplier=-1))
            p(pool.iota(apart[:], pattern=[[-1, P]], base=P, channel_multiplier=1), apart_ready)
            for n, b in enumerate(LEVELS):
                m = level_mask[:, n, :].rearrange("p (k s i) -> p k s i", s=2, i=b)[:, :, 1, :]
                one = ones[:].rearrange("p (k s i) -> p k s i", s=2, i=b)[:, :, 1, :]
                p(pool.affine_select(out=m, in_=one, compare_op=ALU.is_ge, fill=0.0, base=0,
                                     pattern=[[-2 * b, P // (2 * b)], [0, b]], channel_multiplier=1))
                p(pool.affine_select(out=m, in_=m, compare_op=ALU.is_ge, fill=0.0, base=b - 1,
                                     pattern=[[2 * b, P // (2 * b)], [0, b]], channel_multiplier=-1))
            h2 = two_heads[:].rearrange("p (h n) -> p h n", h=2)
            p(pool.affine_select(out=h2, in_=ones[:].rearrange("p (h n) -> p h n", h=2), compare_op=ALU.is_ge,
                                 fill=0.0, base=0, pattern=[[-64, 2], [0, 64]], channel_multiplier=1))
            p(pool.affine_select(out=h2, in_=h2, compare_op=ALU.is_ge, fill=0.0, base=63,
                                 pattern=[[64, 2], [0, 64]], channel_multiplier=-1))
            pool.iota(iota_exp[:], pattern=[[1, N_EXP]], base=0, channel_multiplier=0,
                      allow_small_or_imprecise_dtypes=True).then_inc(consts_ready, 1)
            pool.iota(iota_grp[:], pattern=[[1, GROUPS]], base=0, channel_multiplier=0,
                      allow_small_or_imprecise_dtypes=True).then_inc(consts_ready, 1)
            p(pool.iota(iota_row[:], pattern=[[1, BLK]], base=0, channel_multiplier=0, allow_small_or_imprecise_dtypes=True))
            pool.iota(iota_blk[:], pattern=[[1, LIST_BLK]], base=0, channel_multiplier=0,
                      allow_small_or_imprecise_dtypes=True).then_inc(consts_ready, 1)
            pool.iota(entry[:, 0], pattern=[[0, 2], [P, NT]], base=0, channel_multiplier=1,
                      allow_small_or_imprecise_dtypes=True).then_inc(consts_ready, 1)
            pool.iota(entry[:, 1], pattern=[[T, 2], [P, NT]], base=-2 * T, channel_multiplier=1,
                      allow_small_or_imprecise_dtypes=True).then_inc(consts_ready, 1)
            for i in range(ADA - ADA_FIRST):
                name, acc = f"ada{ADA_FIRST + i}", ada_acc[i % 2]
                if name in unit_of:
                    w = w_slot[unit_of[name] % 2]
                    pool.wait_ge(w_loaded[unit_of[name] % 2], in_slot(name))
                else:
                    w = last_ada
                    pool.wait_ge(ada_loaded[0], 32)
                if i == 0:
                    pool.wait_ge(c_ready, 1)
                if i >= 2:
                    pool.wait_ge(proj_done, out_ready(f"ada{ADA_FIRST + i - 2}"))
                p(pool.tensor_tensor(w, w, along(c_act[:], 512), ALU.mult))
                p(pool.tensor_tensor(w[:, 0:4, :], w[:, 0:4, :], w[:, 4:8, :], ALU.add))
                p(pool.tensor_tensor(w[:, 0:2, :], w[:, 0:2, :], w[:, 2:4, :], ALU.add))
                p(pool.tensor_tensor(acc[:], w[:, 0, :], w[:, 1, :], ALU.add), ada_summed)
            pool.wait_ge(df_out, NT)
            pool.memset(hg_attn, 0.0).then_inc(hg_zeroed, 1)
            pool.wait_ge(dl_prob, len(DIL_SCORES))
            for g in range(2):
                pool.dma_start(stat_dram[g].rearrange("(p a) v -> p a v", a=4), dl_stat[g + 1]).then_inc(dl_stored, 16)
            pool.wait_ge(dl_stored, 32)
            for g in range(2):
                pool.dma_start(dl_nat[g], stat_dram[g].rearrange("(a p) v -> p a v", p=P)).then_inc(dl_back, 16)
            pool.wait_ge(dl_weighed, 3)
            for g in range(2):
                pool.dma_start(weight_dram[g].rearrange("(a p) v -> p a v", p=P), dl_w[g + 1]).then_inc(dl_stored, 16)
            pool.wait_ge(dl_stored, 64)
            for g in range(2):
                pool.dma_start(dl_wg[g], weight_dram[g].rearrange("(p a) v -> p a v", a=4)).then_inc(dl_back, 16)
            pool.wait_ge(h2_stored, 16 * NT)
            pool.wait_ge(plan_ready, 2)
            n_valid = pool.value_load(n_blocks[0:1, 0:1], min_val=MIN_BLOCKS, max_val=MAX_BLOCKS)

            pool.wait_ge(list_ready, 2)

            def gather(b, s, n):
                pool.tensor_copy(blk_tok[s][:], blk_list[:, bass.ds(b, 1)]).then_inc(ids_ready, 1)
                pool.wait_ge(ids_ready, n + 1)
                pool.sem_inc(passed)
                pool.indirect_dma_start(out=xg[s][0:BLK, :], out_offset=None, in_=h2_dram,
                                        in_offset=bass.IndirectOffsetOnAxis(ap=blk_tok[s][:], axis=0)).then_inc(xg_loaded[s], 16)

            def scatter(b, s, n):
                pool.wait_ge(y_ready, 2 * b + 2)
                pool.tensor_copy(blk_dst[s][:], blk_list[:, bass.ds(b + LIST_BLK, 1)]).then_inc(ids_ready, 1)
                pool.wait_ge(ids_ready, n + 1)
                pool.sem_inc(passed)
                pool.indirect_dma_start(out=y_dram, out_offset=bass.IndirectOffsetOnAxis(ap=blk_dst[s][:], axis=0),
                                        in_=yb[s][0:BLK, :], in_offset=None, bounds_check=2 * T - 1, oob_is_err=False)\
                    .then_inc(y_stored[s], 16)

            for s in range(AHEAD):
                gather(s, s, s)
            for s in range(AHEAD):
                pool.wait_ge(xg_turned, s + 1)
                gather(s + AHEAD, s, AHEAD + 2 * s)
                scatter(s, s % 2, AHEAD + 2 * s + 1)
            with pool.Fori(1, N_BLK // AHEAD) as it:
                for s in range(AHEAD):
                    b = AHEAD * it + s
                    with pool.If(b < n_valid):
                        pool.wait_ge(xg_turned, b + 1)
                        gather(b + AHEAD, s, 2 * b + AHEAD)
                        scatter(b, s % 2, 2 * b + AHEAD + 1)

        @block.tensor
        def _(pe):
            pe.wait_ge(consts_ready, 5)
            pe.wait_ge(vec_loaded, 16 * 17)
            pe.transpose(bank[2][:, 0:N_ROWS], rows[:], ident[0:N_ROWS, 0:N_ROWS]).then_inc(cols_turned, 1)
            pe.matmul(bank[3][:, 0:N_BC], ones[0:1, :], bc_row[:], start=True, stop=True).then_inc(bc_spread, 1)

            def sum_partitions(ps, c0, acc):
                for j in range(4):
                    mm = pe.matmul(ps[:, c0 + j:c0 + j + 1], acc[:, P * j:P * j + P], ones[:, 0:1], start=True, stop=True)
                return mm

            def turn_x(k):
                for i in range(NT):
                    mm = pe.transpose(X_BANK[k][:, P * i:P * i + P], x_nrm[:, i, P * k:P * k + P], ident[:])
                mm.then_inc(x_turned, 1)

            pe.wait_ge(xn_ready, NT)
            for k in range(KD - 2):
                turn_x(k)
            for q, u in enumerate(ADA_HEAD):
                pe.wait_ge(w_used, q + 1)
                sum_partitions(MOD_BANK[q // 2], 4 * u, ada_first[q]).then_inc(ada_done, 1)
                if q >= 2:
                    pe.wait_ge(h_ready, q - 1)
                    turn_x(KD - 4 + q)
            pe.wait_ge(h_ready, KD)

            def at_unit(name):
                n = unit_of[name]
                pe.wait_ge(w_loaded[n % 2], in_slot(name))
                return n % 2

            def project(name, m):
                o = first_out[name] + m
                ps = proj_ps[o % 2]
                if not name.startswith("ada"):
                    w = w_slot[unit_of[name] % 2]
                if name.startswith("ada"):
                    pe.wait_ge(ada_summed, int(name[3:]) - ADA_FIRST + 1)
                elif m == 0:
                    at_unit(name)
                if o >= 2:
                    pe.wait_ge(proj_out, o - 1)
                if name.startswith("ada"):
                    mm = sum_partitions(ps, 0, ada_acc[int(name[3:]) % 2])
                elif (name, m) == ("xbc_b", 2):
                    for a in range(NT):
                        for k in range(KD):
                            mm = pe.matmul(ps[:, 8 * a:8 * a + 8], hT[:, k, P * a:P * a + P], w[:, k, 256:264],
                                           start=(k == 0), stop=(k == KD - 1))
                elif name in TOKEN_MAJOR:
                    for k in range(KD):
                        mm = pe.matmul(ps[:], tokens_of(hT[:, k, :], TOKEN_MAJOR[name], m), w[:, k, :], start=(k == 0), stop=(k == KD - 1))
                else:
                    for k in range(KD):
                        mm = pe.matmul(ps[:], w[:, k, P * m:P * m + P], hT[:, k, :], start=(k == 0), stop=(k == KD - 1))
                mm.then_inc(proj_done, 1)

            def merge(t):
                b, name = MERGE_ORDER[t // KD], f"merge{t // 2}"
                slot = unit_of[name] % 2
                if t in BRANCH_DONE:
                    pe.wait_ge(BRANCH_DONE[t], NT)
                    pe.wait_ge(proj_out, out_ready(PROJ[N_BEFORE - 1][0]) if t < 2 * KD else out_ready("v_b2"))
                if t % 2 == 0:
                    at_unit(name)
                if t:
                    pe.wait_ge(gate_out, t)
                c0 = P * (t % 2)
                for k in range(KD):
                    mm = pe.matmul(proj_ps[0][:], g_slot[slot][:, k, c0:c0 + P], hT[:, k, :], start=(k == 0), stop=(k == KD - 1))
                mm.then_inc(gate_done, 1)
                if t:
                    pe.wait_ge(merge_mul, t)
                for k in range(KB):
                    mm = pe.matmul(proj_ps[1][:], m_slot[slot][:, k, c0:c0 + P], branchT[:, b * KB + k, :], start=(k == 0), stop=(k == KB - 1))
                mm.then_inc(merge_done, 1)

            def emit(items):
                for name, m in items:
                    if name == "merge":
                        merge(m)
                    else:
                        project(name, m)

            emit(outputs("z", "xbc_a", "xbc_b"))
            emit(FILL["ssd"][0])
            pe.wait_ge(ssd_act, 6)
            for i in range(NT):
                if i >= 2:
                    pe.wait_ge(ssd_tok, i - 1)
                for t in range(4):
                    mm = pe.transpose(bank[i % 2][:, P * t:P * t + P], xbcT[:, t, P * i:P * i + P], ident[:])
                mm.then_inc(ssd_turned, 1)
            for i in range(NT):
                mm = pe.transpose(bank[2][:, P * i:P * i + P], xbcT[:, 4, P * i:P * i + P], ident[:])
            mm.then_inc(ssd_turned, 1)
            pe.wait_ge(adt_ready, 1)
            pe.matmul(bank[3][:, 0:32], upper[:], adt, start=True, stop=True)
            pe.matmul(bank[3][:, 32:64], ones[:], adt, start=True, stop=True).then_inc(acs_done, 1)
            emit(FILL["ssd"][1])
            pe.wait_ge(acs_ready, 1)
            pe.wait_ge(ssd_tok, NT + 1)
            for i in range(NT):
                s = slice(P * i, P * i + P)
                if i:
                    pe.wait_ge(ssd_m, i)
                    pe.wait_ge(ssd_state, i)
                for g in range(2):
                    pe.matmul(bank[5 * g][:, 0:P], xbcT[64 * g:64 * g + 64, 4, s], xbcT[64 * g:64 * g + 64, 5, s],
                              start=True, stop=True)
                for h in range(SSD_H):
                    mm = pe.matmul(bank[1 + h // 4][:, P * (h % 4):P * (h % 4) + P],
                                   adt[:, 8 * i + h:8 * i + h + 1].to_broadcast([P, P]), upper[:], start=True, stop=True)
                mm.then_inc(ssd_score, 1)
                emit(FILL["ssd"][2 + 2 * i])
                pe.wait_ge(ssd_m, i + 1)
                if i:
                    pe.wait_ge(ssd_out, i)
                for h in range(SSD_H):
                    mm = pe.matmul(bank[3][:, 64 * h:64 * h + 64], ssd_l[:, h, :], xs_dt[:, i % 2, 64 * h:64 * h + 64],
                                   start=True, stop=True)
                if i:
                    pe.wait_ge(ssd_state, i)
                    mm = pe.matmul(bank[4][:], xbcT[:, 5, s], ssd_r, start=True, stop=True)
                if i < NT - 1:
                    mm = pe.matmul(bank[5][:], b_tok[:, i, :], xs_dec[:, i % 2, :], start=True, stop=True)
                mm.then_inc(ssd_y, 1)
                emit(FILL["ssd"][3 + 2 * i])
                pe.wait_ge(ssd_o, i + 1)
                for j in range(KB):
                    mm = pe.transpose(bank[4][:, P * j:P * j + P], ssd_yt[:, P * j:P * j + P], ident[:])
                mm.then_inc(ssd_oT, 1)
            DF_STEPS = [(i, h) for i in range(NT) for h in range(DIFF_H)]
            pe.wait_ge(proj_out, out_ready("v_c"))
            pe.wait_ge(ssd_out, NT)

            def df_scores(n):
                i, h = DF_STEPS[n]
                if n >= 2:
                    pe.wait_ge(df_masked, 2 * n - 2)
                for m in range(2):
                    s = slice(64 * m, 64 * m + 64)
                    mm = pe.matmul(bank[2 * (n % 2) + m][:, 0:P * (i + 1)], df_q[s, h, P * i:P * i + P],
                                   df_k[s, h, 0:P * (i + 1)], start=True, stop=True)
                mm.then_inc(df_score, 1)

            df_scores(0)
            for n, (i, h) in enumerate(DF_STEPS):
                if n + 1 < len(DF_STEPS):
                    df_scores(n + 1)
                emit(FILL["diff"][n])
                pe.wait_ge(df_mixed, n + 1)
                if n:
                    pe.wait_ge(df_copied, n)
                if h == 0 and i:
                    pe.wait_ge(df_out, i)
                for b in range(i + 1):
                    mm = pe.transpose(bank[4][:, P * b:P * b + P], df_attn[:, n % 2, P * b:P * b + P], ident[:])
                mm.then_inc(df_turned, 1)
                pe.wait_ge(df_copied, n + 1)
                for b in range(i + 1):
                    mm = pe.matmul(bank[5][:, P * h:P * h + P], df_attnT[:, n % 2, P * b:P * b + P],
                                   df_v[:, b, P * h:P * h + P], start=(b == 0), stop=(b == i))
                mm.then_inc(df_y, 1)
                if h == DIFF_H - 1:
                    pe.wait_ge(df_ready, i + 1)
                    for j in range(KB):
                        mm = pe.transpose(bank[4][:, P * j:P * j + P], df_o[:, P * j:P * j + P], ident[:])
                    mm.then_inc(df_oT, 1)

            emit(FILL["hg"][0])
            pe.wait_ge(df_out, NT)
            pe.wait_ge(hg_kg, 1)
            for i in range(NT):
                if i >= 2:
                    pe.wait_ge(hg_kcopied, i - 1)
                for n in range(NT):
                    mm = pe.transpose(bank[i % 2][:, P * n:P * n + P], hg_qk[0][:, n, P * i:P * i + P], ident[:])
                mm.then_inc(hg_kturned, 1)
            pe.wait_ge(hg_kcopied, NT)
            for lv in range(len(LEVELS) + 1):
                keys, queries = (hg_k, hg_q) if lv == 0 else (hg_qk[(lv - 1) % 2],) * 2
                if lv:
                    emit(FILL["hg"][lv])
                    pe.wait_ge(hg_scaled, lv)
                for i in range(NT):
                    for s in range(2):
                        q = 8 * lv + 2 * i + s
                        if q >= 6:
                            pe.wait_ge(hg_pick, q - 5)
                        for n in range(NT):
                            mm = pe.matmul(bank[q % 6][:, P * n:P * n + P], keys[64 * s:64 * s + 64, n, P * i:P * i + P],
                                           queries[64 * s:64 * s + 64, n, P * i:P * i + P], start=True, stop=True)
                        mm.then_inc(hg_score, 1)
            emit(FILL["hg"][len(LEVELS) + 1])
            pe.wait_ge(hg_pick, 8 * (len(LEVELS) + 1))
            pe.wait_ge(hg_qgr, 1)
            for i in range(NT):
                if i:
                    pe.wait_ge(hg_state, i)
                    pe.wait_ge(hg_ready, i)
                    for n in range(NT):
                        pe.matmul(bank[0][:, P * n:P * n + P], hg_qg[:, n, P * i:P * i + P], hg_r[:, n, :],
                                  start=(n == 0), stop=False, skip_group_check=True)
                for h in range(HG_H):
                    mm = pe.matmul(bank[0][:, 64 * h:64 * h + 64], hg_attn[:, i, h % 2, h // 2, :],
                                   hg_v[:, i, 64 * h:64 * h + 64], start=(i == 0 and h == 0), stop=(h == HG_H - 1),
                                   skip_group_check=True)
                if i < NT - 1:
                    for n in range(NT):
                        mm = pe.matmul(bank[1][:, P * n:P * n + P], hg_ktok[:, i, P * n:P * n + P],
                                       hg_v[:, i, P * n:P * n + P], start=True, stop=True)
                mm.then_inc(hg_y, 1)
                if i < NT - 1:
                    emit(FILL["hg"][len(LEVELS) + 2 + i])
                pe.wait_ge(hg_ready, i + 1)
                if i:
                    pe.wait_ge(hg_out, i)
                for j in range(KB):
                    mm = pe.transpose(bank[2][:, P * j:P * j + P], hg_o[:, P * j:P * j + P], ident[:])
                mm.then_inc(hg_oT, 1)

            for g in range(3):
                if g == 0:
                    pe.wait_ge(gate_out, 2 * KD)
                    pe.wait_ge(merge_mul, 2 * KD)
                emit(outputs(f"q_b{g}", f"k_b{g}", f"v_b{g}"))
                pe.wait_ge(proj_out, out_ready(f"v_b{g}"))
                if g == 0:
                    pe.wait_ge(hg_out, NT)
                for n, (gg, j, _, tiles, prev) in enumerate(DIL_SCORES):
                    if gg != g:
                        continue
                    if n >= 4:
                        pe.wait_ge(dl_masked, n - 3)
                    for c_, a in enumerate(tiles):
                        mm = pe.matmul(bank[n % 4][:, P * c_:P * c_ + P], tokens_of(dl_q[:, j, :], g, a),
                                       tokens_of(dl_k[:, j, :], g, a - 1 if prev else a), start=True, stop=True)
                    mm.then_inc(dl_score, 1)
            emit(FILL["dil"][0])
            for j in range(DIL_H):
                pe.wait_ge(dl_scaled, 4 * j + 4)
                if j:
                    pe.wait_ge(dl_copied, 4 * j)
                for b in range(DIL_BLOCKS):
                    mm = pe.transpose(bank[b // 4][:, P * (b % 4):P * (b % 4) + P], dl_p[:, j, b, :], ident[:])
                    if b % 4 == 3 or b == DIL_BLOCKS - 1:
                        mm.then_inc(dl_turned, 1)
                emit(FILL["dil"][1 + j])
                pe.wait_ge(dl_copied, 4 * j + 4)
                if j >= 2:
                    pe.wait_ge(dl_out, j - 1)
                y = bank[4 + j % 2][:]
                s = slice(P * j, P * j + P)
                for b in range(DIL_BLOCKS):
                    g, a, key = ((0, b, b) if b < 4 else (0, b - 3, b - 4) if b < 7 else
                                 (1, b - 7, b - 7) if b < 11 else (2, b - 11, b - 11))
                    mm = pe.matmul(tokens_of(y, g, a), dl_v[g][:, key, s], dl_pT[:, b, :],
                                   start=(b == 0), stop=(b == DIL_BLOCKS - 1), skip_group_check=True)
                mm.then_inc(dl_y, 1)
            emit(merges[3 * KD:])
            pe.wait_ge(mod_copied, 1)
            for v, (src, c0) in enumerate(((mod, 16), (scale_ffn, 0), (mod, 24), (mod, 40), (cols, R_FIN))):
                if v == 1:
                    pe.wait_ge(scale2_ready, 1)
                for half in range(2):
                    q = 2 * v + half
                    if q >= 2:
                        pe.wait_ge(row_ready, q - 1)
                    for j in range(4):
                        at_ = c0 + 4 * half + j
                        mm = pe.matmul(bank[2 + q % 2][:, P * j:P * j + P], src[:, at_:at_ + 1].to_broadcast([P, P]), ident[:],
                                       start=True, stop=True)
                    mm.then_inc(row_spread, 1)
            pe.wait_ge(merge_out, 32)
            w_r = down_place[0][:, 0:KD * N_EXP].rearrange("p (k e) -> p k e", k=KD)

            def turn_h2(i):
                pe.wait_ge(h2_ready, i + 1)
                if i:
                    pe.wait_ge(h2T_ready, 2 * i)
                for k in range(KD):
                    mm = pe.transpose(bank[k // 4][:, P * (k % 4):P * (k % 4) + P], h2[:, i, P * k:P * k + P], ident[:])
                mm.then_inc(h2_turned, 1)

            def route(i):
                pe.wait_ge(h2T_ready, 2 * i + 2)
                if i == 0:
                    pe.wait_ge(router_loaded, 16)
                for k in range(KD):
                    mm = pe.matmul(bank[2][:, N_EXP * i:N_EXP * i + N_EXP], h2T[:, k, P * i:P * i + P], w_r[:, k, :],
                                   start=(k == 0), stop=(k == KD - 1))
                mm.then_inc(routed, 1)

            for o, (i, half) in enumerate(OUT_ORDER):
                if o == 6:
                    turn_h2(0)
                if o == 7:
                    route(0)
                    turn_h2(1)
                n = unit_of[f"out{half}"]
                if i == 0:
                    at_unit(f"out{half}")
                if o >= 2:
                    pe.wait_ge(o_out, o - 1)
                for k in range(KD):
                    mm = pe.matmul(bank[4 + o % 2][:], merged[:, k, P * i:P * i + P], w_slot[n % 2][:, k, :],
                                   start=(k == 0), stop=(k == KD - 1))
                mm.then_inc(o_done, 1)
            for i in range(1, NT):
                route(i)
                if i + 1 < NT:
                    turn_h2(i + 1)
            pe.wait_ge(hot_ready, 1)
            pe.matmul(bank[3][:, 0:NT * N_EXP], upper_strict[:], both_hot[:].rearrange("p i e -> p (i e)"), start=True, stop=False,
                      skip_group_check=True)
            pe.matmul(bank[3][:, N_EXP:NT * N_EXP], ones[:], hot_sum[:, 0:NT - 1, :].rearrange("p i e -> p (i e)"), start=False, stop=True,
                      skip_group_check=True)
            pe.matmul(bank[4][:, 0:N_EXP], ones[:], hot_sum[:, NT - 1, :], start=True, stop=True)
            pe.matmul(bank[5][0:N_EXP, 0:1], hot_sum[:, NT - 1, :], ones[:, 0:1], start=True, stop=True).then_inc(ranked, 1)
            pe.wait_ge(nbc_ready, 1)
            pe.matmul(bank[5][0:N_EXP, 0:1], upper[0:N_EXP, 0:N_EXP], nbc[:, 0:1], start=True, stop=True).then_inc(ends_done, 1)
            pe.wait_ge(ended_ready, 1)
            pe.matmul(bank[4][0:1, 0:N_BLK], ones[0:N_EXP, 0:1], ended, start=True, stop=True).then_inc(owners_done, 1)
            pe.wait_ge(list_terms, 2)
            for s in range(2):
                for i in range(NT):
                    mm = pe.matmul(bank[2][0:BLK, 0:2 * LIST_BLK], in_row[:, s, i, :], list_term[:, s, i].rearrange("p v b -> p (v b)"),
                                   start=(s == 0 and i == 0), stop=(s == 1 and i == NT - 1))
            mm.then_inc(list_added, 1)

            pe.wait_ge(plan_ready, 2)
            n_valid = pe.value_load(n_blocks[0:1, 0:1], min_val=MIN_BLOCKS, max_val=MAX_BLOCKS)

            def turn_rows(b, s, first=False):
                pe.wait_ge(xg_loaded[s], 4 * (b - s) + 16)
                if not first:
                    pe.wait_ge(xgT_ready, b)
                pe.sem_inc(passed)
                half = KD // 2
                for k in range(KD):
                    mm = pe.transpose(bank[k // half][:, BLK * (k % half):BLK * (k % half) + BLK], xg[s][0:BLK, :].rearrange("p (q k) -> p k q", k=KD)[:, k, :],
                                      ident[0:BLK, 0:BLK])
                mm.then_inc(xg_turned, 1)

            def expert(b, s):
                pe.wait_ge(e_loaded[s], 8 * (b - s) + 32)
                pe.wait_ge(xgT_ready, b + 1)
                gate, up = bank[2 + s % 2], UP_BANK[s % 2]
                for m in range(4):
                    for k in range(KD):
                        mm = pe.matmul((gate, up)[m // 2][:, BLK * (m % 2):BLK * (m % 2) + BLK], w_wide[s][:, m // 2, k, m % 2:F_EXP:2], xgT[s % 2][:, k, :],
                                       start=(k == 0), stop=(k == KD - 1))
                    if m % 2:
                        mm.then_inc(gu_done, 1)
                turn_rows(b + 1, (s + 1) % AHEAD)
                pe.wait_ge(down_loaded[s], 4 * (b - s) + 16)
                pe.wait_ge(hid_ready, b + 1)
                if not (isinstance(b, int) and b == 0):
                    pe.wait_ge(y_ready, 2 * b)
                for half in range(2):
                    for j in range(2):
                        mm = pe.matmul((bank[5], proj_ps[0])[half][0:BLK, :], e_hid[:, j, :],
                                       w_down[s][:, j, 512 * half:512 * half + 512], start=(j == 0), stop=(j == 1))
                mm.then_inc(down_done, 1)

            assert AHEAD == E_SLOTS
            turn_rows(0, 0, True)
            for s in range(E_SLOTS):
                expert(s, s)
            with pe.Fori(1, N_BLK // E_SLOTS) as it:
                for s in range(E_SLOTS):
                    b = E_SLOTS * it + s
                    with pe.If(b < n_valid):
                        expert(b, s)

        @block.scalar
        def _(act):
            a_ = Order(act, act_order)
            act.wait_ge(vec_loaded, 16 * 17)
            act.activation(c_act[:], c_raw[:], ACT.Silu).then_inc(c_ready, 1)
            act.wait_ge(x_loaded, 16 * NT)
            for i in range(NT):
                a_(act.activation(junk, x_tok[:, i, :], ACT.Square, accum_out=x_sq[:, i:i + 1]))
            act.wait_ge(var_ready, 1)
            a_(act.activation(x_std, x_var, ACT.Sqrt), std_ready)

            def drain(items):
                for name, m in items:
                    if name == "merge":
                        act.wait_ge(gate_done, m + 1)
                        if m >= 2:
                            act.wait_ge(merge_out, m - 1)
                        act.activation(gate_sb[:, m % 2, :], proj_ps[0][:], ACT.Sigmoid).then_inc(gate_out, 1)
                    else:
                        o, dst = first_out[name] + m, DEST[name][m]
                        act.wait_ge(proj_done, o + 1)
                        act.activation(dst, proj_ps[o % 2][:, 0:dst.shape[-1]], ACT.Copy).then_inc(proj_out, 1)

            for k in (0, 1, 2, 3, 6, 7):
                act.wait_ge(x_turned, k + 1)
                act.wait_ge(scale1_ready, k // 4 + 1)
                act.activation(hT[:, k, :], X_BANK[k][:], ACT.Identity, scale=scale_mix[:, k:k + 1], bias=mod[:, k:k + 1]).then_inc(h_ready, 1)
            act.wait_ge(h_ready, KD)
            drain(outputs("z", "xbc_a", "xbc_b"))
            for t in range(6):
                act.wait_ge(ssd_conv, t + 1)
                act.activation(xbcT[:, t, :], xbcT[:, t, :], ACT.Silu, bias=cols[:, R_CONVB + t:R_CONVB + t + 1])\
                   .then_inc(ssd_act, 1)
                if t % 2:
                    drain(DRAIN["ssd"][0][t // 2:t // 2 + 1])
            act.activation(z_tok, z_tok, ACT.Silu).then_inc(z_act, 1)
            act.wait_ge(dt_abs, 1)
            act.activation(dt_e, dt_a, ACT.Exp).then_inc(dt_exp, 1)
            act.activation(a_neg, bc[:, B_ALOG:B_ALOG + 8], ACT.Exp).then_inc(dt_exp, 1)
            act.wait_ge(dt_arg, 1)
            act.activation(dt_e, dt_e, ACT.Ln).then_inc(dt_ln, 1)
            for i in range(NT + 1):
                act.wait_ge(ssd_turned, i + 1)
                dst = xs_tok[:, i, :] if i < NT else b_tok
                act.activation(dst, bank[i % 2 if i < NT else 2][:], ACT.Copy).then_inc(ssd_tok, 1)
            drain(DRAIN["ssd"][1])
            act.wait_ge(acs_ready, 1)
            act.activation(eacs, acs, ACT.Exp).then_inc(acs_exp, 1)
            act.wait_ge(acs_ready, 2)
            act.activation(dec, dec, ACT.Exp).then_inc(acs_exp, 1)
            for i in range(NT):
                drain(DRAIN["ssd"][2 + 2 * i])
                act.wait_ge(ssd_diff, i + 1)
                act.activation(ssd_l, ssd_l, ACT.Exp).then_inc(ssd_decay, 1)
                drain(DRAIN["ssd"][3 + 2 * i])
                act.wait_ge(ssd_gated, i + 1)
                act.activation(ssd_tmp, ssd_yt, ACT.Square, accum_out=y_sq[:, i:i + 1]).then_inc(squared, 1)
                act.wait_ge(var_ready, i + 2)
                act.activation(y_std[:, i:i + 1], y_var[:, i:i + 1], ACT.Sqrt).then_inc(std_ready, 1)
            act.wait_ge(exp_arg, 1)
            act.activation(lam_e, lam_s, ACT.Exp).then_inc(exp_out, 1)
            drain(DRAIN["ssd"][-1])
            act.wait_ge(ssd_out, NT)

            def df_exp(n):
                i = n // DIFF_H
                act.wait_ge(df_masked, 2 * n + 2)
                if n >= 2:
                    act.wait_ge(df_mixed, n - 1)
                for m in range(2):
                    v = 2 * (n % 2) + m
                    act.activation(df_s[:, n % 2, m, 0:P * (i + 1)], df_s[:, n % 2, m, 0:P * (i + 1)], ACT.Exp,
                                   bias=df_nmax[:, v:v + 1], accum_out=df_den[:, v:v + 1]).then_inc(df_prob, 1)

            df_exp(0)
            for n in range(NT * DIFF_H):
                if n + 1 < NT * DIFF_H:
                    df_exp(n + 1)
                drain(DRAIN["diff"][n])
                act.wait_ge(df_turned, n + 1)
                if n >= 2:
                    act.wait_ge(df_y, n - 1)
                w = P * (n // DIFF_H + 1)
                act.activation(df_attnT[:, n % 2, 0:w], bank[4][:, 0:w], ACT.Copy).then_inc(df_copied, 1)
                if n % DIFF_H == DIFF_H - 1:
                    act.wait_ge(df_y, n + 1)
                    act.activation(df_tmp, bank[5][:], ACT.Square).then_inc(squared, 1)
                    act.wait_ge(var_ready, 1 + NT + n // DIFF_H + 1)
                    act.activation(df_std, df_var, ACT.Sqrt).then_inc(std_ready, 1)
            drain(DRAIN["diff"][-1])
            act.wait_ge(exp_arg, 2)
            act.activation(lb_e, lb_e, ACT.Exp).then_inc(exp_out, 1)
            act.wait_ge(proj_out, out_ready(PROJ[N_BEFORE - 1][0]))
            act.activation(hg_k, hg_k, ACT.Sigmoid).then_inc(hg_sig, 1)
            act.activation(hg_q, hg_q, ACT.Silu).then_inc(hg_silu, 1)
            act.activation(hg_g, hg_g, ACT.Silu).then_inc(hg_silu, 1)
            drain(DRAIN["hg"][0][0:1])
            act.wait_ge(hg_f, NT)
            act.wait_ge(df_out, NT)
            act.activation(hg_log, hg_k, ACT.Ln).then_inc(hg_ln, 1)
            drain(DRAIN["hg"][0][1:2])
            act.wait_ge(hg_scan, 16)
            act.activation(hg_last, hg_cum.rearrange("p n (i t) -> p (n i) t", t=P)[:, :, P - 1], ACT.Exp).then_inc(hg_expl, 1)
            act.wait_ge(hg_kgarg, 1)
            act.activation(hg_qk[0], hg_qk[0], ACT.Exp).then_inc(hg_expk, 1)
            act.activation(hg_qg, hg_cum, ACT.Exp).then_inc(hg_expq, 1)
            drain(DRAIN["hg"][0][2:])
            for i in range(NT):
                act.wait_ge(hg_kturned, i + 1)
                act.activation(hg_ktok[:, i, :], bank[i % 2][:], ACT.Copy).then_inc(hg_kcopied, 1)
            for lv in range(1, len(LEVELS) + 1):
                drain(DRAIN["hg"][lv])
                act.wait_ge(hg_dist, lv)
                act.activation(hg_qk[(lv - 1) % 2], hg_qk[(lv - 1) % 2], ACT.Exp).then_inc(hg_decay, 1)
            drain(DRAIN["hg"][len(LEVELS) + 1])
            for i in range(NT):
                drain(DRAIN["hg"][len(LEVELS) + 2 + i])
                act.wait_ge(hg_y, i + 1)
                act.activation(hg_tmp, bank[0][:], ACT.Square).then_inc(squared, 1)
                act.wait_ge(var_ready, 1 + 2 * NT + i + 1)
                act.activation(hg_std, hg_var, ACT.Sqrt).then_inc(std_ready, 1)
            act.wait_ge(hg_out, NT)
            for g in range(3):
                if g:
                    act.wait_ge(dl_score, 4 + 4 * g)
                drain(outputs(f"q_b{g}", f"k_b{g}", f"v_b{g}"))
                for n, (gg, j, b0, tiles, prev) in enumerate(DIL_SCORES):
                    if gg == g and (g or prev):
                        act.wait_ge(dl_masked, n + 1)
                        for part, (first, who) in enumerate(((0, range(NT)), (4, range(1, NT))) if g == 0 else ((b0, tiles),)):
                            stat = dl_prev if part else dl_stat[g]
                            for c_, a in enumerate(who):
                                e = act.activation(dl_p[:, j, first + c_, :], dl_p[:, j, first + c_, :], ACT.Exp,
                                                   bias=dl_stat[g][:, a, j:j + 1], accum_out=stat[:, a, 4 + j:5 + j])
                            e.then_inc(dl_prob, 1)
            drain(DRAIN["dil"][0][0:1])
            act.wait_ge(dl_warg, 3)
            for g in range(3):
                act.activation(dl_w[g], dl_w[g], ACT.Exp).then_inc(dl_wexp, 1)
            drain(DRAIN["dil"][0][1:])
            for j in range(DIL_H):
                drain(DRAIN["dil"][1 + j])
                if j:
                    act.wait_ge(dl_y, j)
                for q in range(4):
                    n = min(4, DIL_BLOCKS - 4 * q)
                    act.wait_ge(dl_turned, 4 * j + q + 1)
                    act.activation(dl_pT[:, 4 * q:4 * q + n, :], bank[q][:, 0:P * n].rearrange("p (b k) -> p b k", k=P), ACT.Copy)\
                       .then_inc(dl_copied, 1)
            drain(DRAIN["dil"][-1] + merges[3 * KD:])
            act.wait_ge(dl_out, NT)
            for v, dst in enumerate((bc_gate1, bc_scale2, bc_shift2, bc_gate2, bc_final)):
                for half in range(2):
                    q = 2 * v + half
                    act.wait_ge(row_spread, q + 1)
                    act.activation(dst[:, 512 * half:512 * half + 512], bank[2 + q % 2][:], ACT.Copy).then_inc(row_ready, 1)
            def sum_squares(i):
                act.wait_ge(o_out, OUT_ORDER.index((i, 1)) + 1)
                act.wait_ge(squared, 3 * NT + i)
                act.activation(yb[0], x2[:, i, :], ACT.Square, accum_out=f_sq[:, i:i + 1]).then_inc(squared, 1)
                act.wait_ge(var_ready, 1 + 3 * NT + i + 1)
                act.activation(f_std[:, i:i + 1], f_var[:, i:i + 1], ACT.Sqrt).then_inc(std_ready, 1)

            def h2T_out(i):
                act.wait_ge(h2_turned, i + 1)
                act.activation(h2T[:, 4:8, P * i:P * i + P], bank[1][:].rearrange("p (k t) -> p k t", k=4), ACT.Copy).then_inc(h2T_ready, 1)

            for i in range(3):
                sum_squares(i)
            for i in range(3):
                h2T_out(i)
            sum_squares(3)
            h2T_out(3)
            act.wait_ge(routed, NT)
            act.activation(scores, bank[2][:, 0:NT * N_EXP].rearrange("p (i e) -> p i e", i=NT), ACT.Sigmoid).then_inc(scored, 1)

            act.wait_ge(plan_ready, 2)
            n_valid = act.value_load(n_blocks[0:1, 0:1], min_val=MIN_BLOCKS, max_val=MAX_BLOCKS)

            def rows_out(b, s):
                act.wait_ge(xg_turned, b + 1)
                for half in range(2):
                    copy = act.activation(xgT[s][:, 4 * half:4 * half + 4, :], bank[half][:, 0:4 * BLK].rearrange("p (k t) -> p k t", k=4), ACT.Copy)
                copy.then_inc(xgT_ready, 1)

            def expert_act(b, s):
                act.wait_ge(gu_done, 2 * b + 1)
                act.activation(e_act, bank[2 + s % 2][:, 0:2 * BLK].rearrange("p (j t) -> p j t", j=2), ACT.Silu).then_inc(gu_act, 1)
                rows_out(b + 1, 1 - s)

            rows_out(0, 0)
            for s in range(2):
                expert_act(s, s)
            with act.Fori(1, N_BLK // 2) as it:
                for s in range(2):
                    b = 2 * it + s
                    with act.If(b < n_valid):
                        expert_act(b, s)
            def store(i):
                act.wait_ge(out_ready_, i + 1)
                act.dma_start(out_dram[:, i, :], out_ring[i]).then_inc(out_stored, 16)

            for i in range(NT):
                act.wait_ge(x3_ready, i + 1)
                act.activation(out_ring[i], x2[:, i, :], ACT.Square, accum_out=f_sq[:, NT + i:NT + i + 1]).then_inc(squared, 1)
                act.wait_ge(var_ready, 1 + 4 * NT + i + 1)
                act.activation(f_std[:, NT + i:NT + i + 1], f_var[:, NT + i:NT + i + 1], ACT.Sqrt).then_inc(std_ready, 1)
                if i:
                    store(i - 1)
            store(NT - 1)
            act.wait_ge(out_stored, 16 * NT)

        @block.vector
        def _(dve):
            d = Order(dve, dve_order)
            dve.wait_ge(apart_ready, 1)
            d(dve.tensor_scalar(apart[:], apart[:], 3, None, ALU.bitwise_and))
            d(dve.tensor_scalar(causal_4th[:], apart[:], 0.0, NEG, ALU.is_gt, ALU.mult))
            dve.wait_ge(cols_turned, 1)
            d(dve.tensor_copy(cols[:], bank[2][:, 0:N_ROWS]))
            dve.wait_ge(bc_spread, 1)
            d(dve.tensor_copy(bc[:], bank[3][:, 0:N_BC]))
            dve.wait_ge(act_order, NT)
            d(dve.tensor_scalar(x_var, x_sq, 1.0 / D, EPS, ALU.mult, ALU.add), var_ready)
            dve.wait_ge(std_ready, 1)
            d(dve.reciprocal(x_rstd, x_std))
            for i in range(NT):
                d(dve.tensor_scalar(x_nrm[:, i, :], x_tok[:, i, :], x_rstd[:, i:i + 1], None, ALU.mult), xn_ready)
            dve.wait_ge(c_ready, 1)
            def ada_sum(q):
                w, acc = ada_slot[q], ada_first[q]
                dve.wait_ge(w_loaded[q] if q < 2 else ada_loaded[q - 2], 16)
                d(dve.tensor_scalar(acc, w[:, 0, :], c_act[:, 0:1], None, ALU.mult))
                for k in range(1, KD):
                    d(dve.scalar_tensor_tensor(acc, w[:, k, :], c_act[:, k:k + 1], acc, ALU.mult, ALU.add),
                      w_used if k == KD - 1 else None)

            def modulation(half):
                dve.wait_ge(ada_done, 2 * half + 2)
                for c0 in (4 * half, KD + 4 * half):
                    d(dve.tensor_tensor(mod[:, c0:c0 + 4], MOD_BANK[half][:, c0:c0 + 4], cols[:, c0:c0 + 4], ALU.add))
                k = slice(4 * half, 4 * half + 4)
                d(dve.scalar_tensor_tensor(scale_mix[:, k], mod[:, KD + 4 * half:KD + 4 * half + 4], 1.0,
                                           cols[:, R_NMIX + 4 * half:R_NMIX + 4 * half + 4], ALU.add, ALU.mult), scale1_ready)

            for q in range(3):
                ada_sum(q)
            modulation(0)
            ada_sum(3)
            modulation(1)
            dve.wait_ge(h_ready, 4)
            for k in (4, 5):
                dve.wait_ge(x_turned, k + 1)
                dve.tensor_scalar(hT[:, k, :], X_BANK[k][:], scale_mix[:, k:k + 1], mod[:, k:k + 1], ALU.mult, ALU.add).then_inc(h_ready, 1)
            dve.wait_ge(proj_out, out_ready("xbc_b"))
            d(dve.memset(xbc_raw[:, :, 0:3], 0.0))
            for t, k in [(t0 + t1, k) for t0 in (0, 2, 4) for k in range(CONV_K) for t1 in range(2)]:
                    step = d.free if t % 2 == 0 else d
                    w = cols[:, R_CONVW + 6 * k + t:R_CONVW + 6 * k + t + 1]
                    if k == 0:
                        step(dve.tensor_scalar(xbcT[:, t, :], xbc_raw[:, t, 0:T], w, None, ALU.mult))
                    else:
                        step(dve.scalar_tensor_tensor(xbcT[:, t, :], xbc_raw[:, t, k:k + T], w, xbcT[:, t, :], ALU.mult, ALU.add),
                          ssd_conv if k == CONV_K - 1 else None)
            d(dve.tensor_tensor(dt_raw.rearrange("p (i h) -> p i h", h=8), dt_raw.rearrange("p (i h) -> p i h", h=8),
                                over(bc[:, B_DTB:B_DTB + 8], NT), ALU.add))
            d(dve.scalar_tensor_tensor(dt_a, dt_raw, -1.0, dt_raw, ALU.mult, ALU.min), dt_abs)
            dve.wait_ge(dt_exp, 2)
            d(dve.tensor_scalar(dt_e, dt_e, 1.0, None, ALU.add), dt_arg)
            dve.wait_ge(dt_ln, 1)
            d(dve.scalar_tensor_tensor(dt, dt_raw, 0.0, dt_e, ALU.max, ALU.add))
            d(dve.scalar_tensor_tensor(adt.rearrange("p (i h) -> p i h", h=8), dt.rearrange("p (i h) -> p i h", h=8), -1.0,
                                       over(a_neg, NT), ALU.mult, ALU.mult), adt_ready)
            dve.wait_ge(acs_done, 1)
            d(dve.tensor_copy(acs, bank[3][:, 0:64]), acs_ready)
            d(dve.tensor_tensor(dec, acs[:, 32:64], acs[:, 0:32], ALU.subtract), acs_ready)
            dve.wait_ge(acs_exp, 2)
            d(dve.tensor_tensor(dec, dec, dt, ALU.mult))
            heads = lambda ap: ap.rearrange("p (h n) -> p h n", n=64)
            for i in range(NT):
                e = slice(8 * i, 8 * i + 8)
                dve.wait_ge(ssd_score, i + 1)
                if i:
                    dve.wait_ge(ssd_y, i)
                for h in range(SSD_H):
                    (d if h == SSD_H - 1 else d.free)(dve.tensor_scalar(ssd_l[:, h, :], bank[1 + h // 4][:, P * (h % 4):P * (h % 4) + P],
                                        acs[:, 8 * i + h:8 * i + h + 1], 0.0, ALU.subtract, ALU.min),
                      ssd_diff if h == SSD_H - 1 else None)
                for g in range(2):
                    d.free(dve.tensor_tensor(ssd_cb[:, g, :], bank[5 * g][:, 0:P], upper[:], ALU.mult))
                dve.wait_ge(ssd_tok, i + 1)
                d.free(dve.tensor_tensor(heads(xs_dt[:, i % 2, :]), heads(xs_tok[:, i, :]), along(dt[:, e], 64), ALU.mult))
                d(dve.tensor_tensor(heads(xs_dec[:, i % 2, :]), heads(xs_tok[:, i, :]), along(dec[:, e], 64), ALU.mult))
                dve.wait_ge(ssd_decay, i + 1)
                for g in range(2):
                    (d if g else d.free)(dve.tensor_tensor(ssd_l[:, 4 * g:4 * g + 4, :], ssd_l[:, 4 * g:4 * g + 4, :], over(ssd_cb[:, g, :], 4), ALU.mult),
                      ssd_m if g else None)
                dve.wait_ge(ssd_y, i + 1)
                d(dve.tensor_tensor(heads(ssd_yt), heads(xs_tok[:, i, :]), along(bc[:, B_DSK:B_DSK + 8], 64), ALU.mult))
                d(dve.tensor_tensor(ssd_yt, ssd_yt, bank[3][:], ALU.add))
                if i:
                    d(dve.tensor_tensor(heads(ssd_tmp), heads(bank[4][:]), along(eacs[:, e], 64), ALU.mult))
                    d(dve.tensor_tensor(ssd_yt, ssd_yt, ssd_tmp, ALU.add))
                if i < NT - 1:
                    mask = along(two_heads[:, 0:P:64], 256)
                    grp = lambda ap: ap.rearrange("p (g n) -> p g n", g=2)
                    if i == 0:
                        d(dve.tensor_tensor(grp(ssd_r), grp(bank[5][:]), mask, ALU.mult), ssd_state)
                    else:
                        d(dve.tensor_tensor(heads(ssd_r), heads(ssd_r), along(eacs[:, 32 + 8 * i:40 + 8 * i], 64), ALU.mult))
                        d(dve.tensor_tensor(grp(ssd_tmp), grp(bank[5][:]), mask, ALU.mult))
                        d(dve.tensor_tensor(ssd_r, ssd_r, ssd_tmp, ALU.add), ssd_state)
                dve.wait_ge(z_act, 1)
                d(dve.tensor_tensor(ssd_yt, ssd_yt, z_tok[:, i, :], ALU.mult), ssd_gated)
                dve.wait_ge(squared, i + 1)
                d(dve.tensor_scalar(y_var[:, i:i + 1], y_sq[:, i:i + 1], 1.0 / BW, EPS, ALU.mult, ALU.add), var_ready)
                dve.wait_ge(std_ready, i + 2)
                d(dve.reciprocal(y_rstd[:, i:i + 1], y_std[:, i:i + 1]))
                d(dve.tensor_scalar(ssd_yt, ssd_yt, y_rstd[:, i:i + 1], None, ALU.mult), ssd_o)
                dve.wait_ge(ssd_oT, i + 1)
                d(dve.tensor_tensor(branchT[:, 0:KB, P * i:P * i + P], bank[4][:].rearrange("p (j t) -> p j t", j=KB),
                                    along(cols[:, R_SSDN:R_SSDN + KB], P), ALU.mult), ssd_out)
            lam4 = bc[:, B_LAM:B_LAM + 256].rearrange("p (m s n) -> p m s n", m=2, s=2)
            prod = lam_p.rearrange("p (m n) -> p m n", m=2)
            d(dve.tensor_tensor(prod, lam4[:, :, 0, :], lam4[:, :, 1, :], ALU.mult))
            d(dve.tensor_reduce(lam_s, prod, AX_X, ALU.add), exp_arg)
            d(dve.tensor_scalar(sub_w, cols[:, R_SUBLN:R_SUBLN + 1], 1.0 - LAM_INIT, None, ALU.mult))
            dve.wait_ge(exp_out, 1)
            d(dve.tensor_tensor(lam_neg, lam_e[:, 1:2], lam_e[:, 0:1], ALU.subtract))
            d(dve.tensor_scalar(lam_neg, lam_neg, -LAM_INIT, None, ALU.add))

            def df_mask(n):
                i = n // DIFF_H
                dve.wait_ge(df_score, n + 1)
                own = slice(P * i, P * i + P)
                for m in range(2):
                    s, ps, v = df_s[:, n % 2, m, :], bank[2 * (n % 2) + m], 2 * (n % 2) + m
                    (d.free if i else d)(dve.scalar_tensor_tensor(s[:, own], ps[:, own], 0.125, causal[:], ALU.mult, ALU.add))
                    if i:
                        d(dve.tensor_scalar(s[:, 0:P * i], ps[:, 0:P * i], 0.125, None, ALU.mult))
                    d(dve.tensor_reduce(df_nmax[:, v:v + 1], s[:, 0:P * (i + 1)], AX_X, ALU.max, negate=True), df_masked)

            df_mask(0)
            for n in range(NT * DIFF_H):
                i, h = n // DIFF_H, n % DIFF_H
                if n + 1 < NT * DIFF_H:
                    df_mask(n + 1)
                w, v = P * (i + 1), 2 * (n % 2)
                dve.wait_ge(df_prob, 2 * n + 2)
                if n >= 2:
                    dve.wait_ge(df_turned, n - 1)
                d(dve.reciprocal(df_r[:, v:v + 2], df_den[:, v:v + 2]))
                d(dve.tensor_tensor(df_r[:, v + 1:v + 2], df_r[:, v + 1:v + 2], lam_neg, ALU.mult))
                d(dve.tensor_scalar(df_attn[:, n % 2, 0:w], df_s[:, n % 2, 1, 0:w], df_r[:, v + 1:v + 2], None, ALU.mult))
                d(dve.scalar_tensor_tensor(df_attn[:, n % 2, 0:w], df_s[:, n % 2, 0, 0:w], df_r[:, v:v + 1],
                                           df_attn[:, n % 2, 0:w], ALU.mult, ALU.add), df_mixed)
                if h == DIFF_H - 1:
                    hd = lambda ap: ap.rearrange("p (h n) -> p h n", h=DIFF_H)
                    dve.wait_ge(squared, NT + i + 1)
                    d(dve.tensor_reduce(df_sq, hd(df_tmp), AX_X, ALU.add))
                    d(dve.tensor_scalar(df_var, df_sq, 1.0 / P, EPS, ALU.mult, ALU.add), var_ready)
                    dve.wait_ge(std_ready, 1 + NT + i + 1)
                    d(dve.reciprocal(df_rstd, df_std))
                    d(dve.tensor_tensor(hd(df_o), hd(bank[5][:]), along(df_rstd, P), ALU.mult), df_ready)
                    dve.wait_ge(df_oT, i + 1)
                    d(dve.tensor_scalar(branchT[:, 2 * KB:3 * KB, P * i:P * i + P],
                                        bank[4][:].rearrange("p (j t) -> p j t", j=KB), sub_w, None, ALU.mult), df_out)

            def add_in(items):
                for _, t in items:
                    dve.wait_ge(gate_out, t + 1)
                    dve.wait_ge(merge_done, t + 1)
                    d(dve.tensor_tensor(gate_sb[:, t % 2, :], gate_sb[:, t % 2, :], proj_ps[1][:], ALU.mult), merge_mul)
                    dst = merged[:, t % KD, :]
                    if t < KD:
                        d(dve.tensor_copy(dst, gate_sb[:, t % 2, :]), merge_out)
                    else:
                        d(dve.tensor_tensor(dst, dst, gate_sb[:, t % 2, :], ALU.add), merge_out)

            lbl = cols[:, R_LB:R_LB + KB]
            d(dve.tensor_tensor(lb_e, lbl, lbl, ALU.subtract), exp_arg)
            dve.wait_ge(exp_out, 2)
            d(dve.reciprocal(lb_r, lb_e))
            d(dve.tensor_tensor(lb_r, lb_r, lb_e, ALU.mult))
            d(dve.tensor_tensor(lb, lb_r, lb_r, ALU.subtract))
            d(dve.tensor_scalar(lb_rest, lb, -1.0, 1.0, ALU.mult, ALU.add))
            dve.wait_ge(hg_sig, 1)
            for n in range(NT):
                d(dve.tensor_scalar(hg_k[:, n, :], hg_k[:, n, :], lb_rest[:, n:n + 1], lb[:, n:n + 1], ALU.mult, ALU.add), hg_f)
            add_in(DRAIN["hg"][0][0:1])
            dve.wait_ge(hg_ln, 1)
            d(dve.tensor_scalar(hg_k, hg_k, -1.0, 1.0, ALU.mult, ALU.add))
            for n in range(NT):
                for i in range(NT):
                    s = slice(P * i, P * i + P)
                    d.free(dve.tensor_tensor_scan(hg_cum[:, n, s], ones[:], hg_log[:, n, s], 0.0, ALU.mult, ALU.add), hg_scan)
            dve.wait_ge(hg_scan, 16)
            add_in(DRAIN["hg"][0][1:2])
            cum16 = hg_cum.rearrange("p n (i t) -> p (n i) t", t=P)
            as16 = lambda ap: ap.rearrange("p n (i t) -> p (n i) t", t=P)
            d(dve.tensor_tensor(as16(hg_qk[0]), along(cum16[:, :, P - 1], P), cum16, ALU.subtract), hg_kgarg)
            dve.wait_ge(hg_expk, 1)
            d(dve.tensor_tensor(hg_qk[0], hg_qk[0], hg_k, ALU.mult), hg_kg)
            dve.wait_ge(hg_expq, 1)
            dve.wait_ge(hg_silu, 2)
            d(dve.tensor_tensor(hg_qg, hg_qg, hg_q, ALU.mult), hg_qgr)
            add_in(DRAIN["hg"][0][2:])
            dve.wait_ge(hg_zeroed, 1)

            def pick(lv):
                mask = ident[:] if lv == 0 else level_mask[:, lv - 1, :]
                for i in range(NT):
                    for s in range(2):
                        q = 8 * lv + 2 * i + s
                        dve.wait_ge(hg_score, q + 1)
                        (d if (i, s) == (NT - 1, 1) else d.free)(dve.copy_predicated(hg_attn[:, i, s], over(mask.bitcast(U32), NT),
                                              bank[q % 6][:].rearrange("p (n q) -> p n q", n=NT)), hg_pick)

            for lv in range(1, len(LEVELS) + 1):
                b, buf = LEVELS[lv - 1], hg_qk[(lv - 1) % 2]
                if lv == 1:
                    dve.wait_ge(hg_kturned, NT)
                if lv > 2:
                    dve.wait_ge(hg_score, 8 * (lv - 1))
                halves = lambda ap: ap.rearrange("p n (k s j) -> p (n k) s j", s=2, j=b)
                cum, dst = halves(hg_cum), halves(buf)
                edge = along(cum[:, :, 0, b - 1], b)
                d.free(dve.tensor_tensor(dst[:, :, 0, :], edge, cum[:, :, 0, :], ALU.subtract))
                d(dve.tensor_tensor(dst[:, :, 1, :], cum[:, :, 1, :], edge, ALU.subtract), hg_dist)
                add_in(DRAIN["hg"][lv])
                pick(lv - 1)
                dve.wait_ge(hg_decay, lv)
                d.free(dve.tensor_tensor(dst[:, :, 0, :], dst[:, :, 0, :], halves(hg_k)[:, :, 0, :], ALU.mult))
                d(dve.tensor_tensor(dst[:, :, 1, :], dst[:, :, 1, :], halves(hg_q)[:, :, 1, :], ALU.mult), hg_scaled)
            add_in(DRAIN["hg"][len(LEVELS) + 1])
            pick(len(LEVELS))
            for i in range(NT):
                add_in(DRAIN["hg"][len(LEVELS) + 2 + i])
                dve.wait_ge(hg_y, i + 1)
                if i < NT - 1:
                    grp = bank[1][:].rearrange("p (n v) -> p n v", n=NT)
                    if i == 0:
                        d(dve.tensor_tensor(hg_r, grp, over(two_heads[:], NT), ALU.mult), hg_state)
                    else:
                        dve.wait_ge(hg_expl, 1)
                        d(dve.tensor_tensor(hg_r, hg_r, along(hg_last[:, i:16:4], P), ALU.mult))
                        d(dve.tensor_tensor(hg_o.rearrange("p (n v) -> p n v", n=NT), grp, over(two_heads[:], NT), ALU.mult))
                        d(dve.tensor_tensor(hg_r, hg_r, hg_o.rearrange("p (n v) -> p n v", n=NT), ALU.add), hg_state)
                dve.wait_ge(squared, 2 * NT + i + 1)
                d(dve.tensor_reduce(hg_sq, hg_tmp.rearrange("p (h v) -> p h v", v=64), AX_X, ALU.add))
                d(dve.tensor_scalar(hg_var, hg_sq, 1.0 / 64, EPS, ALU.mult, ALU.add), var_ready)
                dve.wait_ge(std_ready, 1 + 2 * NT + i + 1)
                d(dve.reciprocal(hg_rstd, hg_std))
                d(dve.tensor_tensor(heads(hg_o), heads(bank[0][:]), along(hg_rstd, 64), ALU.mult))
                d(dve.tensor_tensor(hg_o, hg_o, hg_g[:, i, :], ALU.mult), hg_ready)
                dve.wait_ge(hg_oT, i + 1)
                d(dve.tensor_scalar(branchT[:, 3 * KB:4 * KB, P * i:P * i + P], bank[2][:].rearrange("p (j t) -> p j t", j=KB),
                                    cols[:, R_HGN:R_HGN + 1], None, ALU.mult), hg_out)
            d(dve.tensor_tensor(causal_4th[:], causal_4th[:], causal[:], ALU.min))

            scale = DIL_D ** -0.5
            for n, (g, j, b0, tiles, prev) in enumerate(DIL_SCORES):
                dve.wait_ge(dl_score, n + 1)
                c_ = len(tiles)
                mask = (band_prev if prev else (causal, causal, causal_4th)[g])[:]
                dst = dl_p[:, j, b0:b0 + c_, :]
                own, before = dl_stat[g][:, :, j], dl_prev[:, 1:NT, j]
                d(dve.scalar_tensor_tensor(dst, bank[n % 4][:, 0:P * c_].rearrange("p (a k) -> p a k", k=P), scale,
                                           over(mask, c_), ALU.mult, ALU.add))
                d(dve.tensor_reduce(before if prev else own, dst, AX_X, ALU.max, negate=True),
                  None if prev else dl_masked)
                if prev:
                    d(dve.tensor_tensor(own[:, 1:NT], own[:, 1:NT], before, ALU.min), dl_masked)
            add_in(DRAIN["dil"][0][0:1])
            dve.wait_ge(dl_prob, len(DIL_SCORES))
            d(dve.tensor_tensor(dl_stat[0][:, 1:NT, 4:8], dl_stat[0][:, 1:NT, 4:8], dl_prev[:, 1:NT, 4:8], ALU.add))
            dve.wait_ge(dl_back, 32)
            nat = [dl_stat[0], dl_nat[0], dl_nat[1]]
            d(dve.tensor_tensor(dl_low, nat[0][:, :, 0:4], nat[1][:, :, 0:4], ALU.min))
            d(dve.tensor_tensor(dl_low, dl_low, nat[2][:, :, 0:4], ALU.min))
            for g in range(3):
                d(dve.tensor_tensor(dl_w[g], dl_low, nat[g][:, :, 0:4], ALU.subtract), dl_warg)
            dve.wait_ge(dl_wexp, 3)
            d(dve.tensor_tensor(dl_z, dl_w[0], nat[0][:, :, 4:8], ALU.mult))
            for g in (1, 2):
                d(dve.tensor_tensor(dl_t, dl_w[g], nat[g][:, :, 4:8], ALU.mult))
                d(dve.tensor_tensor(dl_z, dl_z, dl_t, ALU.add))
            d(dve.reciprocal(dl_z, dl_z))
            for g in range(3):
                d(dve.tensor_tensor(dl_w[g], dl_w[g], dl_z, ALU.mult), dl_weighed)
            add_in(DRAIN["dil"][0][1:])
            dve.wait_ge(dl_back, 64)
            for j in range(DIL_H):
                for b0, n, w in ((0, 4, dl_w[0][:, :, j]), (4, 3, dl_w[0][:, 1:NT, j]), (7, 4, dl_wg[0][:, :, j]),
                                 (11, 4, dl_wg[1][:, :, j])):
                    d(dve.tensor_tensor(dl_p[:, j, b0:b0 + n, :], dl_p[:, j, b0:b0 + n, :], along(w, P), ALU.mult), dl_scaled)
            for j in range(DIL_H):
                add_in(DRAIN["dil"][1 + j])
                dve.wait_ge(dl_y, j + 1)
                d(dve.tensor_copy(branchT[:, KB + j, :], bank[4 + j % 2][:]), dl_out)
            dve.wait_ge(proj_out, out_ready(f"ada{ADA - 1}"))
            d(dve.tensor_tensor(mod[:, 16:48], mod[:, 16:48], cols[:, 16:48], ALU.add), mod_copied)
            d(dve.scalar_tensor_tensor(scale_ffn[:], mod[:, 32:40], 1.0, cols[:, R_NFFN:R_NFFN + KD], ALU.add, ALU.mult), scale2_ready)
            add_in(DRAIN["dil"][-1] + merges[3 * KD:])
            dve.wait_ge(x2_loaded, 16)
            dve.wait_ge(row_ready, 10)
            def out_tile(o):
                i, half = OUT_ORDER[o]
                s = slice(512 * half, 512 * half + 512)
                dve.wait_ge(o_done, o + 1)
                tmp = gate_sb[:, o % 2, :]
                d(dve.tensor_tensor(tmp, bank[4 + o % 2][:], bc_gate1[:, s], ALU.mult))
                d(dve.tensor_tensor(x2[:, i, s], x2[:, i, s], tmp, ALU.add), o_out)

            def norm_tile(i):
                v = slice(i, i + 1)
                dve.wait_ge(squared, 3 * NT + i + 1)
                d(dve.tensor_scalar(f_var[:, v], f_sq[:, v], 1.0 / D, EPS, ALU.mult, ALU.add), var_ready)
                dve.wait_ge(std_ready, 1 + 3 * NT + i + 1)
                d(dve.reciprocal(f_rstd[:, v], f_std[:, v]))
                d(dve.scalar_tensor_tensor(h2[:, i, :], x2[:, i, :], f_rstd[:, v], bc_scale2, ALU.mult, ALU.mult))
                d(dve.tensor_tensor(h2[:, i, :], h2[:, i, :], bc_shift2, ALU.add), h2_ready)

            def h2T_out(i):
                dve.wait_ge(h2_turned, i + 1)
                d(dve.tensor_copy(h2T[:, 0:4, P * i:P * i + P], bank[0][:].rearrange("p (k t) -> p k t", k=4)), h2T_ready)

            for o in range(4):
                out_tile(o)
            norm_tile(0)
            out_tile(4)
            out_tile(5)
            norm_tile(1)
            h2T_out(0)
            norm_tile(2)
            out_tile(6)
            h2T_out(1)
            out_tile(7)
            h2T_out(2)
            norm_tile(3)
            h2T_out(3)

            dve.wait_ge(scored, 1)
            d(dve.tensor_tensor(sel, scores, over(bc[:, B_RB:B_RB + N_EXP], NT), ALU.add))
            for i in range(NT):
                for g in range(GROUPS):
                    (d if (i, g) == (NT - 1, GROUPS - 1) else d.free)(dve.max(best8[:, GROUPS * i + g, :], sel[:, i, 8 * g:8 * g + 8]))
            best = best8[:].rearrange("p (i g) m -> p i g m", i=NT)
            d(dve.tensor_tensor(grp_score, best[:, :, :, 0], best[:, :, :, 1], ALU.add))
            last_tile = lambda i: d if i == NT - 1 else d.free
            for i in range(NT):
                last_tile(i)(dve.max(top8[:, i, :], grp_score[:, i, :]))
            for i in range(NT):
                last_tile(i)(dve.max_index(top_i[:, i, :], top8[:, i, :], grp_score[:, i, :]))
            d(dve.tensor_copy(top_f[:], top_i[:]))
            d(dve.tensor_tensor(grp_pen, over(iota_grp[:], NT), along(top_f[:, :, 0], GROUPS), ALU.not_equal))
            d(dve.tensor_scalar(grp_pen, grp_pen, NEG, None, ALU.mult))
            groups = sel.rearrange("p i (g e) -> p (i g) e", g=GROUPS)
            d(dve.tensor_tensor(groups, groups, along(grp_pen.rearrange("p i g -> p (i g)"), 8), ALU.add))
            for i in range(NT):
                last_tile(i)(dve.max(top8[:, i, :], sel[:, i, :]))
            for i in range(NT):
                last_tile(i)(dve.max_index(top_i[:, i, :], top8[:, i, :], sel[:, i, :]))
            d(dve.tensor_copy(top_f[:], top_i[:]))
            for s in range(2):
                (d if s else d.free)(dve.tensor_tensor(hot[s], over(iota_exp[:], NT), along(top_f[:, :, s], N_EXP), ALU.is_equal))
            d(dve.tensor_tensor(both_hot[:], hot[0], hot[1], ALU.add))
            d(dve.tensor_copy(hot_sum[:, 0, :], both_hot[:, 0, :]))
            for i in range(1, NT):
                d(dve.tensor_tensor(hot_sum[:, i, :], hot_sum[:, i - 1, :], both_hot[:, i, :], ALU.add), hot_ready if i == NT - 1 else None)
            for s in range(2):
                d(dve.tensor_tensor(picked[:], hot[s], scores, ALU.mult))
                d(dve.tensor_reduce(pair_s[:, :, s], picked[:], AX_X, ALU.add))
            d(dve.tensor_reduce(pair_z, pair_s, AX_X, ALU.add))
            d(dve.reciprocal(pair_z, pair_z))
            d(dve.tensor_tensor(pair_s, pair_s, along(pair_z, 2), ALU.mult))
            d(dve.memset(endc[:], 0.0))
            dve.wait_ge(ranked, 1)
            for j in range(-(-T // BLK)):
                for step, dst, cnt in ((d.free, nbc[:, 0:1], bank[5][0:N_EXP, 0:1]), (d, n_blk_e[:], bank[4][:, 0:N_EXP])):
                    if j == 0:
                        step(dve.tensor_scalar(dst, cnt, 0.0, None, ALU.is_gt))
                    else:
                        step(dve.scalar_tensor_tensor(dst, cnt, float(BLK * j), dst, ALU.is_gt, ALU.add),
                             nbc_ready if j == -(-T // BLK) - 1 else None)
            d(dve.tensor_tensor_scan(blk_end[:], ones[:, 0:N_EXP], n_blk_e[:], 0.0, ALU.mult, ALU.add))
            d(dve.tensor_copy(n_blocks[:], blk_end[0:1, N_EXP - 1:N_EXP]), plan_ready)
            dve.wait_ge(ends_done, 1)
            d(dve.tensor_copy(endc[:], bank[5][0:N_EXP, 0:1]))
            d(dve.tensor_scalar(ended, iota_blk[0:N_EXP, 0:N_BLK], endc[:, 0:1], None, ALU.is_ge), ended_ready)
            d(dve.tensor_tensor(n_blk_e[:], blk_end[:], n_blk_e[:], ALU.subtract))
            ranks = bank[3][:, 0:NT * N_EXP].rearrange("p (i e) -> p i e", i=NT)
            for s in range(2):
                d.free(dve.tensor_tensor(picked[:], hot[s], ranks, ALU.mult))
                d(dve.tensor_tensor(rank[:], hot[s], over(n_blk_e[:], NT), ALU.mult))
                d.free(dve.tensor_reduce(row_of[:, s, :], picked[:], AX_X, ALU.add))
                d(dve.tensor_reduce(blk_of[:, s, :], rank[:], AX_X, ALU.add))
            dve.wait_ge(owners_done, 1)
            d(dve.tensor_scalar(blk_exp[:], bank[4][0:1, 0:N_BLK], float(N_EXP - 1), None, ALU.min), plan_ready)
            for j in range(1, -(-T // BLK)):
                if j == 1:
                    d(dve.tensor_scalar(blk_in[:], row_of[:], float(BLK * j), None, ALU.is_ge))
                else:
                    d(dve.scalar_tensor_tensor(blk_in[:], row_of[:], float(BLK * j), blk_in[:], ALU.is_ge, ALU.add))
            d.free(dve.tensor_tensor(blk_of[:], blk_of[:], blk_in[:], ALU.add))
            d(dve.scalar_tensor_tensor(row_of[:], blk_in[:], -float(BLK), row_of[:], ALU.mult, ALU.add))
            flat = lambda ap: ap.rearrange("p s i b -> p (s i) b")
            d(dve.tensor_tensor(flat(in_row), over(iota_row[:], 2 * NT), along(row_of[:].rearrange("p s i -> p (s i)"), BLK), ALU.is_equal), list_terms)
            d(dve.tensor_tensor(flat(in_blk), over(iota_blk[:], 2 * NT), along(blk_of[:].rearrange("p s i -> p (s i)"), LIST_BLK), ALU.is_equal))
            for v in range(2):
                d(dve.tensor_tensor(flat(list_term[:, :, :, v, :]), flat(in_blk), along(entry[:, v].rearrange("p s i -> p (s i)"), LIST_BLK), ALU.mult),
                  list_terms if v else None)

            dve.wait_ge(list_added, 1)
            d(dve.tensor_copy(blk_list[:, 0:LIST_BLK], bank[2][0:BLK, 0:LIST_BLK]), list_ready)
            d(dve.tensor_scalar(blk_list[:, LIST_BLK:2 * LIST_BLK], bank[2][0:BLK, LIST_BLK:2 * LIST_BLK], 2.0 * T, None, ALU.add), list_ready)

            n_valid = dve.value_load(n_blocks[0:1, 0:1], min_val=MIN_BLOCKS, max_val=MAX_BLOCKS)

            def expert_dve(b, s, first):
                dve.wait_ge(gu_act, b + 1)
                dve.wait_ge(gu_done, 2 * b + 2)
                dve.tensor_tensor(e_hid, e_act, UP_BANK[s % 2][:, 0:2 * BLK].rearrange("p (j t) -> p j t", j=2), ALU.mult)\
                   .then_inc(hid_ready, 1)
                dve.wait_ge(down_done, b + 1)
                if not first:
                    dve.wait_ge(y_stored[s], 8 * (b - s))
                for half in range(2):
                    c = slice(512 * half, 512 * half + 512)
                    dve.tensor_tensor(yb[s][0:BLK, c], (bank[5], proj_ps[0])[half][0:BLK, :], bc_gate2[0:BLK, c], ALU.mult).then_inc(y_ready, 1)

            for s in range(2):
                expert_dve(s, s, True)
            with dve.Fori(1, N_BLK // 2) as it:
                for s in range(2):
                    b = 2 * it + s
                    with dve.If(b < n_valid):
                        expert_dve(b, s, False)
            def last_norm(i):
                v = slice(NT + i, NT + i + 1)
                dve.wait_ge(squared, 4 * NT + i + 1)
                d(dve.tensor_scalar(f_var[:, v], f_sq[:, v], 1.0 / D, EPS, ALU.mult, ALU.add), var_ready)
                dve.wait_ge(std_ready, 1 + 4 * NT + i + 1)
                d(dve.reciprocal(f_rstd[:, v], f_std[:, v]))
                d(dve.scalar_tensor_tensor(out_ring[i], x2[:, i, :], f_rstd[:, v], bc_final, ALU.mult, ALU.mult), out_ready_)

            for i in range(NT):
                a, b = yg[2 * (i % 2)], yg[2 * (i % 2) + 1]
                dve.wait_ge(yg_loaded[i % 2], 32 * (i // 2 + 1))
                d(dve.scalar_tensor_tensor(x2[:, i, :], a, pair_s[:, i, 0:1], x2[:, i, :], ALU.mult, ALU.add))
                d(dve.scalar_tensor_tensor(x2[:, i, :], b, pair_s[:, i, 1:2], x2[:, i, :], ALU.mult, ALU.add), x3_ready)
                if i:
                    last_norm(i - 1)
            last_norm(NT - 1)


_INS = ["x", "c", "w_ada", "b_ada", "norm_mix_w", "norm_ffn_w", "w_in", "conv_w", "conv_b", "ssd_dt_bias",
        "ssd_a_log", "ssd_d", "ssd_norm_w", "diff_lambda", "diff_subln_w", "hgrn_lb_logits", "hgrn_norm_w",
        "w_merge", "w_out", "w_router", "router_bias", "w_expert_gate", "w_expert_up", "w_expert_down",
        "final_norm_w"]


def kernel(**inputs):
    import numpy as np
    import concourse.bacc as bacc
    from concourse.bass_utils import run_bass_kernel_spmd

    nc = bacc.Bacc("TRN2", target_bir_lowering=False, num_devices=1)
    arrays, args = {}, []
    for name in _INS:
        a = np.ascontiguousarray(inputs[name])
        arrays[f"in_{name}"] = a
        args.append(nc.dram_tensor(f"in_{name}", a.shape, mybir.dt.from_np(a.dtype), kind="ExternalInput").ap())
    for name, shape, dt in (("h2_rows", (T, D), F32),
                            ("y_rows", (2 * T, D), F32), ("dil_stats", (2, T, 8), F32),
                            ("dil_weights", (2, T, 4), F32)):
        args.append(nc.dram_tensor(name, shape, dt, kind="Internal").ap())
    args.append(nc.dram_tensor("out", (1, T, D), F32, kind="ExternalOutput").ap())
    build(nc, *args)
    r = run_bass_kernel_spmd(nc, [arrays], core_ids=[0])
    return r.results[0]["out"]
```
